# Optimizing a Trainium2 kernel written in Bass

```python
import jax, jax.numpy as jnp
from jax import lax
import numpy as np

D_MODEL = 1024
BATCH = 1
SEQ = 512
DEPTH = 1

N_META = 16
BLOCK_Q = 128
EPS = 1e-6
ROPE_THETA = 10000.0
ATT_HEADS = 8
Q_LORA = 256
KV_LORA = 128
QK_NOPE = 64
QK_ROPE = 32
V_HEAD = 64
D_ATT = ATT_HEADS * V_HEAD
D_CONV = D_MODEL - D_ATT
CONV_WIDTH = 3
D_MIX = D_ATT + D_CONV
IN_COLS = Q_LORA + KV_LORA + QK_ROPE + 3 * D_CONV
PEER_HEADS = 8
N_KEYS = 128
N_EXPERTS = N_KEYS * N_KEYS
D_KEY = 256
PEER_TOPK = 16
PEER_BLOCK = 64

kernel_name = 'hymba_mla_shortconv_peer_layer'

def rms_norm(x, g):
    xf = x.astype(jnp.float32)
    y = xf * lax.rsqrt(jnp.mean(xf * xf, axis=-1, keepdims=True) + EPS)
    return (y * g.astype(jnp.float32)).astype(x.dtype)

def rope_tables(L):
    inv = 1.0 / (ROPE_THETA ** (jnp.arange(0, QK_ROPE, 2, dtype=jnp.float32) / QK_ROPE))
    ang = jnp.arange(L, dtype=jnp.float32)[:, None] * inv[None, :]
    return jnp.cos(ang), jnp.sin(ang)

def apply_rope(x, cos, sin):
    xf = x.astype(jnp.float32)
    x1, x2 = xf[..., :QK_ROPE // 2], xf[..., QK_ROPE // 2:]
    return jnp.concatenate([x1 * cos - x2 * sin, x1 * sin + x2 * cos], axis=-1).astype(x.dtype)

def mla_attention(c_q, c_kv, k_rope, q_norm_g, w_uq, kv_norm_g, w_ukv, cos, sin):
    B, L, _ = c_q.shape
    q = jnp.einsum('blr,rf->blf', rms_norm(c_q, q_norm_g), w_uq).reshape(B, L, ATT_HEADS, QK_NOPE + QK_ROPE)
    q_nope = q[..., :QK_NOPE]
    q_rope = apply_rope(q[..., QK_NOPE:], cos[None, :, None], sin[None, :, None])
    kv = jnp.einsum('blr,rf->blf', rms_norm(c_kv, kv_norm_g), w_ukv).reshape(B, L, ATT_HEADS, QK_NOPE + V_HEAD)
    k_nope, v = kv[..., :QK_NOPE], kv[..., QK_NOPE:]
    k_rope = apply_rope(k_rope, cos[None], sin[None])
    q = jnp.concatenate([q_nope, q_rope], axis=-1)
    k = jnp.concatenate([k_nope, jnp.broadcast_to(k_rope[:, :, None], (B, L, ATT_HEADS, QK_ROPE))], axis=-1)
    scale = (QK_NOPE + QK_ROPE) ** -0.5
    n_blk = L // BLOCK_Q
    q_blocks = q.reshape(B, n_blk, BLOCK_Q, ATT_HEADS, QK_NOPE + QK_ROPE).swapaxes(0, 1)
    k_pos = jnp.arange(L)
    neg = jnp.finfo(jnp.float32).min

    def one_block(args):
        qb, i = args
        s = jnp.einsum('bqhd,bkhd->bhqk', qb, k).astype(jnp.float32) * scale
        q_pos = i * BLOCK_Q + jnp.arange(BLOCK_Q)
        s = jnp.where(k_pos[None, :] <= q_pos[:, None], s, neg)
        p = jax.nn.softmax(s, axis=-1).astype(v.dtype)
        return jnp.einsum('bhqk,bkhd->bqhd', p, v)

    out = lax.map(one_block, (q_blocks, jnp.arange(n_blk)))
    return out.swapaxes(0, 1).reshape(B, L, D_ATT)

def short_conv(b_gate, c_gate, u, conv_w, conv_b):
    z = c_gate * u
    zp = jnp.pad(z, ((0, 0), (CONV_WIDTH - 1, 0), (0, 0)))
    L = z.shape[1]
    conv = conv_b + conv_w[0] * zp[:, 0:L] + conv_w[1] * zp[:, 1:L + 1] + conv_w[2] * zp[:, 2:L + 2]
    return b_gate * conv

def peer_ffn(x, w_query, keys1, keys2, u, v):
    B, L, _ = x.shape
    q = jnp.einsum('bld,df->blf', x, w_query).reshape(B, L, PEER_HEADS, 2, D_KEY // 2)
    s1 = jnp.einsum('blhd,nd->blhn', q[..., 0, :], keys1).astype(jnp.float32)
    s2 = jnp.einsum('blhd,nd->blhn', q[..., 1, :], keys2).astype(jnp.float32)
    v1, i1 = lax.top_k(s1, PEER_TOPK)
    v2, i2 = lax.top_k(s2, PEER_TOPK)
    cand = (v1[..., :, None] + v2[..., None, :]).reshape(B, L, PEER_HEADS, PEER_TOPK * PEER_TOPK)
    best, flat = lax.top_k(cand, PEER_TOPK)
    expert = (jnp.take_along_axis(i1, flat // PEER_TOPK, axis=-1) * N_KEYS
              + jnp.take_along_axis(i2, flat % PEER_TOPK, axis=-1))
    gate = jax.nn.softmax(best, axis=-1).astype(x.dtype)
    n_blk = L // PEER_BLOCK

    def blockify(a):
        return a.reshape(B, n_blk, PEER_BLOCK, *a.shape[2:]).swapaxes(0, 1)

    def one_block(args):
        xb, eb, gb = args
        ue = u[eb]
        ve = v[eb]
        act = jax.nn.gelu(jnp.einsum('bthkd,btd->bthk', ue, xb))
        return jnp.einsum('bthk,bthkd->btd', gb * act, ve)

    out = lax.map(one_block, (blockify(x), blockify(expert), blockify(gate)))
    return out.swapaxes(0, 1).reshape(B, L, D_MODEL)

def setup_inputs(seed: int = 0) -> dict:
    key = jax.random.key(seed)
    ks = jax.random.split(key, 24)
    f32 = jnp.float32

    def nrm(k, shape, scale):
        return jax.random.normal(k, shape, f32) * scale

    def gain(k, shape):
        return 1.0 + 0.02 * jax.random.normal(k, shape, f32)

    return {
        'x': nrm(ks[0], (BATCH, SEQ, D_MODEL), 1.0),
        'meta_tokens': nrm(ks[1], (N_META, D_MODEL), 1.0),
        'norm1_g': gain(ks[2], (DEPTH, D_MODEL)),
        'w_in': nrm(ks[3], (DEPTH, D_MODEL, IN_COLS), D_MODEL ** -0.5),
        'q_norm_g': gain(ks[4], (DEPTH, Q_LORA)),
        'w_uq': nrm(ks[5], (DEPTH, Q_LORA, ATT_HEADS * (QK_NOPE + QK_ROPE)), Q_LORA ** -0.5),
        'kv_norm_g': gain(ks[6], (DEPTH, KV_LORA)),
        'w_ukv': nrm(ks[7], (DEPTH, KV_LORA, ATT_HEADS * (QK_NOPE + V_HEAD)), KV_LORA ** -0.5),
        'conv_w': nrm(ks[8], (DEPTH, CONV_WIDTH, D_CONV), CONV_WIDTH ** -0.5),
        'conv_b': nrm(ks[9], (DEPTH, D_CONV), 0.01),
        'attn_out_g': gain(ks[10], (DEPTH, D_ATT)),
        'conv_out_g': gain(ks[11], (DEPTH, D_CONV)),
        'w_out': nrm(ks[12], (DEPTH, D_MIX, D_MODEL), D_MIX ** -0.5),
        'norm2_g': gain(ks[13], (DEPTH, D_MODEL)),
        'peer_w_query': nrm(ks[14], (DEPTH, D_MODEL, PEER_HEADS * D_KEY), D_MODEL ** -0.5),
        'peer_keys1': nrm(ks[15], (DEPTH, N_KEYS, D_KEY // 2), (D_KEY // 2) ** -0.5),
        'peer_keys2': nrm(ks[16], (DEPTH, N_KEYS, D_KEY // 2), (D_KEY // 2) ** -0.5),
        'peer_u': nrm(ks[17], (DEPTH, N_EXPERTS, D_MODEL), D_MODEL ** -0.5),
        'peer_v': nrm(ks[18], (DEPTH, N_EXPERTS, D_MODEL), PEER_HEADS ** -0.5),
        'final_g': gain(ks[19], (D_MODEL,)),
    }

def reference(x, meta_tokens, norm1_g, w_in, q_norm_g, w_uq, kv_norm_g, w_ukv, conv_w, conv_b,
              attn_out_g, conv_out_g, w_out, norm2_g, peer_w_query, peer_keys1, peer_keys2,
              peer_u, peer_v, final_g):
    B, S, _ = x.shape
    L = N_META + S
    L_pad = -(-L // BLOCK_Q) * BLOCK_Q
    meta = jnp.broadcast_to(meta_tokens[None].astype(x.dtype), (B, N_META, D_MODEL))
    h = jnp.concatenate([meta, x], axis=1)
    h = jnp.pad(h, ((0, 0), (0, L_pad - L), (0, 0)))
    cos, sin = rope_tables(L_pad)
    o1 = Q_LORA
    o2 = o1 + KV_LORA
    o3 = o2 + QK_ROPE
    o4 = o3 + D_CONV
    o5 = o4 + D_CONV
    for l in range(DEPTH):
        hn = rms_norm(h, norm1_g[l])
        p = jnp.einsum('bld,df->blf', hn, w_in[l])
        c_q, c_kv, k_rope = p[..., :o1], p[..., o1:o2], p[..., o2:o3]
        b_gate, c_gate, u = p[..., o3:o4], p[..., o4:o5], p[..., o5:]
        attn = mla_attention(c_q, c_kv, k_rope, q_norm_g[l], w_uq[l], kv_norm_g[l], w_ukv[l], cos, sin)
        conv = short_conv(b_gate, c_gate, u, conv_w[l], conv_b[l])
        mixed = jnp.concatenate([rms_norm(attn, attn_out_g[l]), rms_norm(conv, conv_out_g[l])], axis=-1)
        h = h + jnp.einsum('blf,fd->bld', mixed, w_out[l])
        h = h + peer_ffn(rms_norm(h, norm2_g[l]), peer_w_query[l], peer_keys1[l], peer_keys2[l],
                         peer_u[l], peer_v[l])
    return rms_norm(h, final_g)[:, N_META:L]


_drawn_inputs = setup_inputs


def setup_inputs(seed=0):
    import zlib

    import numpy as np

    out = dict(_drawn_inputs(seed))
    spreads = {}
    factors = {'q_norm_g': 3.458,
     'conv_b': 4.998,
     'attn_out_g': 9.913,
     'conv_out_g': 10.423,
     'norm2_g': 9.596,
     'final_g': 8.05}
    for name, (base, spread) in spreads.items():
        noise = np.random.default_rng([zlib.crc32(name.encode()), seed]).standard_normal(out[name].shape)
        drawn = base * np.exp(spread * noise) if base else spread * noise
        out[name] = __import__('jax').numpy.asarray(drawn.astype(out[name].dtype))
    for name, factor in factors.items():
        out[name] = (out[name] * factor).astype(out[name].dtype)
    return out
```

```python
from contextlib import ExitStack

import concourse.bass as bass
import numpy as np
from concourse import mybir

D = 1024
T = 512
META = 16
L = T + META
KD = D // 128
EPS = 1e-6
HEADS, NOPE, ROPE, VDIM = 8, 64, 32, 64
QL, KVL = 256, 128
DC = 512
NK = 128
TOPK = 16
QT = T // 128
SCALE = float(NOPE + ROPE) ** -0.5
NEG = -3.0e38

N_IN = 17
N_OUT = 8
WRING = 4
PHEADS = 8
WIDE = 4
NCAND = WIDE * TOPK + (TOPK - WIDE) * 4
ADV = 8
CHUNKS = NK // 2
HALF = 64
GROUP = 8
SLOTS = 4
GROUPS = HALF // GROUP
GSCALE = 4096.0

G1, GQ, GKV, GA, GC, G2, GF, CW, CB, NVEC = 0, 8, 10, 11, 15, 19, 27, 35, 47, 51


def hymba_peer_kernel(nc, xT, metaT, vecs, consts, rope, w_tiles, w_uq, w_ukv, keysT, w_query, uT, v, yT):
    f32, f32r, f16, u32 = mybir.dt.float32, mybir.dt.float32r, mybir.dt.float16, mybir.dt.uint32
    ALU, ACT, AX = mybir.AluOpType, mybir.ActivationFunctionType, mybir.AxisListType

    gates_dram = nc.dram_tensor("gates_dram", (T // HALF, 128, NK, HALF), f32, kind="Internal").ap()
    gates_of = gates_dram.rearrange("q i j t -> i q j t")
    v_tiles = v.rearrange("(i j) d -> i j d", j=NK)

    ctx = ExitStack()
    with ctx:
        def sb(stack, name, shape, dt=f32):
            return stack.enter_context(nc.sbuf_tensor(name, shape, dt))

        const = sb(ctx, "const", [128, 3 * 128])
        ident, iota, ones = const[:, 0:128], const[:, 128:256], const[:, 256:384]
        vec = sb(ctx, "vec", [128, NVEC])
        eps = sb(ctx, "eps", [128, 1])
        early = ExitStack()
        qr_in = sb(early, "qr_in", [128, 4, T])
        wuq_t = sb(early, "wuq_t", [128, 8, 2, 128])
        early.close()
        acc = sb(ctx, "acc", [128, KD, T])

        front = ExitStack()
        normed = ExitStack()
        h_hi = sb(normed, "h_hi", [128, KD, L], f32r)
        h_lo = sb(normed, "h_lo", [128, KD, L], f32r)
        normed.close()
        m_hi = sb(front, "m_hi", [128, KD, T], f32r)
        m_lo = sb(front, "m_lo", [128, KD, T], f32r)
        spare = sb(front, "spare", [128, 2 * KD * META])
        qn = sb(front, "qn", [128, 4, T])
        qr = sb(front, "qr", [128, 2, T])
        hT = sb(front, "hT", [128, KD, L])
        wring = sb(front, "wring", [128, WRING, KD, 128])
        w_hi_t = sb(front, "w_hi_t", [128, 2, KD, 128], f32r)
        w_lo_t = sb(front, "w_lo_t", [128, 2, KD, 128], f32r)
        kn = sb(front, "kn", [128, 4, L])
        kr = sb(front, "kr", [128, L])
        v_att = sb(front, "v_att", [128, QT, DC])
        v_meta = sb(front, "v_meta", [META, DC])
        conv = sb(front, "conv", [128, 4, T])
        causal = sb(front, "causal", [128, L])
        sq = sb(front, "sq", [128, 2, L])
        rstd = sb(front, "rstd", [128, 2, L])
        rowsum = sb(front, "rowsum", [128, 2, HEADS * QT])
        negmax = sb(front, "negmax", [128, HEADS * QT])
        xn_f = sb(front, "xn_f", [128, 2, L])
        proj = ExitStack()
        c_q = sb(proj, "c_q", [128, 2, T])
        c_kv = sb(proj, "c_kv", [128, L])
        kr_in = sb(proj, "kr_in", [128, 2, L])
        cgate = sb(proj, "cgate", [128, L])
        rope_t = sb(proj, "rope_t", [128, 2, L])
        wukv_t = sb(proj, "wukv_t", [128, 2 * DC])
        zpad = sb(proj, "zpad", [128, 4, 2 + L])
        bgate = sb(proj, "bgate", [128, 4, T])
        proj.close()
        probs = sb(front, "probs", [128, 4, L])
        ptr = sb(front, "ptr", [128, 2, QT, T])
        ptm = sb(front, "ptm", [META, 2, T])
        att = sb(front, "att", [128, 4, T])
        front.close()

        main = ExitStack()
        x_hi = sb(main, "x_hi", [128, KD, T], f32r)
        x_lo = sb(main, "x_lo", [128, KD, T], f32r)
        act = sb(main, "act", [128, ADV, 2, T])
        raw, s_hi, s_lo = [None, None], [None, None], [None, None]
        raw[0], s_hi[0], s_lo[0] = (sb(main, "raw0", [128, 2, KD, 128]), sb(main, "s_hi0", [128, 2, KD, 128], f32r),
                                    sb(main, "s_lo0", [128, 2, KD, 128], f32r))
        onehots = ExitStack()
        onehot = sb(onehots, "onehot", [128, SLOTS, 3, NK, GROUP], f16)
        onehots.close()
        raw[1], s_hi[1], s_lo[1] = (sb(main, "raw1", [128, 2, KD, 128]), sb(main, "s_hi1", [128, 2, KD, 128], f32r),
                                    sb(main, "s_lo1", [128, 2, KD, 128], f32r))
        choose = ExitStack()
        keys = sb(choose, "keys", [128, 2, NK])
        xtmp = sb(choose, "xtmp", [128, 2, T])
        qk = sb(choose, "qk", [128, 2, 2, T])
        score = sb(choose, "score", [128, 4, QT, 2, NK])
        rest = sb(choose, "rest", [128, QT, 2, NK])
        topv = sb(choose, "topv", [128, 2, QT, TOPK])
        topi = sb(choose, "topi", [128, 2, QT, TOPK], u32)
        cand = sb(choose, "cand", [128, QT, NCAND])
        cand2 = sb(choose, "cand2", [128, QT, NCAND])
        digit = sb(choose, "digit", [128, 3, QT, TOPK], u32)
        bestv = sb(choose, "bestv", [128, QT, TOPK])
        flat = sb(choose, "flat", [128, QT, TOPK], u32)
        pos = sb(choose, "pos", [128, 2, QT, TOPK])
        hit = sb(choose, "hit", [128, 2, 2, QT, TOPK, TOPK])
        topi_f = sb(choose, "topi_f", [128, 2, 2, QT, TOPK])
        expert = sb(choose, "expert", [128, 2, QT, PHEADS, TOPK])
        best = sb(choose, "best", [128, QT, PHEADS, TOPK])
        bsum = sb(choose, "bsum", [128, QT * PHEADS])
        choose.close()
        gatep = ExitStack()
        stage = sb(gatep, "stage", [128, 2, NK, HALF])
        pick = sb(gatep, "pick", [128, 4, T], f16)
        pgate = sb(gatep, "pgate", [128, T])
        iotas = sb(gatep, "iotas", [128, NK, GROUP], f16)
        gatep.close()
        v_raw = sb(main, "v_raw", [128, 2, 2, D])
        v_hi = sb(main, "v_hi", [128, 2, 2, D], f32r)
        v_lo = sb(main, "v_lo", [128, 2, 2, D], f32r)
        w_hi = sb(main, "w_hi", [128, 2, 2, T], f32r)
        w_lo = sb(main, "w_lo", [128, 2, 2, T], f32r)
        gate = sb(main, "gate", [128, 2, T // HALF, 2, HALF])
        main.close()
        fin = ExitStack()
        fin_sq = sb(fin, "fin_sq", [128, 2, T])
        fin_r = sb(fin, "fin_r", [128, T])
        fin.close()
        bank = [ctx.enter_context(nc.psum_tensor(f"bank{p}", [128, 1024], f32)) for p in range(4)]

        def across(pair):
            return pair[:, :].rearrange("p (h n) -> p h n", h=2)[:, :, 0:L // 2]

        def halves(columns):
            return columns.rearrange("p (h n) -> p h n", h=2)

        def spans(with_meta):
            if with_meta:
                return [(slice(h * L // 2, (h + 1) * L // 2), slice(512 * h, 512 * h + L // 2)) for h in range(2)]
            return [(slice(0, T), slice(0, T))]

        def sem(name):
            return ctx.enter_context(nc.semaphore(name))

        x_loaded = [sem(f"x_loaded{k}") for k in range(4)]
        meta_loaded, vec_loaded, const_loaded, causal_loaded, rope_loaded = (
            sem("meta_loaded"), sem("vec_loaded"), sem("const_loaded"), sem("causal_loaded"), sem("rope_loaded"))
        wuq_loaded, wukv_loaded, keys_loaded = sem("wuq_loaded"), sem("wukv_loaded"), sem("keys_loaded")
        w_loaded = [sem(f"w_loaded{s}") for s in range(WRING)]
        raw_loaded = [sem("raw_loaded0"), sem("raw_loaded1")]
        v_loaded = [sem("v_loaded0"), sem("v_loaded1")]
        gate_loaded = [sem("gate_loaded0"), sem("gate_loaded1")]
        stage_stored = [sem("stage_stored0"), sem("stage_stored1")]
        y_stored = sem("y_stored")
        sq_ready, sq_summed, sum_ready, root_ready = sem("sq_ready"), sem("sq_summed"), sem("sum_ready"), sem("root_ready")
        rstd_ready, norm_applied = sem("rstd_ready"), sem("norm_applied")
        eps_set = sem("eps_set")
        tile_done, copied, z_ready, conv_ready, resid_ready = (
            sem("tile_done"), sem("copied"), sem("z_ready"), sem("conv_ready"), sem("resid_ready"))
        blk_ready, blk_hi, blk_lo = sem("blk_ready"), sem("blk_hi"), sem("blk_lo")
        wt_hi, wt_lo = sem("wt_hi"), sem("wt_lo")
        krope_ready, qrope_ready = sem("krope_ready"), sem("qrope_ready")
        scores_ready, bias_ready, probs_ready, probs_scaled = (
            sem("scores_ready"), sem("bias_ready"), sem("probs_ready"), sem("probs_scaled"))
        pt_ready, pt_copied, pv_ready, pv_copied = sem("pt_ready"), sem("pt_copied"), sem("pv_ready"), sem("pv_copied")
        xf_ready, xhi_ready, xlo_ready = sem("xf_ready"), sem("xhi_ready"), sem("xlo_ready")
        hi_ready, lo_ready, prod_done, prod_taken = sem("hi_ready"), sem("lo_ready"), sem("prod_done"), sem("prod_taken")
        keyscore_done, keyscore_copied, keyscore_taken = sem("keyscore_done"), sem("keyscore_copied"), sem("keyscore_taken")
        hit_ready, hit_weighed = sem("hit_ready"), sem("hit_weighed")
        shifted, exps_ready, choice_ready = sem("shifted"), sem("exps_ready"), sem("choice_ready")
        pick_done, pick_copied = sem("pick_done"), sem("pick_copied")
        iotas_ready, pgate_ready, plo_ready = sem("iotas_ready"), sem("pgate_ready"), sem("plo_ready")
        onehot_hi_ready, onehot_lo_ready = sem("onehot_hi_ready"), sem("onehot_lo_ready")
        gmat_done, gmat_staged = sem("gmat_done"), sem("gmat_staged")
        w_ready, whi_ready, wlo_ready, vhi_ready, vlo_ready = (
            sem("w_ready"), sem("whi_ready"), sem("wlo_ready"), sem("vhi_ready"), sem("vlo_ready"))
        out_done, out_free = sem("out_done"), sem("out_free")
        y_ready = sem("y_ready")
        dve_step, act_step, pool_step = sem("dve_step"), sem("act_step"), sem("pool_step")

        passed = {e: sem(f"passed_{e}") for e in ("act", "dve")}

        def wait_apart(eng, name, s, value):
            eng.wait_ge(s, value)
            eng.sem_inc(passed[name], 1)

        def is_u(n):
            return 5 <= n < N_IN and (n - 5) % 3 == 1

        def wait_taken(eng, n):
            if is_u(n):
                eng.wait_ge(z_ready, (n - 5) // 3 + 1)
            else:
                eng.wait_ge(copied, sum(not is_u(m) for m in range(n + 1)))

        N_QKV = 17
        N_PROJ = N_IN + N_QKV
        PROJ_COPIES = N_PROJ - 4
        NORM1, NORMQ, NORMKV, NORMC, NORMA, NORM2, NORMF = range(7)
        SQ_FROM = [0, 8, 10, 11, 15, 19, 27]
        N_ATT = HEADS * QT
        MIX_STEPS = [9, 11, 13, 15]

        def score_banks(i):
            return (bank[0][:, 0:512], bank[0][:, 512:1024], bank[1][:, 0:512], bank[3])[i]

        def turn_bank(n):
            return bank[1][:, 512:1024] if n % 2 else bank[2][:, 0:512]

        value_bank = bank[2][:, 512:1024]

        def meta_block(n):
            i = n % QT
            return turn_bank(n)[0:META, 128 * (i + 1):128 * (i + 2)] if i < QT - 1 else bank[3][0:META, 640:768]

        block = ctx.enter_context(nc.Block())

        @block.sync
        def _(sp):
            sp.dma_start(hT[:, :, T:L], metaT).then_inc(meta_loaded, 16)
            for k in range(4):
                sp.dma_start(hT[:, 2 * k:2 * k + 2, 0:T], xT[:, 2 * k:2 * k + 2, :]).then_inc(x_loaded[k], 16)
            sp.dma_start(const[:, :], consts[:, 0:384]).then_inc(const_loaded, 16)
            sp.dma_start(vec[:, :], vecs).then_inc(vec_loaded, 16)

            def load_w(n):
                if n >= WRING:
                    sp.wait_ge(wt_lo, n - WRING + 1)
                sp.dma_start(wring[:, n % WRING, :, :], w_tiles[n]).then_inc(w_loaded[n % WRING], 16)

            for n in range(WRING):
                load_w(n)
            sp.dma_start(rope_t[:, :, :], rope).then_inc(rope_loaded, 16)
            sp.dma_start(wuq_t[:, :, :, :], w_uq).then_inc(wuq_loaded, 16)
            sp.dma_start(wukv_t[:, :], w_ukv).then_inc(wukv_loaded, 16)
            sp.dma_start(causal[:, :], consts[:, 384:384 + L]).then_inc(causal_loaded, 16)
            for n in range(WRING, N_IN + N_OUT):
                load_w(n)

            sp.wait_ge(resid_ready, N_OUT)

            def load_query(h):
                sp.dma_start(raw[h % 2][:, :, :, :], w_query[h]).then_inc(raw_loaded[h % 2], 16)

            def load_u(c, b):
                sp.wait_ge(lo_ready, c + PHEADS - 1)
                sp.dma_start(raw[b][:, :, :, :], uT[bass.ds(c, 1)].rearrange("c p t k e -> (c p) t k e")).then_inc(raw_loaded[b], 16)

            def load_v(c, b, first=False):
                if not first:
                    sp.wait_ge(vlo_ready, c - 1)
                sp.dma_start(v_raw[:, b], v_tiles[:, bass.ds(2 * c, 2), :]).then_inc(v_loaded[b], 16)

            def load_gate(c, b, first=False):
                if not first:
                    sp.wait_ge(w_ready, c - 1)
                sp.dma_start(gate[:, b], gates_of[:, :, bass.ds(2 * c, 2), :]).then_inc(gate_loaded[b], 16)

            for h in range(PHEADS):
                if h >= 2:
                    sp.wait_ge(lo_ready, h - 1)
                load_query(h)
                if h == 0:
                    sp.wait_ge(norm_applied, NORM2 + 1)
                    sp.dma_start(keys[:, :, :], keysT).then_inc(keys_loaded, 16)
            for c in range(ADV + 1):
                load_u(c, c % 2)
            for b in range(2):
                sp.wait_ge(stage_stored[b], 16 * (T // HALF // 2))
            load_u(ADV + 1, 1)
            for c in range(2):
                load_v(c, c % 2, first=True)
                load_gate(c, c % 2, first=True)
            for c in range(2, 4):
                load_u(c + ADV, c % 2)
                load_v(c, c % 2)
                load_gate(c, c % 2)
            with sp.Fori(2, (CHUNKS - ADV) // 2) as i:
                for b in range(2):
                    load_u(2 * i + b + ADV, b)
                    load_v(2 * i + b, b)
                    load_gate(2 * i + b, b)
            with sp.Fori((CHUNKS - ADV) // 2, CHUNKS // 2) as i:
                for b in range(2):
                    load_v(2 * i + b, b)
                    load_gate(2 * i + b, b)

            for k in range(KD):
                sp.wait_ge(y_ready, k + 1)
                sp.dma_start(yT[:, k, :], acc[:, k, :]).then_inc(y_stored, 16)
            sp.wait_ge(y_stored, 16 * KD)

        @block.tensor
        def _(pe):
            def sum_squares(n, count, pair, meta, only=None):
                for k in range(count) if only is None else (only,):
                    q = SQ_FROM[n] + k
                    pe.wait_ge(sq_ready, q + 1)
                    src = sq[:, q % 2, :] if n != NORMF else fin_sq[:, q % 2, :]
                    for cols, to in spans(meta):
                        last = nc.tensor.matmul(bank[pair][:, to], ones, src[:, cols], start=(k == 0), stop=(k == count - 1))
                    if k == count - 1:
                        last.then_inc(sum_ready, 1)
                    else:
                        last.then_inc(sq_summed, 1)

            pe.wait_ge(const_loaded, 16)
            sum_squares(NORM1, KD, 2, True)

            def parts_product(to, n, x_parts, part, order, waits=None):
                first = True
                for ws, xs in ((w_hi_t, x_parts[0]), (w_lo_t, x_parts[0]), (w_hi_t, x_parts[1])):
                    for k in order:
                        if waits is not None:
                            at = k if waits == 0 else KD + (k + 4) % KD
                            pe.wait_ge(blk_lo if xs is x_parts[1] else blk_hi, at + 1)
                        last = nc.tensor.matmul(to, ws[:, n % 2, k, :], xs[:, k, part], start=first,
                                                stop=(ws is w_hi_t and xs is x_parts[1] and k == order[-1]))
                        first = False
                return last

            def in_product(n):
                pe.wait_ge(wt_lo, n + 1)
                if n >= 2:
                    wait_taken(pe, n - 2)
                for cols, to in spans(n >= 2 and (n < 5 or (n - 5) % 3 < 2)):
                    last = parts_product(bank[n % 2][:, to], n, (h_hi, h_lo), cols, range(KD), 0 if n == 0 else None)
                last.then_inc(tile_done, 1)

            for n in range(8):
                in_product(n)
            sum_squares(NORMQ, 2, 3, False)
            pe.wait_ge(root_ready, NORM1 + 1)
            sum_squares(NORMKV, 1, 2, True)
            for n in range(8, N_IN):
                in_product(n)

            pe.wait_ge(wuq_loaded, 16)
            pe.wait_ge(wukv_loaded, 16)
            pe.wait_ge(norm_applied, NORMKV + 1)
            for m in range(N_QKV):
                n = N_IN + m
                wait_taken(pe, n - 2)
                to = bank[n % 2]
                if m < 8:
                    for k in range(2):
                        last = nc.tensor.matmul(to[:, 0:T], wuq_t[:, m, k, :], c_q[:, k, :], start=(k == 0), stop=(k == 1))
                elif m < 12:
                    w = wukv_t[:, (m - 8) * 128:(m - 7) * 128]
                    for cols, where in spans(True):
                        last = nc.tensor.matmul(to[:, where], w, c_kv[:, cols], start=True, stop=True)
                elif m < 16:
                    last = nc.tensor.matmul(to[:, 0:T], c_kv[:, (m - 12) * 128:(m - 11) * 128], wukv_t[:, DC:2 * DC],
                                            start=True, stop=True)
                else:
                    last = nc.tensor.matmul(to[0:META, 0:T], c_kv[:, T:L], wukv_t[:, DC:2 * DC], start=True, stop=True)
                last.then_inc(tile_done, 1)

            sum_squares(NORMC, 4, 2, False)

            pe.wait_ge(copied, PROJ_COPIES)
            pe.wait_ge(krope_ready, 1)
            pe.wait_ge(qrope_ready, 1)

            def scores(n):
                h, i = n // QT, n % QT
                if n >= QT:
                    pe.wait_ge(probs_ready, n - QT + 1)
                if i == QT - 1 and n > QT:
                    pe.wait_ge(pt_copied, n - QT + 1)
                if n == 3:
                    pe.wait_ge(root_ready, NORMC + 1)
                keys_n = 128 * (i + 1)
                s = score_banks(i)
                a, r = 64 * (h % 2), 32 * (h % 4)
                qa = qn[a:a + 64, h // 2, 128 * i:128 * i + 128]
                qb = qr[r:r + 32, h // 4, 128 * i:128 * i + 128]
                nc.tensor.matmul(s[:, 0:keys_n], qa, kn[a:a + 64, h // 2, 0:keys_n], start=True, stop=False)
                nc.tensor.matmul(s[:, 0:keys_n], qb, kr[r:r + 32, 0:keys_n], start=False, stop=True)
                to = s[:, keys_n:keys_n + META]
                nc.tensor.matmul(to, qa, kn[a:a + 64, h // 2, T:L], start=True, stop=False)
                nc.tensor.matmul(to, qb, kr[r:r + 32, T:L], start=False, stop=True).then_inc(scores_ready, 1)

            def transpose_probs(n):
                i = n % QT
                pe.wait_ge(probs_scaled, n + 1)
                if n >= 2:
                    pe.wait_ge(pt_copied, n - 1)
                for j in range(i + 1):
                    nc.tensor.transpose(turn_bank(n)[:, 128 * j:128 * j + 128], probs[:, n % 4, 128 * j:128 * j + 128], ident)
                nc.tensor.transpose(meta_block(n), probs[:, n % 4, 128 * (i + 1):128 * (i + 1) + META],
                                    ident).then_inc(pt_ready, 1)

            def attend(h):
                pe.wait_ge(pt_copied, QT * (h + 1))
                if h >= 2 and h % 2 == 0:
                    pe.wait_ge(pv_copied, h // 2)
                to = value_bank[64 * (h % 2):64 * (h % 2) + 64, :]
                nc.tensor.matmul(to[:, 0:T], v_meta[:, VDIM * h:VDIM * h + VDIM], ptm[:, h % 2, :], start=True, stop=False)
                for j in range(QT):
                    last = nc.tensor.matmul(to[:, 128 * j:T], v_att[:, j, VDIM * h:VDIM * h + VDIM],
                                            ptr[:, h % 2, j, 128 * j:T], start=False, stop=(j == QT - 1))
                last.then_inc(pv_ready, 1)

            for n in range(3):
                scores(n)
            for n in range(N_ATT):
                if n + 3 < N_ATT:
                    scores(n + 3)
                transpose_probs(n)
                if n % QT == 1 and n > QT:
                    attend(n // QT - 1)
            attend(HEADS - 1)
            pe.wait_ge(pt_copied, N_ATT)
            sum_squares(NORMA, 4, 3, False)

            for m in range(N_OUT):
                n = N_IN + m
                pe.wait_ge(wt_lo, n + 1)
                if m >= 2:
                    pe.wait_ge(resid_ready, m - 1)
                parts_product(bank[m % 2][:, 0:T], n, (m_hi, m_lo), slice(0, T), (4, 5, 6, 7, 0, 1, 2, 3),
                              "mixed" if m == 0 else None).then_inc(tile_done, 1)
                if m >= 2:
                    sum_squares(NORM2, KD, 2, False, m - 2)
            sum_squares(NORM2, KD, 2, False, N_OUT - 2)
            sum_squares(NORM2, KD, 2, False, N_OUT - 1)

            def product(b, to):
                for t in range(2):
                    n = 0
                    for ws, xs in ((s_hi, x_hi), (s_hi, x_lo), (s_lo, x_hi)):
                        for k in range(KD):
                            last = nc.tensor.matmul(to[:, 512 * t:512 * t + 512], ws[b][:, t, k, :], xs[:, k, :],
                                                    start=(n == 0), stop=(n == 3 * KD - 1))
                            n += 1
                last.then_inc(prod_done, 1)

            pe.wait_ge(xlo_ready, KD)
            pe.wait_ge(resid_ready, N_OUT)
            pe.wait_ge(keys_loaded, 16)
            def two_heads(g):
                for b in range(2):
                    pe.wait_ge(lo_ready, 2 * g + b + 1)
                    if not isinstance(g, int):
                        pe.wait_ge(prod_taken, 2 * g)
                    product(b, bank[b])
                for b in range(2):
                    pe.wait_ge(prod_taken, 2 * g + b + 1)
                    if not isinstance(g, int):
                        pe.wait_ge(keyscore_copied, 2 * g)
                    for t in range(QT):
                        for side in range(2):
                            last = nc.tensor.matmul(bank[2 + b][:, (2 * t + side) * NK:(2 * t + side + 1) * NK],
                                                    qk[:, b, side, 128 * t:128 * t + 128], keys[:, side, :],
                                                    start=True, stop=True)
                    last.then_inc(keyscore_done, 1)

            two_heads(0)
            with pe.Fori(1, PHEADS // 2) as g:
                two_heads(g)

            def u_product(c, b):
                pe.wait_ge(lo_ready, c + PHEADS + 1)
                pe.wait_ge(prod_taken, c + PHEADS - 1)
                product(b, bank[b])

            with pe.Fori(0, ADV // 2) as i:
                for b in range(2):
                    u_product(2 * i + b, b)

            pe.wait_ge(choice_ready, 1)
            pe.wait_ge(prod_taken, ADV + PHEADS)
            pe.wait_ge(keyscore_copied, PHEADS)
            for a in range(3):
                for t in range(QT):
                    src = expert[:, a, t] if a < 2 else best[:, t]
                    last = nc.tensor.transpose(bank[a][:, 128 * t:128 * t + 128], src.rearrange("p h s -> p (h s)"), ident)
                last.then_inc(pick_done, 1)

            pe.wait_ge(pick_copied, 4)

            def gate_matrices(i):
                for g in range(GROUPS):
                    pe.wait_ge(onehot_hi_ready, GROUPS * i + g + 1)
                    if g % 4 < 3:
                        pe.wait_ge(onehot_lo_ready, 3 * GROUPS // 4 * i + g - g // 4 + 1)
                    if not isinstance(i, int) or g > 1:
                        pe.wait_ge(gmat_staged, GROUPS * i + g - 1)
                    for t in range(GROUP):
                        to = bank[2 + g % 2][:, t * NK:(t + 1) * NK]
                        row = onehot[:, g % SLOTS, 0, :, t]
                        nc.tensor.matmul(to, row, onehot[:, g % SLOTS, 2, :, t], start=True, stop=False)
                        last = nc.tensor.matmul(to, row, onehot[:, g % SLOTS, 1, :, t], start=False, stop=True)
                    last.then_inc(gmat_done, 1)

            gate_matrices(0)
            with pe.Fori(1, T // HALF) as i:
                gate_matrices(i)

            def out_product(c, b):
                pe.wait_ge(vlo_ready, c + 1)
                pe.wait_ge(wlo_ready, c + 1)
                for m in range(KD):
                    pe.wait_ge(out_free, KD * c + m + 1)
                    to = bank[2 + m % 4 // 2][:, 512 * (m % 2):512 * (m % 2) + 512]
                    n = 0
                    for t in range(2):
                        for vs, ws in ((v_hi, w_hi), (v_hi, w_lo), (v_lo, w_hi)):
                            last = nc.tensor.matmul(to, vs[:, b, t, 128 * m:128 * m + 128], ws[:, b, t, :],
                                                    start=(n == 0), stop=(n == 5))
                            n += 1
                    last.then_inc(out_done, 1)

            with pe.Fori(0, (CHUNKS - ADV) // 2) as i:
                for b in range(2):
                    u_product(2 * i + b + ADV, b)
                    out_product(2 * i + b, b)
            with pe.Fori((CHUNKS - ADV) // 2, CHUNKS // 2) as i:
                for b in range(2):
                    out_product(2 * i + b, b)

            pe.wait_ge(prod_taken, CHUNKS + PHEADS)
            sum_squares(NORMF, KD, 0, False)

        @block.scalar
        def _(sc):
            def square(n, k, src):
                q = SQ_FROM[n] + k
                if q >= 2:
                    ends = sum(SQ_FROM[m + 1] <= q - 2 + 1 for m in range(6))
                    if ends:
                        sc.wait_ge(sum_ready, ends)
                    sc.wait_ge(sq_summed, q - 1 - ends)
                to = (sq if n != NORMF else fin_sq)[:, q % 2, 0:src.shape[-1]]
                nc.scalar.activation(to, src, ACT.Square).then_inc(sq_ready, 1)

            def root(n, pair, width, count):
                sc.wait_ge(sum_ready, n + 1)
                if n >= 2:
                    sc.wait_ge(norm_applied, n - 1)
                to = rstd[:, n % 2, 0:width] if n != NORMF else fin_r[:, 0:width]
                src = bank[pair][:, 0:width]
                if width == L:
                    to, src = halves(to), across(bank[pair])
                nc.scalar.activation(to, src, ACT.Sqrt, bias=eps[:, :],
                                     scale=1.0 / count).then_inc(root_ready, 1)

            sc.wait_ge(meta_loaded, 16)
            for k in range(KD):
                sc.wait_ge(x_loaded[k // 2], 16)
                square(NORM1, k, hT[:, k, :])

            def tile_hi(n):
                sc.wait_ge(w_loaded[n % WRING], 16 * (n // WRING + 1))
                if n >= 2:
                    sc.wait_ge(tile_done, n - 1 + (N_QKV if n - 2 >= N_IN else 0))
                nc.scalar.activation(w_hi_t[:, n % 2], wring[:, n % WRING], ACT.Copy).then_inc(wt_hi, 1)

            def block_hi(k, to):
                sc.wait_ge(blk_ready, k + 1)
                nc.scalar.activation(to, xn_f[:, k % 2, 0:to.shape[-1]], ACT.Copy).then_inc(blk_hi, 1)

            tile_hi(0)
            tile_hi(1)
            sc.wait_ge(eps_set, 1)
            root(NORM1, 2, L, D)
            for k in range(KD):
                block_hi(k, h_hi[:, k, :])

            def take(n, to, src, scale=1.0):
                sc.wait_ge(tile_done, n + 1)
                nc.scalar.activation(to, src, ACT.Copy, scale=scale).then_inc(copied, 1)

            for n, (to, width) in enumerate(((c_q[:, 0, :], T), (c_q[:, 1, :], T), (c_kv[:, :], L), (kr_in[:, 0, :], L),
                                             (kr_in[:, 1, :], L))):
                tile_hi(n + 2)
                take(n, to if width == T else halves(to), bank[n % 2][:, 0:T] if width == T else across(bank[n % 2]))
            sc.wait_ge(copied, 3)
            for k in range(2):
                square(NORMQ, k, c_q[:, k, :])
            for j in range(4):
                n = 5 + 3 * j
                if j:
                    sc.wait_ge(z_ready, j)
                tile_hi(n + 2)
                take(n, halves(cgate[:, :]), across(bank[n % 2]))
                tile_hi(n + 3)
                tile_hi(n + 4)
                take(n + 2, bgate[:, j, :], bank[n % 2][:, 0:T])
                if j == 0:
                    square(NORMKV, 0, c_kv[:, :])
                    root(NORMQ, 3, T, QL)
                    root(NORMKV, 2, L, KVL)
            for m in range(N_QKV):
                n = N_IN + m
                src = bank[n % 2]
                if m < 4:
                    take(n, qn[:, m, :], src[:, 0:T], -SCALE)
                elif m < 8:
                    take(n, qr_in[:, m - 4, :], src[:, 0:T], -SCALE)
                elif m < 12:
                    take(n, halves(kn[:, m - 8, :]), across(src))
                elif m < 16:
                    take(n, v_att[:, m - 12, :], src[:, 0:T])
                else:
                    take(n, v_meta[:, :], src[0:META, 0:T])

            for k in range(4):
                sc.wait_ge(conv_ready, k + 1)
                square(NORMC, k, conv[:, k, :])
            root(NORMC, 2, T, DC)

            sc.wait_ge(tile_done, N_PROJ)
            sc.wait_ge(qrope_ready, 1)
            sc.wait_ge(krope_ready, 1)

            def copy_transposed(n):
                h, i = n // QT, n % QT
                sc.wait_ge(pt_ready, n + 1)
                if h >= 2:
                    sc.wait_ge(pv_ready, h - 1)
                nc.scalar.activation(ptr[:, h % 2, 0:i + 1, 128 * i:128 * i + 128],
                                     turn_bank(n)[:, 0:128 * (i + 1)].rearrange("p (j q) -> p j q", q=128), ACT.Copy)
                nc.scalar.activation(ptm[:, h % 2, 128 * i:128 * i + 128], meta_block(n), ACT.Copy).then_inc(pt_copied, 1)

            def exponentiate(n):
                i = n % QT
                width = 128 * (i + 1) + META
                sc.wait_ge(bias_ready, n + 1)
                if n >= 4:
                    sc.wait_ge(pt_ready, n - 3)
                nc.scalar.activation(probs[:, n % 4, 0:width], score_banks(i)[:, 0:width], ACT.Exp,
                                     bias=negmax[:, n:n + 1], scale=-1.0,
                                     accum_out=rowsum[:, 0, n:n + 1]).then_inc(probs_ready, 1)

            exponentiate(0)
            for n in range(N_ATT):
                if n + 1 < N_ATT:
                    exponentiate(n + 1)
                if n in MIX_STEPS:
                    k = MIX_STEPS.index(n)
                    block_hi(KD + k, m_hi[:, 4 + k, :])
                copy_transposed(n)

            for k in range(4):
                sc.wait_ge(pv_copied, k + 1)
                square(NORMA, k, att[:, k, :])
            root(NORMA, 3, T, DC)
            for k in range(4):
                block_hi(KD + 4 + k, m_hi[:, k, :])
            for k in range(KD):
                if k < N_OUT - 2:
                    tile_hi(N_IN + k + 2)
                sc.wait_ge(resid_ready, k + 1)
                square(NORM2, k, acc[:, k, :])
            root(NORM2, 2, T, D)

            def split_hi(c, b):
                n = c + PHEADS
                sc.wait_ge(raw_loaded[b], 16 * ((n - b) // 2 + 1) if isinstance(n, int) else 8 * (n - b) + 16)
                if not (isinstance(n, int) and n < 2):
                    sc.wait_ge(prod_done, n - 1)
                nc.scalar.activation(s_hi[b][:, :, :, :], raw[b][:, :, :, :], ACT.Copy).then_inc(hi_ready, 1)

            sc.wait_ge(tile_done, N_PROJ + N_OUT)
            for k in range(KD):
                sc.wait_ge(xf_ready, k + 1)
                nc.scalar.activation(x_hi[:, k, :], xtmp[:, k % 2, :], ACT.Copy).then_inc(xhi_ready, 1)
                if k == 1:
                    split_hi(-PHEADS, 0)
            for h in range(PHEADS):
                split_hi(h + 1 - PHEADS, (h + 1) % 2)
                sc.wait_ge(prod_done, h + 1)
                if h >= 2:
                    sc.wait_ge(keyscore_done, h - 1)
                nc.scalar.activation(qk[:, h % 2], bank[h % 2][:, :].rearrange("p (s t) -> p s t", s=2),
                                     ACT.Copy).then_inc(prod_taken, 1)
                sc.wait_ge(keyscore_done, h + 1)
                if h >= 4:
                    sc.wait_ge(keyscore_taken, h - 3)
                nc.scalar.activation(score[:, h % 4], bank[2 + h % 2][:, :].rearrange("p (t s n) -> p t s n", t=QT, s=2),
                                     ACT.Copy).then_inc(keyscore_copied, 1)

            def gelu(c, b, slot):
                wait_apart(sc, "act", prod_done, c + PHEADS + 1)
                nc.scalar.activation(act[:, slot].rearrange("p s t n -> p (s t n)"), bank[b][:, :],
                                     ACT.Gelu_apprx_tanh).then_inc(prod_taken, 1)

            for c in range(ADV):
                split_hi(c + 1, (c + 1) % 2)
                gelu(c, c % 2, slice(c, c + 1))

            sc.wait_ge(shifted, 1)
            nc.scalar.activation(best[:, :, :, :], best[:, :, :, :], ACT.Exp).then_inc(exps_ready, 1)
            for a in range(2):
                sc.wait_ge(pick_done, a + 1)
                nc.scalar.activation(pick[:, a, :], bank[a][:, 0:T], ACT.Copy).then_inc(pick_copied, 1)
            sc.wait_ge(pick_done, 3)
            nc.scalar.activation(pgate[:, :], bank[2][:, 0:T], ACT.Copy, scale=GSCALE).then_inc(pick_copied, 1)
            nc.scalar.activation(pick[:, 2, :], bank[2][:, 0:T], ACT.Copy, scale=GSCALE).then_inc(pick_copied, 1)

            def stage_half(q, s):
                if not isinstance(q, int):
                    sc.wait_ge(stage_stored[s], 16 * q)
                with sc.Fori(0, GROUPS // 2) as i:
                    for r in range(2):
                        wait_apart(sc, "act", gmat_done, (2 * q + s) * GROUPS + 2 * i + r + 1)
                        nc.scalar.activation(
                            stage[:, s, :, bass.ds(GROUP * (2 * i + r), GROUP)].rearrange("p j t -> p t j"),
                            bank[2 + r][:, :].rearrange("p (t j) -> p t j", t=GROUP), ACT.Copy,
                            scale=1.0 / GSCALE).then_inc(gmat_staged, 1)
                sc.wait_ge(gmat_staged, (2 * q + s + 1) * GROUPS)
                sc.dma_start(gates_dram[bass.ds(2 * q + s, 1)].rearrange("q i j t -> (q i) j t"),
                             stage[:, s]).then_inc(stage_stored[s], 16)

            stage_half(0, 0)
            stage_half(0, 1)
            with sc.Fori(1, T // HALF // 2) as q:
                for s in range(2):
                    stage_half(q, s)

            def out_hi(c, b, slot):
                sc.wait_ge(v_loaded[b], 16 * (c // 2) + 16 if isinstance(c, int) else 8 * (c - b) + 16)
                if not (isinstance(c, int) and c < 2):
                    sc.wait_ge(out_done, KD * (c - 1))
                nc.scalar.activation(v_hi[:, b], v_raw[:, b], ACT.Copy).then_inc(vhi_ready, 1)
                wait_apart(sc, "act", w_ready, c + 1)
                nc.scalar.activation(w_hi[:, b].rearrange("p t n -> p (t n)"), act[:, slot].rearrange("p s t n -> p (s t n)"),
                                     ACT.Copy).then_inc(whi_ready, 1)

            for b in range(2):
                sc.wait_ge(stage_stored[b], 16 * (T // HALF // 2))
            out_hi(0, 0, slice(0, 1))

            def step(c, b, slot, next_slot, last=False):
                out_hi(c + 1, 1 - b, next_slot)
                if not last:
                    split_hi(c + ADV + 1, 1 - b)
                sc.wait_ge(wlo_ready, c + 1)
                gelu(c + ADV, b, slot)

            for c in range(2):
                step(c, c, slice(c, c + 1), slice(c + 1, c + 2))
            with sc.Fori(1, (CHUNKS - ADV) // 2 - 1) as i:
                for b in range(2):
                    c = 2 * i + b
                    step(c, b, bass.ds(c % ADV, 1), bass.ds((c + 1) % ADV, 1))
            for c in range(CHUNKS - ADV - 2, CHUNKS - ADV):
                step(c, c % 2, slice(c % ADV, c % ADV + 1), slice((c + 1) % ADV, (c + 1) % ADV + 1), last=c == CHUNKS - ADV - 1)
            for c in range(CHUNKS - ADV + 1, CHUNKS):
                out_hi(c, c % 2, slice(c % ADV, c % ADV + 1))

            sc.wait_ge(out_done, KD * CHUNKS)
            for k in range(KD):
                sc.wait_ge(out_free, 4 + KD * (CHUNKS - 1) + k + 1)
                square(NORMF, k, acc[:, k, :])
            root(NORMF, 0, T, D)

        @block.gpsimd
        def _(pool):
            def tile_lo(n):
                pool.wait_ge(wt_hi, n + 1)
                nc.gpsimd.tensor_tensor(w_lo_t[:, n % 2].rearrange("p k e -> p (k e)"),
                                        wring[:, n % WRING].rearrange("p k e -> p (k e)"),
                                        w_hi_t[:, n % 2].rearrange("p k e -> p (k e)").bitcast(f32), ALU.subtract).then_inc(wt_lo, 1)

            def block_lo(k, to, hi):
                pool.wait_ge(blk_hi, k + 1)
                nc.gpsimd.tensor_tensor(to, xn_f[:, k % 2, 0:to.shape[-1]], hi.bitcast(f32), ALU.subtract).then_inc(blk_lo, 1)

            tile_lo(0)
            tile_lo(1)
            for k in range(KD):
                block_lo(k, h_lo[:, k, :], h_hi[:, k, :])
            for n in range(2, 7):
                tile_lo(n)
            pool.wait_ge(rope_loaded, 16)
            pool.wait_ge(copied, 5)
            nc.gpsimd.tensor_tensor(kr[:, :], kr_in[:, 0, :], rope_t[:, 0, :], ALU.mult)
            nc.gpsimd.tensor_tensor(kr_in[:, 1, :], kr_in[:, 1, :], rope_t[:, 1, :], ALU.mult).then_inc(pool_step, 1)
            pool.wait_ge(pool_step, 1)
            nc.gpsimd.tensor_tensor(kr[:, :], kr[:, :], kr_in[:, 1, :], ALU.add).then_inc(krope_ready, 1)
            for n in range(7, N_IN + 2):
                tile_lo(n)
            for k in range(4):
                block_lo(KD + k, m_lo[:, 4 + k, :], m_hi[:, 4 + k, :])
            for k in range(4):
                block_lo(KD + 4 + k, m_lo[:, k, :], m_hi[:, k, :])
            for n in range(N_IN + 2, N_IN + N_OUT):
                tile_lo(n)

            for k in range(KD):
                pool.wait_ge(xhi_ready, k + 1)
                nc.gpsimd.tensor_tensor(x_lo[:, k, :], xtmp[:, k % 2, :], x_hi[:, k, :].bitcast(f32),
                                        ALU.subtract).then_inc(xlo_ready, 1)

            def lookup(h):
                pool.wait_ge(hit_ready, h + 1)
                for s in range(2):
                    last = nc.gpsimd.tensor_tensor(hit[:, h % 2, s], hit[:, h % 2, s],
                                                   topi_f[:, h % 2, s].unsqueeze(2).broadcast_to([128, QT, TOPK, TOPK]), ALU.mult)
                last.then_inc(hit_weighed, 1)

            def split_lo(c, b):
                n = c + PHEADS
                pool.wait_ge(hi_ready, n + 1)
                nc.gpsimd.tensor_tensor(s_lo[b][:, :, :, :].rearrange("p t k e -> p (t k e)"),
                                        raw[b][:, :, :, :].rearrange("p t k e -> p (t k e)"),
                                        s_hi[b][:, :, :, :].rearrange("p t k e -> p (t k e)").bitcast(f32),
                                        ALU.subtract).then_inc(lo_ready, 1)

            for n in range(PHEADS + ADV + 1):
                split_lo(n - PHEADS, n % 2)
                if 3 <= n < PHEADS + 3:
                    lookup(n - 3)

            pool.wait_ge(plo_ready, 1)

            def low_columns(i):
                for g in range(GROUPS):
                    if g % 4 < 3:
                        pool.wait_ge(onehot_hi_ready, GROUPS * i + g + 1)
                        lo = pick[:, 3, bass.ds(HALF * i + GROUP * g, GROUP)]
                        nc.gpsimd.tensor_tensor(onehot[:, g % SLOTS, 1], onehot[:, g % SLOTS, 1],
                                                lo.unsqueeze(1).broadcast_to([128, NK, GROUP]), ALU.mult).then_inc(onehot_lo_ready, 1)

            with pool.Fori(0, T // HALF) as i:
                low_columns(i)

            def weigh(c, b, slot):
                pool.wait_ge(gate_loaded[b], 16 * (c // 2) + 16 if isinstance(c, int) else 8 * (c - b) + 16)
                pool.wait_ge(prod_taken, c + PHEADS + 1)
                w = act[:, slot].rearrange("p s t (q n) -> p (s t) q n", n=HALF)
                nc.gpsimd.tensor_tensor(w, w, gate[:, b].rearrange("p q t n -> p t q n"), ALU.mult).then_inc(w_ready, 1)

            weigh(0, 0, slice(0, 1))
            with pool.Fori(0, (CHUNKS - ADV) // 2 - 1) as i:
                for b in range(2):
                    c = 2 * i + b
                    weigh(c + 1, 1 - b, bass.ds((c + 1) % ADV, 1))
                    split_lo(c + ADV + 1, 1 - b)
            for c in range(CHUNKS - ADV - 2, CHUNKS - 1):
                weigh(c + 1, (c + 1) % 2, slice((c + 1) % ADV, (c + 1) % ADV + 1))
                if c < CHUNKS - ADV - 1:
                    split_lo(c + ADV + 1, (c + 1) % 2)

        @block.vector
        def _(dve):
            steps = [0]

            def chain(ins):
                steps[0] += 1
                ins.then_inc(dve_step, 1)
                dve.wait_ge(dve_step, steps[0])

            def invert(n, width):
                dve.wait_ge(root_ready, n + 1)
                r = rstd[:, n % 2, 0:width] if n != NORMF else fin_r[:, 0:width]
                nc.vector.reciprocal(r, r).then_inc(rstd_ready, 1)
                dve.wait_ge(rstd_ready, n + 1)
                return r

            def apply(to, src, gain, r):
                return nc.vector.scalar_tensor_tensor(to, src, vec[:, gain:gain + 1], r, ALU.mult, ALU.mult)

            nc.vector.memset(eps[:, :], EPS).then_inc(eps_set, 1)
            dve.wait_ge(vec_loaded, 16)
            r = invert(NORM1, L)
            for k in range(KD):
                if k >= 2:
                    dve.wait_ge(blk_lo, k - 1)
                apply(xn_f[:, k % 2, :], hT[:, k, :], G1 + k, r).then_inc(blk_ready, 1)
            dve.wait_ge(blk_ready, KD)
            dve.sem_inc(norm_applied, 1)

            def conv_input(j):
                n = 6 + 3 * j
                dve.wait_ge(tile_done, n + 1)
                dve.wait_ge(copied, [6, 8, 10, 12][j])
                nc.vector.tensor_tensor(halves(zpad[:, j, 2:]), across(bank[n % 2]), halves(cgate[:, :]), ALU.mult)
                nc.vector.tensor_tensor(zpad[:, j, 0:2], across(bank[n % 2])[:, 1, L // 2 - 2:], cgate[:, L - 2:L],
                                        ALU.mult).then_inc(z_ready, 1)

            conv_input(0)
            r = invert(NORMQ, T)
            for k in range(2):
                last = apply(c_q[:, k, :], c_q[:, k, :], GQ + k, r)
            last.then_inc(norm_applied, 1)
            r = invert(NORMKV, L)
            apply(c_kv[:, :], c_kv[:, :], GKV, r).then_inc(norm_applied, 1)
            for j in range(1, 4):
                conv_input(j)

            dve.wait_ge(z_ready, 4)
            dve.wait_ge(copied, PROJ_COPIES - N_QKV)
            for j in range(4):
                last = nc.vector.tensor_scalar(conv[:, j, :], zpad[:, j, 0:T], vec[:, CW + j:CW + j + 1],
                                               vec[:, CB + j:CB + j + 1], ALU.mult, ALU.add)
            chain(last)
            for tap in (1, 2):
                for j in range(4):
                    w = CW + 4 * tap + j
                    last = nc.vector.scalar_tensor_tensor(conv[:, j, :], zpad[:, j, tap:T + tap], vec[:, w:w + 1],
                                                          conv[:, j, :], ALU.mult, ALU.add)
                chain(last)
            for j in range(4):
                nc.vector.tensor_tensor(conv[:, j, :], conv[:, j, :], bgate[:, j, 0:T], ALU.mult).then_inc(conv_ready, 1)

            dve.wait_ge(rope_loaded, 16)
            dve.wait_ge(copied, PROJ_COPIES - N_QKV + 8)
            for m in range(2):
                nc.vector.tensor_tensor(qr[:, m, :], qr_in[:, m, :], rope_t[:, 0, 0:T], ALU.mult)
            for m in range(2):
                last = nc.vector.tensor_tensor(qr_in[:, 2 + m, :], qr_in[:, 2 + m, :], rope_t[:, 1, 0:T], ALU.mult)
            chain(last)
            for m in range(2):
                last = nc.vector.tensor_tensor(qr[:, m, :], qr[:, m, :], qr_in[:, 2 + m, :], ALU.add)
            last.then_inc(qrope_ready, 1)

            dve.wait_ge(causal_loaded, 16)

            def maximum(n):
                i = n % QT
                width = 128 * (i + 1) + META
                s = score_banks(i)[:, 0:width]
                dve.wait_ge(scores_ready, n + 1)
                nc.vector.tensor_tensor_reduce(out=s, in0=s, in1=causal[:, T - 128 * (i + 1):L], scale=1.0, scalar=-NEG,
                                               op0=ALU.add, op1=ALU.min, accum_out=negmax[:, n:n + 1]).then_inc(bias_ready, 1)

            def normalise(n):
                width = 128 * (n % QT + 1) + META
                dve.wait_ge(probs_ready, n + 1)
                chain(nc.vector.reciprocal(rowsum[:, 1, n:n + 1], rowsum[:, 0, n:n + 1]))
                nc.vector.tensor_scalar(probs[:, n % 4, 0:width], probs[:, n % 4, 0:width], rowsum[:, 1, n:n + 1],
                                        None, ALU.mult).then_inc(probs_scaled, 1)

            def take_pair(p):
                dve.wait_ge(pv_ready, 2 * p + 2)
                nc.vector.tensor_copy(att[:, p, :], value_bank).then_inc(pv_copied, 1)

            def mix(n, src, gain, b, k):
                if k == 0:
                    invert(n, T)
                dve.wait_ge(blk_lo, b - 1)
                apply(xn_f[:, b % 2, 0:T], src[:, k, :], gain + k, rstd[:, n % 2, 0:T]).then_inc(blk_ready, 1)
                if k == 3:
                    dve.wait_ge(blk_ready, b + 1)
                    dve.sem_inc(norm_applied, 1)

            maximum(0)
            maximum(1)
            for n in range(N_ATT):
                if n + 2 < N_ATT:
                    maximum(n + 2)
                normalise(n)
                if n + 1 in MIX_STEPS:
                    k = MIX_STEPS.index(n + 1)
                    mix(NORMC, conv, GC, KD + k, k)
                if n % (2 * QT) == 2 and n > 2 * QT:
                    take_pair(n // (2 * QT) - 1)
            take_pair(3)
            for k in range(4):
                mix(NORMA, att, GA, KD + 4 + k, k)

            for m in range(N_OUT):
                dve.wait_ge(tile_done, N_PROJ + m + 1)
                nc.vector.tensor_tensor(acc[:, m, :], bank[m % 2][:, 0:T], hT[:, m, 0:T], ALU.add).then_inc(resid_ready, 1)

            r = invert(NORM2, T)
            dve.wait_ge(resid_ready, N_OUT)
            for k in range(KD):
                if k >= 2:
                    dve.wait_ge(xlo_ready, k - 1)
                apply(xtmp[:, k % 2, :], acc[:, k, :], G2 + k, r).then_inc(xf_ready, 1)
            dve.wait_ge(xf_ready, KD)
            dve.sem_inc(norm_applied, 1)

            first = steps[0]
            tails = 0

            def top16(values, vals, idx, scratch, link):
                n = len(values)
                for i in range(n):
                    last = nc.vector.max(vals[i][:, 0:8], values[i])
                link(last)
                for i in range(n):
                    nc.vector.max_index(idx[i][:, 0:8], vals[i][:, 0:8], values[i])
                    last = nc.vector.match_replace(scratch[i], vals[i][:, 0:8], values[i], NEG)
                link(last)
                for i in range(n):
                    last = nc.vector.max(vals[i][:, 8:16], scratch[i])
                link(last)
                for i in range(n):
                    last = nc.vector.max_index(idx[i][:, 8:16], vals[i][:, 8:16], scratch[i])
                return last

            def reduce_hits(h, b):
                wait_apart(dve, "dve", hit_weighed, h + 1)
                for s in range(2):
                    nc.vector.tensor_reduce(expert[:, s, :, bass.ds(h, 1), :].rearrange("p t h s -> p t (h s)"),
                                            hit[:, b, s], AX.X, ALU.add)

            PER_HEAD = 12
            with dve.Fori(0, PHEADS // 4) as g:
                for q in range(4):
                    h = 4 * g + q
                    done = [0]

                    def link(ins):
                        done[0] += 1
                        ins.then_inc(dve_step, 1)
                        wait_apart(dve, "dve", dve_step, first + PER_HEAD * h + done[0])

                    wait_apart(dve, "dve", keyscore_copied, h + 1)
                    both = [(t, s) for t in range(QT) for s in range(2)]
                    last = top16([score[:, q, t, s, :] for t, s in both], [topv[:, s, t, :] for t, s in both],
                                 [topi[:, s, t, :] for t, s in both], [rest[:, t, s, :] for t, s in both], link)
                    link(last)
                    dve.sem_inc(keyscore_taken, 1)
                    wide = cand[:, :, 0:WIDE * TOPK].rearrange("p t (a b) -> p t a b", a=WIDE)
                    tall = cand[:, :, WIDE * TOPK:NCAND].rearrange("p t (a b) -> p t a b", b=4)
                    nc.vector.tensor_tensor(wide, topv[:, 0, :, 0:WIDE].unsqueeze(3).broadcast_to([128, QT, WIDE, TOPK]),
                                            topv[:, 1].unsqueeze(2).broadcast_to([128, QT, WIDE, TOPK]), ALU.add)
                    nc.vector.tensor_copy(topi_f[:, q % 2], topi[:, :, :, :])
                    link(nc.vector.tensor_tensor(tall, topv[:, 0, :, WIDE:].unsqueeze(3).broadcast_to([128, QT, TOPK - WIDE, 4]),
                                                 topv[:, 1, :, 0:4].unsqueeze(2).broadcast_to([128, QT, TOPK - WIDE, 4]), ALU.add))
                    last = top16([cand[:, t] for t in range(QT)], [bestv[:, t, :] for t in range(QT)],
                                 [flat[:, t, :] for t in range(QT)], [cand2[:, t, :] for t in range(QT)], link)
                    if q:
                        reduce_hits(h - 1, (q - 1) % 2)
                    link(last)
                    nc.vector.tensor_copy(best[:, :, bass.ds(h, 1), :].rearrange("p t h s -> p t (h s)"), bestv[:, :, :])
                    nc.vector.tensor_scalar(digit[:, 0], flat[:, :, :], 2, None, ALU.logical_shift_right)
                    nc.vector.tensor_scalar(digit[:, 1], flat[:, :, :], 4, None, ALU.logical_shift_right)
                    nc.vector.tensor_scalar(digit[:, 2], flat[:, :, :], 12, None, ALU.bitwise_and)
                    link(nc.vector.tensor_scalar(flat[:, :, :], flat[:, :, :], TOPK * WIDE + 3, None, ALU.bitwise_and))
                    nc.vector.scalar_tensor_tensor(pos[:, 0], digit[:, 0], -12.0, digit[:, 1], ALU.add, ALU.max)
                    nc.vector.scalar_tensor_tensor(pos[:, 1], flat[:, :, :], float(TOPK * WIDE), digit[:, 2], ALU.is_lt, ALU.mult)
                    link(nc.vector.tensor_scalar(flat[:, :, :], flat[:, :, :], 3, None, ALU.bitwise_and))
                    link(nc.vector.tensor_tensor(pos[:, 1], pos[:, 1], flat[:, :, :], ALU.add))
                    for s in range(2):
                        last = nc.vector.tensor_tensor(hit[:, q % 2, s], pos[:, s].unsqueeze(3).broadcast_to([128, QT, TOPK, TOPK]),
                                                       iota[:, 0:TOPK].unsqueeze(1).unsqueeze(1).broadcast_to([128, QT, TOPK, TOPK]),
                                                       ALU.is_equal)
                    last.then_inc(hit_ready, 1)
                    if q == 3:
                        reduce_hits(h, 1)
                    assert done[0] == PER_HEAD, done[0]
            steps[0] = first + PER_HEAD * PHEADS

            gates = best[:, :, :, :].rearrange("p t h s -> p (t h) s")
            chain(nc.vector.tensor_copy(bsum[:, :], gates[:, :, 0]))
            nc.vector.tensor_tensor(gates, gates, bsum[:, :].unsqueeze(2).broadcast_to([128, QT * PHEADS, TOPK]),
                                    ALU.subtract).then_inc(shifted, 1)
            dve.wait_ge(exps_ready, 1)
            chain(nc.vector.tensor_reduce(bsum[:, :], gates, AX.X, ALU.add))
            chain(nc.vector.reciprocal(bsum[:, :], bsum[:, :]))
            nc.vector.tensor_tensor(gates, gates, bsum[:, :].unsqueeze(2).broadcast_to([128, QT * PHEADS, TOPK]),
                                    ALU.mult).then_inc(choice_ready, 1)

            for t in range(GROUP):
                last = nc.vector.tensor_copy(iotas[:, :, t], iota)
            chain(last)
            dve.wait_ge(pick_copied, 4)
            nc.vector.tensor_tensor(pick[:, 3, :], pgate[:, :], pick[:, 2, :], ALU.subtract).then_inc(plo_ready, 1)
            first_hot = steps[0]

            def onehots_of(i):
                for g in range(GROUPS):
                    def spread(a):
                        return pick[:, a, bass.ds(HALF * i + GROUP * g, GROUP)].unsqueeze(1).broadcast_to([128, NK, GROUP])

                    if not isinstance(i, int) or g >= SLOTS:
                        wait_apart(dve, "dve", gmat_done, GROUPS * i + g - SLOTS + 1)
                    hot = onehot[:, g % SLOTS]
                    nc.vector.tensor_tensor(hot[:, 1], iotas[:, :, :], spread(1), ALU.is_equal).then_inc(dve_step, 1)
                    nc.vector.tensor_tensor(hot[:, 0], iotas[:, :, :], spread(0), ALU.is_equal)
                    wait_apart(dve, "dve", dve_step, first_hot + GROUPS * i + g + 1)
                    last = nc.vector.tensor_tensor(hot[:, 2], hot[:, 1], spread(2), ALU.mult)
                    if g % 4 == 3:
                        last = nc.vector.tensor_tensor(hot[:, 1], hot[:, 1], spread(3), ALU.mult)
                    last.then_inc(onehot_hi_ready, 1)

            onehots_of(0)
            with dve.Fori(1, T // HALF) as i:
                onehots_of(i)

            def out_lo(c, b, slot):
                dve.wait_ge(vhi_ready, c + 1)
                nc.vector.tensor_tensor(v_lo[:, b], v_raw[:, b], v_hi[:, b].bitcast(f32), ALU.subtract).then_inc(vlo_ready, 1)
                dve.wait_ge(whi_ready, c + 1)
                nc.vector.tensor_tensor(w_lo[:, b].rearrange("p t n -> p (t n)"), act[:, slot].rearrange("p s t n -> p (s t n)"),
                                        w_hi[:, b].rearrange("p t n -> p (t n)").bitcast(f32), ALU.subtract).then_inc(wlo_ready, 1)

            def add_out(c):
                for m in range(KD):
                    dve.wait_ge(out_done, KD * c + m + 1)
                    nc.vector.tensor_tensor(acc[:, m, :], acc[:, m, :], bank[2 + m % 4 // 2][:, 512 * (m % 2):512 * (m % 2) + 512],
                                            ALU.add).then_inc(out_free, 1)

            for b in range(2):
                dve.wait_ge(stage_stored[b], 16 * (T // HALF // 2))
            dve.sem_inc(out_free, 4)
            out_lo(0, 0, slice(0, 1))
            with dve.Fori(0, CHUNKS // 2 - 1) as i:
                for b in range(2):
                    c = 2 * i + b
                    out_lo(c + 1, 1 - b, bass.ds((c + 1) % ADV, 1))
                    add_out(c)
            out_lo(CHUNKS - 1, 1, slice((CHUNKS - 1) % ADV, (CHUNKS - 1) % ADV + 1))
            add_out(CHUNKS - 2)
            add_out(CHUNKS - 1)

            r = invert(NORMF, T)
            for k in range(KD):
                apply(acc[:, k, :], acc[:, k, :], GF + k, r).then_inc(y_ready, 1)


def _rope_tables():
    half = ROPE // 2
    inv = (1.0 / (np.float32(10000.0) ** (np.arange(0, ROPE, 2, dtype=np.float32) / np.float32(ROPE)))).astype(np.float32)
    position = np.concatenate([np.arange(META, META + T), np.arange(META)]).astype(np.float32)
    angle = inv[:, None] * position[None, :]
    cos = np.concatenate([np.cos(angle)] * 2)
    sin = np.concatenate([-np.sin(angle), np.sin(angle)])
    return np.tile(np.stack([cos, sin], 1), (128 // ROPE, 1, 1)).astype(np.float32)


def _lay_out(x, meta_tokens, norm1_g, w_in, q_norm_g, w_uq, kv_norm_g, w_ukv, conv_w, conv_b, attn_out_g, conv_out_g,
             w_out, norm2_g, peer_w_query, peer_keys1, peer_keys2, peer_u, peer_v, final_g):
    c = np.ascontiguousarray

    def columns(g):
        return g.reshape(-1, 128).T

    def tiles(w):
        return w.reshape(w.shape[0] // 128, 128, -1, 128).transpose(2, 1, 0, 3)

    wi = w_in[0]
    o2, o3 = QL + KVL, QL + KVL + ROPE
    kr = wi[:, o2:o3]
    swapped = np.concatenate([kr[:, ROPE // 2:], kr[:, :ROPE // 2]], 1)
    parts = [wi[:, :o2]] + [kr] * 4 + [swapped] * 4
    bcu = [wi[:, o3 + n * DC:o3 + (n + 1) * DC] for n in range(3)]
    for j in range(4):
        parts += [bcu[n][:, 128 * j:128 * j + 128] for n in (1, 2, 0)]
    q = w_uq[0].reshape(QL, HEADS, NOPE + ROPE)
    q_rope = q[:, :, NOPE:]
    q_swap = np.concatenate([q_rope[:, :, ROPE // 2:], q_rope[:, :, :ROPE // 2]], 2)
    uq = np.concatenate([q[:, :, :NOPE].reshape(QL, -1), q_rope.reshape(QL, -1), q_swap.reshape(QL, -1)], 1)
    kv = w_ukv[0].reshape(KVL, HEADS, NOPE + VDIM)
    tri = np.where(np.arange(128)[None, :] <= np.arange(128)[:, None], 0.0, 1e30)
    zeros = np.zeros((128, 1))
    consts = np.concatenate([np.eye(128), np.tile(np.arange(128.0), (128, 1)), np.ones((128, 128)),
                             np.tile(zeros, (1, T - 128)), tri, np.tile(zeros, (1, META))], 1)
    return {
        "xT": c(x[0].T.reshape(KD, 128, T).transpose(1, 0, 2)),
        "metaT": c(meta_tokens.T.reshape(KD, 128, META).transpose(1, 0, 2)),
        "vecs": c(np.concatenate([columns(norm1_g[0]), columns(q_norm_g[0]), columns(kv_norm_g[0]), columns(attn_out_g[0]),
                                  columns(conv_out_g[0]), columns(norm2_g[0]), columns(final_g), columns(conv_w[0].reshape(-1)),
                                  columns(conv_b[0])], 1)),
        "consts": consts.astype(np.float32),
        "rope": _rope_tables(),
        "w_tiles": c(np.concatenate([tiles(np.concatenate(parts, 1)), tiles(w_out[0])])),
        "w_uq": c(tiles(uq).transpose(1, 0, 2, 3)),
        "w_ukv": c(np.concatenate([kv[:, :, :NOPE].reshape(KVL, -1), kv[:, :, NOPE:].reshape(KVL, -1)], 1)),
        "keysT": c(np.stack([peer_keys1[0].T, peer_keys2[0].T], 1)),
        "w_query": c(tiles(peer_w_query[0]).reshape(PHEADS, 2, 128, KD, 128).transpose(0, 2, 1, 3, 4)),
        "uT": c(peer_u[0].reshape(128, CHUNKS, 2, KD, 128).transpose(1, 4, 2, 3, 0)),
        "v": c(peer_v[0]),
    }


def kernel(**inputs):
    import concourse.bacc as bacc
    from concourse.bass_utils import run_bass_kernel_spmd

    arrays = _lay_out(**{n: np.asarray(a) for n, a in inputs.items()})
    nc = bacc.Bacc("TRN2", target_bir_lowering=False, num_devices=1)
    args = {n: nc.dram_tensor(n, a.shape, mybir.dt.from_np(a.dtype), kind="ExternalInput").ap() for n, a in arrays.items()}
    yT = nc.dram_tensor("yT", (128, KD, T), mybir.dt.float32, kind="ExternalOutput").ap()
    hymba_peer_kernel(nc, **args, yT=yT)
    result = run_bass_kernel_spmd(nc, [arrays], core_ids=[0])
    y = result.results[0]["yT"]
    return np.ascontiguousarray(y.transpose(2, 1, 0).reshape(1, T, D))
```

```python
from contextlib import ExitStack

import concourse.bass as bass
import numpy as np
from concourse import mybir

D = 1024
T = 512
META = 16
L = T + META
KD = D // 128
EPS = 1e-6
HEADS, NOPE, ROPE, VDIM = 8, 64, 32, 64
QL, KVL = 256, 128
DC = 512
NK = 128
TOPK = 16
QT = T // 128
SCALE = float(NOPE + ROPE) ** -0.5
NEG = -3.0e38

N_IN = 17
N_OUT = 8
WRING = 4
PHEADS = 8
WIDE = 4
NCAND = WIDE * TOPK + (TOPK - WIDE) * 4
ADV = 10
EARLY = 6
SOLO = ADV - EARLY
CHUNKS = NK // 2
HALF = 64
GROUP = 8
SLOTS = 4
GROUPS = HALF // GROUP
GSCALE = 4096.0

G1, GQ, GKV, GA, GC, G2, GF, CW, CB, NVEC = 0, 8, 10, 11, 15, 19, 27, 35, 47, 51


def hymba_peer_kernel(nc, xT, metaT, vecs, consts, rope, w_tiles, w_uq, w_ukv, keysT, w_query, uT, v, yT):
    f32, f32r, f16, u32 = mybir.dt.float32, mybir.dt.float32r, mybir.dt.float16, mybir.dt.uint32
    ALU, ACT, AX = mybir.AluOpType, mybir.ActivationFunctionType, mybir.AxisListType

    gates_dram = nc.dram_tensor("gates_dram", (T // HALF, 128, NK, HALF), f32, kind="Internal").ap()
    gates_of = gates_dram.rearrange("q i j t -> i q j t")
    v_tiles = v.rearrange("(i j) d -> i j d", j=NK)

    ctx = ExitStack()
    with ctx:
        def sb(stack, name, shape, dt=f32):
            return stack.enter_context(nc.sbuf_tensor(name, shape, dt))

        const = sb(ctx, "const", [128, 3 * 128])
        ident, iota, ones = const[:, 0:128], const[:, 128:256], const[:, 256:384]
        vec = sb(ctx, "vec", [128, NVEC])
        eps = sb(ctx, "eps", [128, 1])
        early = ExitStack()
        qr_in = sb(early, "qr_in", [128, 4, T])
        wuq_t = sb(early, "wuq_t", [128, 8, 2, 128])
        early.close()
        acc = sb(ctx, "acc", [128, KD, T])

        front = ExitStack()
        normed = ExitStack()
        h_hi = sb(normed, "h_hi", [128, KD, L], f32r)
        h_lo = sb(normed, "h_lo", [128, KD, L], f32r)
        normed.close()
        m_hi = sb(front, "m_hi", [128, KD, T], f32r)
        m_lo = sb(front, "m_lo", [128, KD, T], f32r)
        spare = sb(front, "spare", [128, 2 * KD * META])
        qn = sb(front, "qn", [128, 4, T])
        qr = sb(front, "qr", [128, 2, T])
        hT = sb(front, "hT", [128, KD, L])
        wring = sb(front, "wring", [128, WRING, KD, 128])
        w_hi_t = sb(front, "w_hi_t", [128, 2, KD, 128], f32r)
        w_lo_t = sb(front, "w_lo_t", [128, 2, KD, 128], f32r)
        kn = sb(front, "kn", [128, 4, L])
        kr = sb(front, "kr", [128, L])
        v_att = sb(front, "v_att", [128, QT, DC])
        v_meta = sb(front, "v_meta", [META, DC])
        conv = sb(front, "conv", [128, 4, T])
        causal = sb(front, "causal", [128, L])
        sq = sb(front, "sq", [128, 2, L])
        rstd = sb(front, "rstd", [128, 2, L])
        rowsum = sb(front, "rowsum", [128, 2, HEADS * QT])
        negmax = sb(front, "negmax", [128, HEADS * QT])
        xn_f = sb(front, "xn_f", [128, 2, T])
        r_in = sb(front, "r_in", [128, 2, L])
        proj = ExitStack()
        c_q = sb(proj, "c_q", [128, 2, T])
        c_kv = sb(proj, "c_kv", [128, L])
        kr_in = sb(proj, "kr_in", [128, 2, L])
        cgate = sb(proj, "cgate", [128, L])
        rope_t = sb(proj, "rope_t", [128, 2, L])
        wukv_t = sb(proj, "wukv_t", [128, 2 * DC])
        zpad = sb(proj, "zpad", [128, 4, 2 + L])
        bgate = sb(proj, "bgate", [128, 4, T])
        proj.close()
        probs = sb(front, "probs", [128, 4, L])
        ptr = sb(front, "ptr", [128, 2, QT, T])
        ptm = sb(front, "ptm", [META, 2, T])
        att = sb(front, "att", [128, 4, T])
        front.close()

        main = ExitStack()
        x_hi = sb(main, "x_hi", [128, KD, T], f32r)
        x_lo = sb(main, "x_lo", [128, KD, T], f32r)
        act = sb(main, "act", [128, ADV, 2, T])
        raw, s_hi, s_lo = [None, None], [None, None], [None, None]
        raw[0], s_hi[0], s_lo[0] = (sb(main, "raw0", [128, 2, KD, 128]), sb(main, "s_hi0", [128, 2, KD, 128], f32r),
                                    sb(main, "s_lo0", [128, 2, KD, 128], f32r))
        onehots = ExitStack()
        onehot = sb(onehots, "onehot", [128, SLOTS, 3, NK, GROUP], f16)
        onehots.close()
        raw[1], s_hi[1], s_lo[1] = (sb(main, "raw1", [128, 2, KD, 128]), sb(main, "s_hi1", [128, 2, KD, 128], f32r),
                                    sb(main, "s_lo1", [128, 2, KD, 128], f32r))
        choose = ExitStack()
        keys = sb(choose, "keys", [128, 2, NK])
        qk = sb(choose, "qk", [128, 2, 2, T])
        score = sb(choose, "score", [128, 4, QT, 2, NK])
        rest = sb(choose, "rest", [128, QT, 2, NK])
        topv = sb(choose, "topv", [128, 2, QT, TOPK])
        topi = sb(choose, "topi", [128, 2, QT, TOPK], u32)
        cand = sb(choose, "cand", [128, QT, NCAND])
        cand2 = sb(choose, "cand2", [128, QT, NCAND])
        digit = sb(choose, "digit", [128, 3, QT, TOPK], u32)
        bestv = sb(choose, "bestv", [128, QT, TOPK])
        flat = sb(choose, "flat", [128, QT, TOPK], u32)
        pos = sb(choose, "pos", [128, 2, QT, TOPK])
        norming = ExitStack()
        xtmp = sb(norming, "xtmp", [128, KD, T])
        norming.close()
        hit = sb(choose, "hit", [128, 2, 2, QT, TOPK, TOPK])
        topi_f = sb(choose, "topi_f", [128, 2, 2, QT, TOPK])
        expert = sb(choose, "expert", [128, 2, QT, PHEADS, TOPK])
        best = sb(choose, "best", [128, QT, PHEADS, TOPK])
        bsum = sb(choose, "bsum", [128, QT * PHEADS])
        choose.close()
        gatep = ExitStack()
        gates_in = ExitStack()
        pgate = sb(gates_in, "pgate", [128, T])
        gates_in.close()
        stage = sb(gatep, "stage", [128, 2, NK, HALF])
        pick = sb(gatep, "pick", [128, 4, T], f16)
        iotas = sb(gatep, "iotas", [128, NK, GROUP], f16)
        gatep.close()
        v_raw = sb(main, "v_raw", [128, 2, D])
        v_hi = sb(main, "v_hi", [128, 2, 2, D], f32r)
        gate = sb(main, "gate", [128, 2, T // HALF, 2, HALF])
        v_lo = sb(main, "v_lo", [128, 2, 2, D], f32r)
        w_hi = sb(main, "w_hi", [128, 2, 2, T], f32r)
        w_lo = sb(main, "w_lo", [128, 2, 2, T], f32r)
        main.close()
        fin = ExitStack()
        fin_sq = sb(fin, "fin_sq", [128, 2, T])
        fin_r = sb(fin, "fin_r", [128, T])
        fin.close()
        bank = [ctx.enter_context(nc.psum_tensor(f"bank{p}", [128, 1024], f32)) for p in range(4)]

        def across(pair):
            return pair[:, :].rearrange("p (h n) -> p h n", h=2)[:, :, 0:L // 2]

        def halves(columns):
            return columns.rearrange("p (h n) -> p h n", h=2)

        def spans(with_meta):
            if with_meta:
                return [(slice(h * L // 2, (h + 1) * L // 2), slice(512 * h, 512 * h + L // 2)) for h in range(2)]
            return [(slice(0, T), slice(0, T))]

        def sem(name):
            return ctx.enter_context(nc.semaphore(name))

        x_loaded = [sem(f"x_loaded{k}") for k in range(4)]
        meta_loaded, vec_loaded, const_loaded, causal_loaded, rope_loaded = (
            sem("meta_loaded"), sem("vec_loaded"), sem("const_loaded"), sem("causal_loaded"), sem("rope_loaded"))
        wuq_loaded, wukv_loaded, keys_loaded = sem("wuq_loaded"), sem("wukv_loaded"), sem("keys_loaded")
        w_loaded = [sem(f"w_loaded{s}") for s in range(WRING)]
        raw_loaded = [sem("raw_loaded0"), sem("raw_loaded1")]
        v_loaded = sem("v_loaded")
        gate_loaded = [sem("gate_loaded0"), sem("gate_loaded1")]
        stage_stored = [[sem(f"stage_stored_j{p}_{s}") for s in range(2)] for p in range(2)]
        y_stored = sem("y_stored")
        sq_ready, sq_summed, sum_ready, root_ready = sem("sq_ready"), sem("sq_summed"), sem("sum_ready"), sem("root_ready")
        rstd_ready, norm_applied = sem("rstd_ready"), sem("norm_applied")
        eps_set = sem("eps_set")
        tile_done, in_taken, copied, conv_ready, resid_ready = (
            sem("tile_done"), sem("in_taken"), sem("copied"), sem("conv_ready"), sem("resid_ready"))
        h_hi_ready, h_lo_ready = sem("h_hi_ready"), sem("h_lo_ready")
        blk_ready, blk_hi, blk_lo = sem("blk_ready"), sem("blk_hi"), sem("blk_lo")
        wt_hi, wt_lo = sem("wt_hi"), sem("wt_lo")
        krope_ready, qrope_ready = sem("krope_ready"), sem("qrope_ready")
        scores_ready, bias_ready, probs_ready, probs_scaled = (
            sem("scores_ready"), sem("bias_ready"), sem("probs_ready"), sem("probs_scaled"))
        pt_ready, pt_copied, pv_ready, pv_copied = sem("pt_ready"), sem("pt_copied"), sem("pv_ready"), sem("pv_copied")
        xf_ready, xhi_ready, xlo_ready, xlo_pool_ready = (
            sem("xf_ready"), sem("xhi_ready"), sem("xlo_ready"), sem("xlo_pool_ready"))
        hi_ready, lo_ready, prod_done, prod_taken = sem("hi_ready"), sem("lo_ready"), sem("prod_done"), sem("prod_taken")
        keyscore_done, keyscore_copied, keyscore_taken = sem("keyscore_done"), sem("keyscore_copied"), sem("keyscore_taken")
        hit_ready, hit_weighed = sem("hit_ready"), sem("hit_weighed")
        shifted, exps_ready, choice_ready = sem("shifted"), sem("exps_ready"), sem("choice_ready")
        pick_done, pick_copied = sem("pick_done"), sem("pick_copied")
        iotas_ready, pgate_ready, plo_ready = sem("iotas_ready"), sem("pgate_ready"), sem("plo_ready")
        onehot_hi_ready, onehot_lo_ready = sem("onehot_hi_ready"), sem("onehot_lo_ready")
        gmat_done, gmat_staged = sem("gmat_done"), sem("gmat_staged")
        w_ready, whi_ready, wlo_ready, vhi_ready, vlo_ready = (
            sem("w_ready"), sem("whi_ready"), sem("wlo_ready"), sem("vhi_ready"), sem("vlo_ready"))
        out_done, out_free = sem("out_done"), sem("out_free")
        y_ready = sem("y_ready")
        dve_step, act_step, pool_step = sem("dve_step"), sem("act_step"), sem("pool_step")

        passed = {e: sem(f"passed_{e}") for e in ("act", "dve")}

        def wait_apart(eng, name, s, value):
            eng.wait_ge(s, value)
            eng.sem_inc(passed[name], 1)

        def wait_taken(eng, n):
            if n < N_IN:
                eng.wait_ge(in_taken, n + 1)
            else:
                eng.wait_ge(copied, n - N_IN + 1)

        N_QKV = 17
        N_PROJ = N_IN + N_QKV
        NORM1, NORMQ, NORMKV, NORMC, NORMA, NORM2, NORMF = range(7)
        SQ_FROM = [0, 8, 10, 11, 15, 19, 27]
        N_ATT = HEADS * QT
        MIX_STEPS = [9, 11, 13, 15]

        SOLO_FROM = PHEADS + EARLY
        POOL_BLOCKS = (0, 2, 4)
        LOOKUP_AFTER = [3, 4, 5, 7, 8, 10, 12, 13]

        def buffer_of(n):
            return 0 if SOLO_FROM <= n < SOLO_FROM + SOLO else n % 2

        def before(n, solo=False):
            if not isinstance(n, int):
                return n - 1 if solo else n - 2
            return max(m for m in range(n) if buffer_of(m) == buffer_of(n))

        def loads_until(n, b, solo=False):
            if isinstance(n, int):
                return 16 * sum(buffer_of(m) == b for m in range(n + 1))
            if solo:
                return 16 * n - 16 * (SOLO_FROM - SOLO_FROM // 2 - 1)
            return 8 * (n - b) + 16 * (1 - SOLO // 2 if b else 1 + SOLO // 2)

        def score_banks(i):
            return (bank[0][:, 0:512], bank[0][:, 512:1024], bank[1][:, 0:512], bank[3])[i]

        def turn_bank(n):
            return bank[1][:, 512:1024] if n % 2 else bank[2][:, 0:512]

        value_bank = bank[2][:, 512:1024]

        def meta_block(n):
            i = n % QT
            return turn_bank(n)[0:META, 128 * (i + 1):128 * (i + 2)] if i < QT - 1 else bank[3][0:META, 640:768]

        def wait_stored(eng, p, buffers=(0, 1)):
            for s in buffers:
                eng.wait_ge(stage_stored[p][s], 16 * (T // HALF // 2))

        def pick_bank(a):
            return bank[3][:, 0:T] if a == 2 else bank[2][:, 512 * a:512 * a + T]

        block = ctx.enter_context(nc.Block())

        @block.sync
        def _(sp):
            sp.dma_start(vec[:, :], vecs).then_inc(vec_loaded, 16)
            sp.dma_start(hT[:, :, T:L], metaT).then_inc(meta_loaded, 16)

            def load_w(n):
                if n >= WRING:
                    sp.wait_ge(wt_lo, n - WRING + 1)
                sp.dma_start(wring[:, n % WRING, :, :], w_tiles[n]).then_inc(w_loaded[n % WRING], 16)

            for k in range(4):
                sp.dma_start(hT[:, 2 * k:2 * k + 2, 0:T], xT[:, 2 * k:2 * k + 2, :]).then_inc(x_loaded[k], 16)
                if k == 0:
                    load_w(0)
            sp.dma_start(const[:, :], consts[:, 0:384]).then_inc(const_loaded, 16)
            for n in range(1, WRING):
                load_w(n)
            sp.dma_start(rope_t[:, :, :], rope).then_inc(rope_loaded, 16)
            sp.dma_start(wuq_t[:, :, :, :], w_uq).then_inc(wuq_loaded, 16)
            sp.dma_start(wukv_t[:, :], w_ukv).then_inc(wukv_loaded, 16)
            sp.dma_start(causal[:, :], consts[:, 384:384 + L]).then_inc(causal_loaded, 16)
            for n in range(WRING, N_IN + N_OUT):
                load_w(n)

            sp.wait_ge(resid_ready, N_OUT)

            def load_query(h):
                sp.dma_start(raw[h % 2][:, :, :, :], w_query[h]).then_inc(raw_loaded[h % 2], 16)

            def load_u(c, b):
                sp.wait_ge(lo_ready, before(c + PHEADS) + 1)
                sp.dma_start(raw[b][:, :, :, :], uT[bass.ds(c, 1)].rearrange("c p t k e -> (c p) t k e")).then_inc(raw_loaded[b], 16)

            def load_v(c):
                if not isinstance(c, int) or c:
                    sp.wait_ge(vlo_ready, c)
                sp.dma_start(v_raw[:, :, :], v_tiles[:, bass.ds(2 * c, 2), :]).then_inc(v_loaded, 16)

            def load_gate(c, b):
                if not isinstance(c, int) or c >= 2:
                    sp.wait_ge(w_ready, c - 1)
                sp.dma_start(gate[:, b], gates_of[:, :, bass.ds(2 * c, 2), :]).then_inc(gate_loaded[b], 16)

            for h in range(PHEADS):
                if h >= 2:
                    sp.wait_ge(lo_ready, h - 1)
                load_query(h)
                if h == 0:
                    sp.wait_ge(norm_applied, NORM2 + 1)
                    sp.dma_start(keys[:, :, :], keysT).then_inc(keys_loaded, 16)
            for c in range(ADV + 1):
                load_u(c, buffer_of(c + PHEADS))
            sp.wait_ge(gmat_done, T // GROUP)
            load_u(ADV + 1, 1)
            wait_stored(sp, 0)
            wait_stored(sp, 1, (0,))
            for c in range(2):
                load_v(c)
                load_gate(c, c % 2)
            wait_stored(sp, 1)
            with sp.Fori(1, (CHUNKS - ADV) // 2) as i:
                for b in range(2):
                    load_u(2 * i + b + ADV, b)
                    load_v(2 * i + b)
                    load_gate(2 * i + b, b)
            with sp.Fori((CHUNKS - ADV) // 2, CHUNKS // 2) as i:
                for b in range(2):
                    load_v(2 * i + b)
                    load_gate(2 * i + b, b)

            for k in range(KD):
                sp.wait_ge(y_ready, k + 1)
                sp.dma_start(yT[:, k, :], acc[:, k, :]).then_inc(y_stored, 16)
            sp.wait_ge(y_stored, 16 * KD)

        @block.tensor
        def _(pe):
            def sum_squares(n, count, pair, meta, only=None):
                for k in range(count) if only is None else (only,):
                    q = SQ_FROM[n] + k
                    pe.wait_ge(sq_ready, q + 1)
                    src = sq[:, q % 2, :] if n != NORMF else fin_sq[:, q % 2, :]
                    for cols, to in spans(meta):
                        last = nc.tensor.matmul(bank[pair][:, to], ones, src[:, cols], start=(k == 0), stop=(k == count - 1))
                    if k == count - 1:
                        last.then_inc(sum_ready, 1)
                    else:
                        last.then_inc(sq_summed, 1)

            def parts_product(to, n, x_parts, part, order, waits=None):
                first = True
                for ws, xs in ((w_hi_t, x_parts[0]), (w_lo_t, x_parts[0]), (w_hi_t, x_parts[1])):
                    for k in order:
                        if waits is not None:
                            pe.wait_ge(waits[1] if xs is x_parts[1] else waits[0], order.index(k) + 1)
                        last = nc.tensor.matmul(to, ws[:, n % 2, k, :], xs[:, k, part], start=first,
                                                stop=(ws is w_hi_t and xs is x_parts[1] and k == order[-1]))
                        first = False
                return last

            def in_product(n):
                pe.wait_ge(wt_lo, n + 1)
                if n >= 2:
                    wait_taken(pe, n - 2)
                for cols, to in spans(n >= 2 and (n < 5 or (n - 5) % 3 < 2)):
                    last = parts_product(bank[n % 2][:, to], n, (h_hi, h_lo), cols, range(KD), (h_hi_ready, h_lo_ready) if n == 0 else None)
                last.then_inc(tile_done, 1)

            in_product(0)
            pe.wait_ge(const_loaded, 16)
            sum_squares(NORM1, KD, 2, True)
            for n in range(1, 8):
                in_product(n)
            sum_squares(NORMQ, 2, 3, False)
            pe.wait_ge(root_ready, NORM1 + 1)
            sum_squares(NORMKV, 1, 2, True)
            for n in range(8, N_IN):
                in_product(n)

            pe.wait_ge(wuq_loaded, 16)
            pe.wait_ge(wukv_loaded, 16)
            pe.wait_ge(norm_applied, NORMKV + 1)
            for m in range(N_QKV):
                n = N_IN + m
                wait_taken(pe, n - 2)
                to = bank[n % 2]
                if m < 8:
                    for k in range(2):
                        last = nc.tensor.matmul(to[:, 0:T], wuq_t[:, m, k, :], c_q[:, k, :], start=(k == 0), stop=(k == 1))
                elif m < 12:
                    w = wukv_t[:, (m - 8) * 128:(m - 7) * 128]
                    for cols, where in spans(True):
                        last = nc.tensor.matmul(to[:, where], w, c_kv[:, cols], start=True, stop=True)
                elif m < 16:
                    last = nc.tensor.matmul(to[:, 0:T], c_kv[:, (m - 12) * 128:(m - 11) * 128], wukv_t[:, DC:2 * DC],
                                            start=True, stop=True)
                else:
                    last = nc.tensor.matmul(to[0:META, 0:T], c_kv[:, T:L], wukv_t[:, DC:2 * DC], start=True, stop=True)
                last.then_inc(tile_done, 1)

            sum_squares(NORMC, 4, 2, False)

            pe.wait_ge(copied, N_QKV)
            pe.wait_ge(krope_ready, 1)
            pe.wait_ge(qrope_ready, 1)

            def scores(n):
                h, i = n // QT, n % QT
                if n >= QT:
                    pe.wait_ge(probs_ready, n - QT + 1)
                if i == QT - 1 and n > QT:
                    pe.wait_ge(pt_copied, n - QT + 1)
                if n == 3:
                    pe.wait_ge(root_ready, NORMC + 1)
                keys_n = 128 * (i + 1)
                s = score_banks(i)
                a, r = 64 * (h % 2), 32 * (h % 4)
                qa = qn[a:a + 64, h // 2, 128 * i:128 * i + 128]
                qb = qr[r:r + 32, h // 4, 128 * i:128 * i + 128]
                nc.tensor.matmul(s[:, 0:keys_n], qa, kn[a:a + 64, h // 2, 0:keys_n], start=True, stop=False)
                nc.tensor.matmul(s[:, 0:keys_n], qb, kr[r:r + 32, 0:keys_n], start=False, stop=True)
                to = s[:, keys_n:keys_n + META]
                nc.tensor.matmul(to, qa, kn[a:a + 64, h // 2, T:L], start=True, stop=False)
                nc.tensor.matmul(to, qb, kr[r:r + 32, T:L], start=False, stop=True).then_inc(scores_ready, 1)

            def transpose_probs(n):
                i = n % QT
                pe.wait_ge(probs_scaled, n + 1)
                if n >= 2:
                    pe.wait_ge(pt_copied, n - 1)
                for j in range(i + 1):
                    nc.tensor.transpose(turn_bank(n)[:, 128 * j:128 * j + 128], probs[:, n % 4, 128 * j:128 * j + 128], ident)
                nc.tensor.transpose(meta_block(n), probs[:, n % 4, 128 * (i + 1):128 * (i + 1) + META],
                                    ident).then_inc(pt_ready, 1)

            def attend(h):
                pe.wait_ge(pt_copied, QT * (h + 1))
                if h >= 2 and h % 2 == 0:
                    pe.wait_ge(pv_copied, h // 2)
                to = value_bank[64 * (h % 2):64 * (h % 2) + 64, :]
                nc.tensor.matmul(to[:, 0:T], v_meta[:, VDIM * h:VDIM * h + VDIM], ptm[:, h % 2, :], start=True, stop=False)
                for j in range(QT):
                    last = nc.tensor.matmul(to[:, 128 * j:T], v_att[:, j, VDIM * h:VDIM * h + VDIM],
                                            ptr[:, h % 2, j, 128 * j:T], start=False, stop=(j == QT - 1))
                last.then_inc(pv_ready, 1)

            for n in range(3):
                scores(n)
            for n in range(N_ATT):
                if n + 3 < N_ATT:
                    scores(n + 3)
                transpose_probs(n)
                if n % QT == 1 and n > QT:
                    attend(n // QT - 1)
            attend(HEADS - 1)
            pe.wait_ge(pt_copied, N_ATT)
            sum_squares(NORMA, 4, 3, False)

            for m in range(N_OUT):
                n = N_IN + m
                pe.wait_ge(wt_lo, n + 1)
                if m >= 2:
                    pe.wait_ge(resid_ready, m - 1)
                parts_product(bank[m % 2][:, 0:T], n, (m_hi, m_lo), slice(0, T), (4, 5, 6, 7, 0, 1, 2, 3),
                              (blk_hi, blk_lo) if m == 0 else None).then_inc(tile_done, 1)
                if m >= 2:
                    sum_squares(NORM2, KD, 2, False, m - 2)
            sum_squares(NORM2, KD, 2, False, N_OUT - 2)
            sum_squares(NORM2, KD, 2, False, N_OUT - 1)

            def product(b, to, piece=range(6 * KD)):
                parts = ((s_hi, x_hi), (s_hi, x_lo), (s_lo, x_hi))
                for n in piece:
                    t, (ws, xs), k = n // (3 * KD), parts[n // KD % 3], n % KD
                    last = nc.tensor.matmul(to[:, 512 * t:512 * t + 512], ws[b][:, t, k, :], xs[:, k, :],
                                            start=(n % (3 * KD) == 0), stop=(n % (3 * KD) == 3 * KD - 1))
                if n == 6 * KD - 1:
                    last.then_inc(prod_done, 1)

            pe.wait_ge(resid_ready, N_OUT)

            def first_product():
                def part(ws, xs, k, start=False, stop=False):
                    for t in range(2):
                        last = nc.tensor.matmul(bank[0][:, 512 * t:512 * t + 512], ws[0][:, t, k, :], xs[:, k, :],
                                                start=start, stop=stop)
                    return last

                pe.wait_ge(hi_ready, 1)
                for k in range(KD):
                    pe.wait_ge(xhi_ready, k + 1)
                    part(s_hi, x_hi, k, start=(k == 0))
                pe.wait_ge(lo_ready, 1)
                for k in range(KD):
                    part(s_lo, x_hi, k)
                pe.wait_ge(xlo_ready, KD - len(POOL_BLOCKS))
                pe.wait_ge(xlo_pool_ready, len(POOL_BLOCKS))
                for k in range(KD):
                    last = part(s_hi, x_lo, k, stop=(k == KD - 1))
                last.then_inc(prod_done, 1)

            def two_heads(g):
                for b in range(2):
                    if isinstance(g, int) and b == 0:
                        first_product()
                        pe.wait_ge(keys_loaded, 16)
                        continue
                    pe.wait_ge(lo_ready, 2 * g + b + 1)
                    if not isinstance(g, int):
                        pe.wait_ge(prod_taken, 2 * g)
                    product(b, bank[b])
                for b in range(2):
                    pe.wait_ge(prod_taken, 2 * g + b + 1)
                    if not isinstance(g, int):
                        pe.wait_ge(keyscore_copied, 2 * g)
                    for t in range(QT):
                        for side in range(2):
                            last = nc.tensor.matmul(bank[2 + b][:, (2 * t + side) * NK:(2 * t + side + 1) * NK],
                                                    qk[:, b, side, 128 * t:128 * t + 128], keys[:, side, :],
                                                    start=True, stop=True)
                    last.then_inc(keyscore_done, 1)

            two_heads(0)
            with pe.Fori(1, PHEADS // 2) as g:
                two_heads(g)

            def u_product(c, b):
                pe.wait_ge(lo_ready, c + PHEADS + 1)
                pe.wait_ge(prod_taken, c + PHEADS - 1)
                product(b, bank[b])

            with pe.Fori(0, EARLY // 2) as i:
                for b in range(2):
                    u_product(2 * i + b, b)

            pe.wait_ge(choice_ready, 1)
            pe.wait_ge(keyscore_copied, PHEADS)
            for a in range(3):
                for t in range(QT):
                    src = expert[:, a, t] if a < 2 else best[:, t]
                    last = nc.tensor.transpose(pick_bank(a)[:, 128 * t:128 * t + 128], src.rearrange("p h s -> p (h s)"), ident)
                last.then_inc(pick_done, 1)

            pe.wait_ge(pick_copied, 4)
            PIECES = 5

            def gate_matrices(i, solo=None):
                for g in range(GROUPS):
                    pe.wait_ge(onehot_hi_ready, GROUPS * i + g + 1)
                    if g % 4 < 3:
                        pe.wait_ge(onehot_lo_ready, 3 * GROUPS // 4 * i + g - g // 4 + 1)
                    if not isinstance(i, int) or i or g > 1:
                        pe.wait_ge(gmat_staged, GROUPS * i + g - 1)
                    for t in range(GROUP):
                        to = bank[2 + g % 2][:, t * NK:(t + 1) * NK]
                        row = onehot[:, g % SLOTS, 0, :, t]
                        nc.tensor.matmul(to, row, onehot[:, g % SLOTS, 2, :, t], start=True, stop=False)
                        last = nc.tensor.matmul(to, row, onehot[:, g % SLOTS, 1, :, t], start=False, stop=True)
                    last.then_inc(gmat_done, 1)
                    p = g - GROUPS + PIECES
                    if solo is not None and p >= 0:
                        if p == 0:
                            pe.wait_ge(lo_ready, SOLO_FROM + i + 1)
                            pe.wait_ge(prod_taken, SOLO_FROM + i - 1)
                        product(0, bank[solo], range(6 * KD * p // PIECES, 6 * KD * (p + 1) // PIECES))

            for s in range(2):
                gate_matrices(s, s)
            with pe.Fori(1, SOLO // 2) as i:
                for s in range(2):
                    gate_matrices(2 * i + s, s)
            with pe.Fori(SOLO, T // HALF) as i:
                gate_matrices(i)

            def out_product(c, b):
                pe.wait_ge(vlo_ready, c + 1)
                pe.wait_ge(wlo_ready, c + 1)
                for m in range(KD):
                    pe.wait_ge(out_free, KD * c + m + 1)
                    to = bank[2 + m % 4 // 2][:, 512 * (m % 2):512 * (m % 2) + 512]
                    n = 0
                    for t in range(2):
                        for vs, ws in ((v_hi, w_hi), (v_hi, w_lo), (v_lo, w_hi)):
                            last = nc.tensor.matmul(to, vs[:, b, t, 128 * m:128 * m + 128], ws[:, b, t, :],
                                                    start=(n == 0), stop=(n == 5))
                            n += 1
                    last.then_inc(out_done, 1)

            with pe.Fori(0, (CHUNKS - ADV) // 2) as i:
                for b in range(2):
                    u_product(2 * i + b + ADV, b)
                    out_product(2 * i + b, b)
            with pe.Fori((CHUNKS - ADV) // 2, CHUNKS // 2) as i:
                for b in range(2):
                    out_product(2 * i + b, b)

            pe.wait_ge(prod_taken, CHUNKS + PHEADS)
            sum_squares(NORMF, KD, 0, False)

        @block.scalar
        def _(sc):
            def square(n, k, src):
                q = SQ_FROM[n] + k
                if q >= 2:
                    ends = sum(SQ_FROM[m + 1] <= q - 2 + 1 for m in range(6))
                    if ends:
                        sc.wait_ge(sum_ready, ends)
                    sc.wait_ge(sq_summed, q - 1 - ends)
                to = (sq if n != NORMF else fin_sq)[:, q % 2, 0:src.shape[-1]]
                nc.scalar.activation(to, src, ACT.Square).then_inc(sq_ready, 1)

            def root(n, pair, width, count):
                sc.wait_ge(sum_ready, n + 1)
                if n >= 2:
                    sc.wait_ge(norm_applied, n - 1)
                to = r_in[:, 0, :] if n == NORM1 else fin_r[:, :] if n == NORMF else rstd[:, n % 2, 0:width]
                src = bank[pair][:, 0:width]
                if width == L:
                    to, src = halves(to), across(bank[pair])
                nc.scalar.activation(to, src, ACT.Sqrt, bias=eps[:, :],
                                     scale=1.0 / count).then_inc(root_ready, 1)


            def tile_hi(n):
                sc.wait_ge(w_loaded[n % WRING], 16 * (n // WRING + 1))
                if n >= 2:
                    sc.wait_ge(tile_done, n - 1 + (N_QKV if n - 2 >= N_IN else 0))
                nc.scalar.activation(w_hi_t[:, n % 2], wring[:, n % WRING], ACT.Copy).then_inc(wt_hi, 1)

            def block_hi(k, to):
                sc.wait_ge(blk_ready, k + 1)
                nc.scalar.activation(to, xn_f[:, k % 2, 0:to.shape[-1]], ACT.Copy).then_inc(blk_hi, 1)

            sc.wait_ge(vec_loaded, 16)
            sc.wait_ge(meta_loaded, 16)
            for k in range(KD):
                sc.wait_ge(x_loaded[k // 2], 16)
                nc.scalar.activation(h_hi[:, k, :], hT[:, k, :], ACT.Copy, scale=vec[:, G1 + k:G1 + k + 1]).then_inc(h_hi_ready, 1)
                if k == 1:
                    tile_hi(0)
            for k in range(KD):
                square(NORM1, k, hT[:, k, :])
                if k == 1:
                    tile_hi(1)
            sc.wait_ge(eps_set, 1)
            root(NORM1, 2, L, D)

            def take(n, to, src, scale=1.0):
                sc.wait_ge(tile_done, n + 1)
                nc.scalar.activation(to, src, ACT.Copy, scale=scale).then_inc(copied, 1)

            for n in range(2, N_IN + 2):
                tile_hi(n)
                if n == 6:
                    sc.wait_ge(in_taken, 3)
                    for k in range(2):
                        square(NORMQ, k, c_q[:, k, :])
                if n == 8:
                    square(NORMKV, 0, c_kv[:, :])
                if n == 9:
                    root(NORMQ, 3, T, QL)
                    root(NORMKV, 2, L, KVL)
            for m in range(N_QKV):
                n = N_IN + m
                src = bank[n % 2]
                if m < 4:
                    take(n, qn[:, m, :], src[:, 0:T], -SCALE)
                elif m < 8:
                    take(n, qr_in[:, m - 4, :], src[:, 0:T], -SCALE)
                elif m < 12:
                    take(n, halves(kn[:, m - 8, :]), across(src))
                elif m < 16:
                    take(n, v_att[:, m - 12, :], src[:, 0:T])
                else:
                    take(n, v_meta[:, :], src[0:META, 0:T])

            for k in range(4):
                sc.wait_ge(conv_ready, k + 1)
                square(NORMC, k, conv[:, k, :])
            root(NORMC, 2, T, DC)

            sc.wait_ge(tile_done, N_PROJ)
            sc.wait_ge(qrope_ready, 1)
            sc.wait_ge(krope_ready, 1)

            def copy_transposed(n):
                h, i = n // QT, n % QT
                sc.wait_ge(pt_ready, n + 1)
                if h >= 2:
                    sc.wait_ge(pv_ready, h - 1)
                nc.scalar.activation(ptr[:, h % 2, 0:i + 1, 128 * i:128 * i + 128],
                                     turn_bank(n)[:, 0:128 * (i + 1)].rearrange("p (j q) -> p j q", q=128), ACT.Copy)
                nc.scalar.activation(ptm[:, h % 2, 128 * i:128 * i + 128], meta_block(n), ACT.Copy).then_inc(pt_copied, 1)

            def exponentiate(n):
                i = n % QT
                width = 128 * (i + 1) + META
                sc.wait_ge(bias_ready, n + 1)
                if n >= 4:
                    sc.wait_ge(pt_ready, n - 3)
                nc.scalar.activation(probs[:, n % 4, 0:width], score_banks(i)[:, 0:width], ACT.Exp,
                                     bias=negmax[:, n:n + 1], scale=-1.0,
                                     accum_out=rowsum[:, 0, n:n + 1]).then_inc(probs_ready, 1)

            exponentiate(0)
            for n in range(N_ATT):
                if n + 1 < N_ATT:
                    exponentiate(n + 1)
                if n in MIX_STEPS:
                    k = MIX_STEPS.index(n)
                    block_hi(k, m_hi[:, 4 + k, :])
                copy_transposed(n)

            for k in range(4):
                sc.wait_ge(pv_copied, k + 1)
                square(NORMA, k, att[:, k, :])
            root(NORMA, 3, T, DC)
            for k in range(4):
                block_hi(4 + k, m_hi[:, k, :])
            for k in range(KD):
                if k < N_OUT - 2:
                    tile_hi(N_IN + k + 2)
                sc.wait_ge(resid_ready, k + 1)
                square(NORM2, k, acc[:, k, :])
            root(NORM2, 2, T, D)

            def split_hi(c, b, solo=False):
                n = c + PHEADS
                sc.wait_ge(raw_loaded[b], loads_until(n, b, solo))
                if not (isinstance(n, int) and n < 2):
                    sc.wait_ge(prod_done, before(n, solo) + 1)
                nc.scalar.activation(s_hi[b][:, :, :, :], raw[b][:, :, :, :], ACT.Copy).then_inc(hi_ready, 1)

            sc.wait_ge(tile_done, N_PROJ + N_OUT)
            split_hi(-PHEADS, 0)
            for k in range(KD):
                sc.wait_ge(xf_ready, k + 1)
                nc.scalar.activation(x_hi[:, k, :], xtmp[:, k, :], ACT.Copy).then_inc(xhi_ready, 1)
            for h in range(PHEADS):
                split_hi(h + 1 - PHEADS, (h + 1) % 2)
                sc.wait_ge(prod_done, h + 1)
                if h >= 2:
                    sc.wait_ge(keyscore_done, h - 1)
                nc.scalar.activation(qk[:, h % 2], bank[h % 2][:, :].rearrange("p (s t) -> p s t", s=2),
                                     ACT.Copy).then_inc(prod_taken, 1)
                sc.wait_ge(keyscore_done, h + 1)
                if h >= 4:
                    sc.wait_ge(keyscore_taken, h - 3)
                nc.scalar.activation(score[:, h % 4], bank[2 + h % 2][:, :].rearrange("p (t s n) -> p t s n", t=QT, s=2),
                                     ACT.Copy).then_inc(keyscore_copied, 1)

            def gelu(c, b, slot):
                wait_apart(sc, "act", prod_done, c + PHEADS + 1)
                nc.scalar.activation(act[:, slot].rearrange("p s t n -> p (s t n)"), bank[b][:, :],
                                     ACT.Gelu_apprx_tanh).then_inc(prod_taken, 1)

            for c in range(EARLY):
                split_hi(c + 1, (c + 1) % 2)
                gelu(c, c % 2, slice(c, c + 1))

            sc.wait_ge(shifted, 1)
            nc.scalar.activation(best[:, :, :, :], best[:, :, :, :], ACT.Exp).then_inc(exps_ready, 1)
            for a in range(2):
                sc.wait_ge(pick_done, a + 1)
                nc.scalar.activation(pick[:, a, :], pick_bank(a), ACT.Copy).then_inc(pick_copied, 1)
            sc.wait_ge(pick_done, 3)
            nc.scalar.activation(pgate[:, :], pick_bank(2), ACT.Copy, scale=GSCALE).then_inc(pick_copied, 1)
            nc.scalar.activation(pick[:, 2, :], pick_bank(2), ACT.Copy, scale=GSCALE).then_inc(pick_copied, 1)

            def stage_half(q, s):
                if not isinstance(q, int) or q:
                    for p in range(2):
                        sc.wait_ge(stage_stored[p][s], 16 * q)
                with sc.Fori(0, GROUPS // 2) as i:
                    for r in range(2):
                        wait_apart(sc, "act", gmat_done, (2 * q + s) * GROUPS + 2 * i + r + 1)
                        nc.scalar.activation(
                            stage[:, s, :, bass.ds(GROUP * (2 * i + r), GROUP)].rearrange("p j t -> p t j"),
                            bank[2 + r][:, :].rearrange("p (t j) -> p t j", t=GROUP), ACT.Copy,
                            scale=1.0 / GSCALE).then_inc(gmat_staged, 1)
                sc.wait_ge(gmat_staged, (2 * q + s + 1) * GROUPS)
                for p in range(2):
                    js = slice(p * NK // 2, (p + 1) * NK // 2)
                    sc.dma_start(gates_dram[bass.ds(2 * q + s, 1), :, js].rearrange("q i j t -> (q i) j t"),
                                 stage[:, s, js]).then_inc(stage_stored[p][s], 16)

            def solo(c, b, slot):
                split_hi(c + 1, 0, solo=True)
                gelu(c, b, slot)

            for q in range(2):
                stage_half(0, q)
                solo(EARLY + q, q, slice(EARLY + q, EARLY + q + 1))
            with sc.Fori(1, SOLO // 2) as q:
                for s in range(2):
                    stage_half(q, s)
                    solo(EARLY + 2 * q + s, s, bass.ds(EARLY + 2 * q + s, 1))
            with sc.Fori(SOLO // 2, T // HALF // 2) as q:
                for s in range(2):
                    stage_half(q, s)

            def out_hi(c, b, slot):
                sc.wait_ge(v_loaded, 16 * c + 16)
                if not (isinstance(c, int) and c < 2):
                    sc.wait_ge(out_done, KD * (c - 1))
                nc.scalar.activation(v_hi[:, b], v_raw[:, :, :], ACT.Copy).then_inc(vhi_ready, 1)
                if isinstance(c, int) and c == 0:
                    wait_stored(sc, 1)
                wait_apart(sc, "act", w_ready, c + 1)
                nc.scalar.activation(w_hi[:, b].rearrange("p t n -> p (t n)"), act[:, slot].rearrange("p s t n -> p (s t n)"),
                                     ACT.Copy).then_inc(whi_ready, 1)

            out_hi(0, 0, slice(0, 1))

            def step(c, b, slot, next_slot, last=False):
                out_hi(c + 1, 1 - b, next_slot)
                if not last:
                    split_hi(c + ADV + 1, 1 - b)
                sc.wait_ge(wlo_ready, c + 1)
                gelu(c + ADV, b, slot)

            for c in range(2):
                step(c, c, slice(c, c + 1), slice(c + 1, c + 2))
            with sc.Fori(1, (CHUNKS - ADV) // 2 - 1) as i:
                for b in range(2):
                    c = 2 * i + b
                    step(c, b, bass.ds(c % ADV, 1), bass.ds((c + 1) % ADV, 1))
            for c in range(CHUNKS - ADV - 2, CHUNKS - ADV):
                step(c, c % 2, slice(c % ADV, c % ADV + 1), slice((c + 1) % ADV, (c + 1) % ADV + 1), last=c == CHUNKS - ADV - 1)
            for c in range(CHUNKS - ADV + 1, CHUNKS):
                out_hi(c, c % 2, slice(c % ADV, c % ADV + 1))

            sc.wait_ge(out_done, KD * CHUNKS)
            for k in range(KD):
                sc.wait_ge(out_free, 4 + KD * (CHUNKS - 1) + k + 1)
                square(NORMF, k, acc[:, k, :])
            root(NORMF, 0, T, D)

        @block.gpsimd
        def _(pool):
            def tile_lo(n):
                pool.wait_ge(wt_hi, n + 1)
                nc.gpsimd.tensor_tensor(w_lo_t[:, n % 2].rearrange("p k e -> p (k e)"),
                                        wring[:, n % WRING].rearrange("p k e -> p (k e)"),
                                        w_hi_t[:, n % 2].rearrange("p k e -> p (k e)").bitcast(f32), ALU.subtract).then_inc(wt_lo, 1)

            def block_lo(k, to, hi):
                pool.wait_ge(blk_hi, k + 1)
                nc.gpsimd.tensor_tensor(to, xn_f[:, k % 2, 0:to.shape[-1]], hi.bitcast(f32), ALU.subtract).then_inc(blk_lo, 1)

            tile_lo(0)
            tile_lo(1)
            for n in range(2, 7):
                tile_lo(n)
            pool.wait_ge(rope_loaded, 16)
            pool.wait_ge(in_taken, 5)
            nc.gpsimd.tensor_tensor(kr[:, :], kr_in[:, 0, :], rope_t[:, 0, :], ALU.mult)
            nc.gpsimd.tensor_tensor(kr_in[:, 1, :], kr_in[:, 1, :], rope_t[:, 1, :], ALU.mult).then_inc(pool_step, 1)
            pool.wait_ge(pool_step, 1)
            nc.gpsimd.tensor_tensor(kr[:, :], kr[:, :], kr_in[:, 1, :], ALU.add).then_inc(krope_ready, 1)
            for n in range(7, N_IN + 2):
                tile_lo(n)
            for k in range(4):
                block_lo(k, m_lo[:, 4 + k, :], m_hi[:, 4 + k, :])
            for k in range(4):
                block_lo(4 + k, m_lo[:, k, :], m_hi[:, k, :])
            for n in range(N_IN + 2, N_IN + N_OUT):
                tile_lo(n)

            def lookup(h):
                pool.wait_ge(hit_ready, h + 1)
                for s in range(2):
                    last = nc.gpsimd.tensor_tensor(hit[:, h % 2, s], hit[:, h % 2, s],
                                                   topi_f[:, h % 2, s].unsqueeze(2).broadcast_to([128, QT, TOPK, TOPK]), ALU.mult)
                last.then_inc(hit_weighed, 1)

            def split_lo(c, b):
                n = c + PHEADS
                pool.wait_ge(hi_ready, n + 1)
                nc.gpsimd.tensor_tensor(s_lo[b][:, :, :, :].rearrange("p t k e -> p (t k e)"),
                                        raw[b][:, :, :, :].rearrange("p t k e -> p (t k e)"),
                                        s_hi[b][:, :, :, :].rearrange("p t k e -> p (t k e)").bitcast(f32),
                                        ALU.subtract).then_inc(lo_ready, 1)

            for n in range(SOLO_FROM + 1):
                split_lo(n - PHEADS, n % 2)
                for k in POOL_BLOCKS if n == 0 else ():
                    pool.wait_ge(xhi_ready, k + 1)
                    nc.gpsimd.tensor_tensor(x_lo[:, k, :], xtmp[:, k, :], x_hi[:, k, :].bitcast(f32),
                                            ALU.subtract).then_inc(xlo_pool_ready, 1)
                if n in LOOKUP_AFTER:
                    lookup(LOOKUP_AFTER.index(n))

            pool.wait_ge(plo_ready, 1)

            def low_columns(i, solo=True):
                for g in range(GROUPS):
                    if g == 3 and solo:
                        split_lo(EARLY + i, 0)
                    if g % 4 < 3:
                        pool.wait_ge(onehot_hi_ready, GROUPS * i + g + 1)
                        lo = pick[:, 3, bass.ds(HALF * i + GROUP * g, GROUP)]
                        nc.gpsimd.tensor_tensor(onehot[:, g % SLOTS, 1], onehot[:, g % SLOTS, 1],
                                                lo.unsqueeze(1).broadcast_to([128, NK, GROUP]), ALU.mult).then_inc(onehot_lo_ready, 1)

            low_columns(0, solo=False)
            with pool.Fori(1, SOLO + 1) as i:
                low_columns(i)
            with pool.Fori(SOLO + 1, T // HALF) as i:
                low_columns(i, solo=False)

            def weigh(c, b, slot):
                pool.wait_ge(gate_loaded[b], 16 * (c // 2) + 16 if isinstance(c, int) else 8 * (c - b) + 16)
                pool.wait_ge(prod_taken, c + PHEADS + 1)
                w = act[:, slot].rearrange("p s t (q n) -> p (s t) q n", n=HALF)
                nc.gpsimd.tensor_tensor(w, w, gate[:, b].rearrange("p q t n -> p t q n"), ALU.mult).then_inc(w_ready, 1)

            weigh(0, 0, slice(0, 1))
            with pool.Fori(0, (CHUNKS - ADV) // 2 - 1) as i:
                for b in range(2):
                    c = 2 * i + b
                    weigh(c + 1, 1 - b, bass.ds((c + 1) % ADV, 1))
                    split_lo(c + ADV + 1, 1 - b)
            for c in range(CHUNKS - ADV - 2, CHUNKS - 1):
                weigh(c + 1, (c + 1) % 2, slice((c + 1) % ADV, (c + 1) % ADV + 1))
                if c < CHUNKS - ADV - 1:
                    split_lo(c + ADV + 1, (c + 1) % 2)

        @block.vector
        def _(dve):
            steps = [0]

            def chain(ins):
                steps[0] += 1
                ins.then_inc(dve_step, 1)
                dve.wait_ge(dve_step, steps[0])

            def invert(n, width):
                dve.wait_ge(root_ready, n + 1)
                r = r_in[:, 0, :] if n == NORM1 else fin_r[:, :] if n == NORMF else rstd[:, n % 2, 0:width]
                nc.vector.reciprocal(r, r).then_inc(rstd_ready, 1)
                dve.wait_ge(rstd_ready, n + 1)
                return r

            def apply(to, src, gain, r):
                return nc.vector.scalar_tensor_tensor(to, src, vec[:, gain:gain + 1], r, ALU.mult, ALU.mult)

            nc.vector.memset(eps[:, :], EPS).then_inc(eps_set, 1)
            dve.wait_ge(vec_loaded, 16)
            for k in range(KD):
                dve.wait_ge(h_hi_ready, k + 1)
                nc.vector.scalar_tensor_tensor(h_lo[:, k, :], hT[:, k, :], vec[:, G1 + k:G1 + k + 1], h_hi[:, k, :].bitcast(f32),
                                               ALU.mult, ALU.subtract).then_inc(h_lo_ready, 1)
            r = invert(NORM1, L)
            chain(nc.vector.tensor_tensor(r_in[:, 1, :], r, r, ALU.mult))
            dve.sem_inc(norm_applied, 1)

            def take(n, to, width, square=0):
                dve.wait_ge(tile_done, n + 1)
                if width == L:
                    to, src, by = halves(to), across(bank[n % 2]), halves(r_in[:, square, :])
                else:
                    src, by = bank[n % 2][:, 0:T], r_in[:, square, 0:T]
                nc.vector.tensor_tensor(to, src, by, ALU.mult).then_inc(in_taken, 1)

            def conv_input(j):
                n = 6 + 3 * j
                dve.wait_ge(tile_done, n + 1)
                dve.wait_ge(in_taken, n)
                nc.vector.tensor_tensor(halves(zpad[:, j, 2:]), across(bank[n % 2]), halves(cgate[:, :]), ALU.mult)
                nc.vector.tensor_tensor(zpad[:, j, 0:2], across(bank[n % 2])[:, 1, L // 2 - 2:], cgate[:, L - 2:L],
                                        ALU.mult).then_inc(in_taken, 1)

            take(0, c_q[:, 0, :], T)
            take(1, c_q[:, 1, :], T)
            take(2, c_kv[:, :], L)
            take(3, kr_in[:, 0, :], L)
            take(4, kr_in[:, 1, :], L)
            for j in range(4):
                take(5 + 3 * j, cgate[:, :], L, square=1)
                if j == 1:
                    r = invert(NORMKV, L)
                    apply(c_kv[:, :], c_kv[:, :], GKV, r).then_inc(norm_applied, 1)
                conv_input(j)
                take(7 + 3 * j, bgate[:, j, :], T)
                if j == 0:
                    r = invert(NORMQ, T)
                    for k in range(2):
                        last = apply(c_q[:, k, :], c_q[:, k, :], GQ + k, r)
                    last.then_inc(norm_applied, 1)

            dve.wait_ge(in_taken, N_IN)
            for j in range(4):
                last = nc.vector.tensor_scalar(conv[:, j, :], zpad[:, j, 0:T], vec[:, CW + j:CW + j + 1],
                                               vec[:, CB + j:CB + j + 1], ALU.mult, ALU.add)
            chain(last)
            for tap in (1, 2):
                for j in range(4):
                    w = CW + 4 * tap + j
                    last = nc.vector.scalar_tensor_tensor(conv[:, j, :], zpad[:, j, tap:T + tap], vec[:, w:w + 1],
                                                          conv[:, j, :], ALU.mult, ALU.add)
                chain(last)
            for j in range(4):
                nc.vector.tensor_tensor(conv[:, j, :], conv[:, j, :], bgate[:, j, 0:T], ALU.mult).then_inc(conv_ready, 1)

            dve.wait_ge(rope_loaded, 16)
            dve.wait_ge(copied, 8)
            for m in range(2):
                nc.vector.tensor_tensor(qr[:, m, :], qr_in[:, m, :], rope_t[:, 0, 0:T], ALU.mult)
            for m in range(2):
                last = nc.vector.tensor_tensor(qr_in[:, 2 + m, :], qr_in[:, 2 + m, :], rope_t[:, 1, 0:T], ALU.mult)
            chain(last)
            for m in range(2):
                last = nc.vector.tensor_tensor(qr[:, m, :], qr[:, m, :], qr_in[:, 2 + m, :], ALU.add)
            last.then_inc(qrope_ready, 1)

            dve.wait_ge(causal_loaded, 16)

            def maximum(n):
                i = n % QT
                width = 128 * (i + 1) + META
                s = score_banks(i)[:, 0:width]
                dve.wait_ge(scores_ready, n + 1)
                nc.vector.tensor_tensor_reduce(out=s, in0=s, in1=causal[:, T - 128 * (i + 1):L], scale=1.0, scalar=-NEG,
                                               op0=ALU.add, op1=ALU.min, accum_out=negmax[:, n:n + 1]).then_inc(bias_ready, 1)

            def normalise(n):
                width = 128 * (n % QT + 1) + META
                dve.wait_ge(probs_ready, n + 1)
                chain(nc.vector.reciprocal(rowsum[:, 1, n:n + 1], rowsum[:, 0, n:n + 1]))
                nc.vector.tensor_scalar(probs[:, n % 4, 0:width], probs[:, n % 4, 0:width], rowsum[:, 1, n:n + 1],
                                        None, ALU.mult).then_inc(probs_scaled, 1)

            def take_pair(p):
                dve.wait_ge(pv_ready, 2 * p + 2)
                nc.vector.tensor_copy(att[:, p, :], value_bank).then_inc(pv_copied, 1)

            def mix(n, src, gain, b, k):
                if k == 0:
                    invert(n, T)
                if b >= 2:
                    dve.wait_ge(blk_lo, b - 1)
                apply(xn_f[:, b % 2, 0:T], src[:, k, :], gain + k, rstd[:, n % 2, 0:T]).then_inc(blk_ready, 1)
                if k == 3:
                    dve.wait_ge(blk_ready, b + 1)
                    dve.sem_inc(norm_applied, 1)

            maximum(0)
            maximum(1)
            for n in range(N_ATT):
                if n + 2 < N_ATT:
                    maximum(n + 2)
                normalise(n)
                if n + 1 in MIX_STEPS:
                    k = MIX_STEPS.index(n + 1)
                    mix(NORMC, conv, GC, k, k)
                if n % (2 * QT) == 2 and n > 2 * QT:
                    take_pair(n // (2 * QT) - 1)
            take_pair(3)
            for k in range(4):
                mix(NORMA, att, GA, 4 + k, k)

            for m in range(N_OUT):
                dve.wait_ge(tile_done, N_PROJ + m + 1)
                nc.vector.tensor_tensor(acc[:, m, :], bank[m % 2][:, 0:T], hT[:, m, 0:T], ALU.add).then_inc(resid_ready, 1)

            r = invert(NORM2, T)
            dve.wait_ge(resid_ready, N_OUT)
            for k in range(KD):
                apply(xtmp[:, k, :], acc[:, k, :], G2 + k, r).then_inc(xf_ready, 1)
            dve.wait_ge(xf_ready, KD)
            dve.sem_inc(norm_applied, 1)
            for k in range(KD):
                if k not in POOL_BLOCKS:
                    dve.wait_ge(xhi_ready, k + 1)
                    nc.vector.tensor_tensor(x_lo[:, k, :], xtmp[:, k, :], x_hi[:, k, :].bitcast(f32),
                                            ALU.subtract).then_inc(xlo_ready, 1)

            first = steps[0]
            tails = 0

            def top16(values, vals, idx, scratch, link):
                n = len(values)
                for i in range(n):
                    last = nc.vector.max(vals[i][:, 0:8], values[i])
                link(last)
                for i in range(n):
                    nc.vector.max_index(idx[i][:, 0:8], vals[i][:, 0:8], values[i])
                    last = nc.vector.match_replace(scratch[i], vals[i][:, 0:8], values[i], NEG)
                link(last)
                for i in range(n):
                    last = nc.vector.max(vals[i][:, 8:16], scratch[i])
                link(last)
                for i in range(n):
                    last = nc.vector.max_index(idx[i][:, 8:16], vals[i][:, 8:16], scratch[i])
                return last

            def reduce_hits(h, b):
                wait_apart(dve, "dve", hit_weighed, h + 1)
                for s in range(2):
                    nc.vector.tensor_reduce(expert[:, s, :, bass.ds(h, 1), :].rearrange("p t h s -> p t (h s)"),
                                            hit[:, b, s], AX.X, ALU.add)

            PER_HEAD = 12
            with dve.Fori(0, PHEADS // 4) as g:
                for q in range(4):
                    h = 4 * g + q
                    done = [0]

                    def link(ins):
                        done[0] += 1
                        ins.then_inc(dve_step, 1)
                        wait_apart(dve, "dve", dve_step, first + PER_HEAD * h + done[0])

                    wait_apart(dve, "dve", keyscore_copied, h + 1)
                    both = [(t, s) for t in range(QT) for s in range(2)]
                    last = top16([score[:, q, t, s, :] for t, s in both], [topv[:, s, t, :] for t, s in both],
                                 [topi[:, s, t, :] for t, s in both], [rest[:, t, s, :] for t, s in both], link)
                    link(last)
                    dve.sem_inc(keyscore_taken, 1)
                    wide = cand[:, :, 0:WIDE * TOPK].rearrange("p t (a b) -> p t a b", a=WIDE)
                    tall = cand[:, :, WIDE * TOPK:NCAND].rearrange("p t (a b) -> p t a b", b=4)
                    nc.vector.tensor_tensor(wide, topv[:, 0, :, 0:WIDE].unsqueeze(3).broadcast_to([128, QT, WIDE, TOPK]),
                                            topv[:, 1].unsqueeze(2).broadcast_to([128, QT, WIDE, TOPK]), ALU.add)
                    nc.vector.tensor_copy(topi_f[:, q % 2], topi[:, :, :, :])
                    link(nc.vector.tensor_tensor(tall, topv[:, 0, :, WIDE:].unsqueeze(3).broadcast_to([128, QT, TOPK - WIDE, 4]),
                                                 topv[:, 1, :, 0:4].unsqueeze(2).broadcast_to([128, QT, TOPK - WIDE, 4]), ALU.add))
                    last = top16([cand[:, t] for t in range(QT)], [bestv[:, t, :] for t in range(QT)],
                                 [flat[:, t, :] for t in range(QT)], [cand2[:, t, :] for t in range(QT)], link)
                    if q:
                        reduce_hits(h - 1, (q - 1) % 2)
                    link(last)
                    nc.vector.tensor_copy(best[:, :, bass.ds(h, 1), :].rearrange("p t h s -> p t (h s)"), bestv[:, :, :])
                    nc.vector.tensor_scalar(digit[:, 0], flat[:, :, :], 2, None, ALU.logical_shift_right)
                    nc.vector.tensor_scalar(digit[:, 1], flat[:, :, :], 4, None, ALU.logical_shift_right)
                    nc.vector.tensor_scalar(digit[:, 2], flat[:, :, :], 12, None, ALU.bitwise_and)
                    link(nc.vector.tensor_scalar(flat[:, :, :], flat[:, :, :], TOPK * WIDE + 3, None, ALU.bitwise_and))
                    nc.vector.scalar_tensor_tensor(pos[:, 0], digit[:, 0], -12.0, digit[:, 1], ALU.add, ALU.max)
                    nc.vector.scalar_tensor_tensor(pos[:, 1], flat[:, :, :], float(TOPK * WIDE), digit[:, 2], ALU.is_lt, ALU.mult)
                    link(nc.vector.tensor_scalar(flat[:, :, :], flat[:, :, :], 3, None, ALU.bitwise_and))
                    link(nc.vector.tensor_tensor(pos[:, 1], pos[:, 1], flat[:, :, :], ALU.add))
                    for s in range(2):
                        last = nc.vector.tensor_tensor(hit[:, q % 2, s], pos[:, s].unsqueeze(3).broadcast_to([128, QT, TOPK, TOPK]),
                                                       iota[:, 0:TOPK].unsqueeze(1).unsqueeze(1).broadcast_to([128, QT, TOPK, TOPK]),
                                                       ALU.is_equal)
                    last.then_inc(hit_ready, 1)
                    if q == 3:
                        reduce_hits(h, 1)
                    assert done[0] == PER_HEAD, done[0]
            steps[0] = first + PER_HEAD * PHEADS

            gates = best[:, :, :, :].rearrange("p t h s -> p (t h) s")
            chain(nc.vector.tensor_copy(bsum[:, :], gates[:, :, 0]))
            nc.vector.tensor_tensor(gates, gates, bsum[:, :].unsqueeze(2).broadcast_to([128, QT * PHEADS, TOPK]),
                                    ALU.subtract).then_inc(shifted, 1)
            dve.wait_ge(exps_ready, 1)
            chain(nc.vector.tensor_reduce(bsum[:, :], gates, AX.X, ALU.add))
            chain(nc.vector.reciprocal(bsum[:, :], bsum[:, :]))
            nc.vector.tensor_tensor(gates, gates, bsum[:, :].unsqueeze(2).broadcast_to([128, QT * PHEADS, TOPK]),
                                    ALU.mult).then_inc(choice_ready, 1)

            for t in range(GROUP):
                last = nc.vector.tensor_copy(iotas[:, :, t], iota)
            chain(last)
            dve.wait_ge(pick_copied, 4)
            nc.vector.tensor_tensor(pick[:, 3, :], pgate[:, :], pick[:, 2, :], ALU.subtract).then_inc(plo_ready, 1)
            first_hot = steps[0]

            def onehots_of(i):
                for g in range(GROUPS):
                    def spread(a):
                        return pick[:, a, bass.ds(HALF * i + GROUP * g, GROUP)].unsqueeze(1).broadcast_to([128, NK, GROUP])

                    if not isinstance(i, int) or g >= SLOTS:
                        wait_apart(dve, "dve", gmat_done, GROUPS * i + g - SLOTS + 1)
                    hot = onehot[:, g % SLOTS]
                    nc.vector.tensor_tensor(hot[:, 1], iotas[:, :, :], spread(1), ALU.is_equal).then_inc(dve_step, 1)
                    nc.vector.tensor_tensor(hot[:, 0], iotas[:, :, :], spread(0), ALU.is_equal)
                    wait_apart(dve, "dve", dve_step, first_hot + GROUPS * i + g + 1)
                    last = nc.vector.tensor_tensor(hot[:, 2], hot[:, 1], spread(2), ALU.mult)
                    if g % 4 == 3:
                        last = nc.vector.tensor_tensor(hot[:, 1], hot[:, 1], spread(3), ALU.mult)
                    last.then_inc(onehot_hi_ready, 1)

            onehots_of(0)
            with dve.Fori(1, T // HALF) as i:
                onehots_of(i)

            def out_lo(c, b, slot):
                dve.wait_ge(vhi_ready, c + 1)
                nc.vector.tensor_tensor(v_lo[:, b], v_raw[:, :, :], v_hi[:, b].bitcast(f32), ALU.subtract).then_inc(vlo_ready, 1)
                dve.wait_ge(whi_ready, c + 1)
                nc.vector.tensor_tensor(w_lo[:, b].rearrange("p t n -> p (t n)"), act[:, slot].rearrange("p s t n -> p (s t n)"),
                                        w_hi[:, b].rearrange("p t n -> p (t n)").bitcast(f32), ALU.subtract).then_inc(wlo_ready, 1)

            def add_out(c):
                for m in range(KD):
                    dve.wait_ge(out_done, KD * c + m + 1)
                    nc.vector.tensor_tensor(acc[:, m, :], acc[:, m, :], bank[2 + m % 4 // 2][:, 512 * (m % 2):512 * (m % 2) + 512],
                                            ALU.add).then_inc(out_free, 1)

            dve.sem_inc(out_free, 4)
            out_lo(0, 0, slice(0, 1))
            with dve.Fori(0, CHUNKS // 2 - 1) as i:
                for b in range(2):
                    c = 2 * i + b
                    out_lo(c + 1, 1 - b, bass.ds((c + 1) % ADV, 1))
                    add_out(c)
            out_lo(CHUNKS - 1, 1, slice((CHUNKS - 1) % ADV, (CHUNKS - 1) % ADV + 1))
            add_out(CHUNKS - 2)
            add_out(CHUNKS - 1)

            r = invert(NORMF, T)
            for k in range(KD):
                apply(acc[:, k, :], acc[:, k, :], GF + k, r).then_inc(y_ready, 1)


def _rope_tables():
    half = ROPE // 2
    inv = (1.0 / (np.float32(10000.0) ** (np.arange(0, ROPE, 2, dtype=np.float32) / np.float32(ROPE)))).astype(np.float32)
    position = np.concatenate([np.arange(META, META + T), np.arange(META)]).astype(np.float32)
    angle = inv[:, None] * position[None, :]
    cos = np.concatenate([np.cos(angle)] * 2)
    sin = np.concatenate([-np.sin(angle), np.sin(angle)])
    return np.tile(np.stack([cos, sin], 1), (128 // ROPE, 1, 1)).astype(np.float32)


def _lay_out(x, meta_tokens, norm1_g, w_in, q_norm_g, w_uq, kv_norm_g, w_ukv, conv_w, conv_b, attn_out_g, conv_out_g,
             w_out, norm2_g, peer_w_query, peer_keys1, peer_keys2, peer_u, peer_v, final_g):
    c = np.ascontiguousarray

    def columns(g):
        return g.reshape(-1, 128).T

    def tiles(w):
        return w.reshape(w.shape[0] // 128, 128, -1, 128).transpose(2, 1, 0, 3)

    wi = w_in[0]
    o2, o3 = QL + KVL, QL + KVL + ROPE
    kr = wi[:, o2:o3]
    swapped = np.concatenate([kr[:, ROPE // 2:], kr[:, :ROPE // 2]], 1)
    parts = [wi[:, :o2]] + [kr] * 4 + [swapped] * 4
    bcu = [wi[:, o3 + n * DC:o3 + (n + 1) * DC] for n in range(3)]
    for j in range(4):
        parts += [bcu[n][:, 128 * j:128 * j + 128] for n in (1, 2, 0)]
    q = w_uq[0].reshape(QL, HEADS, NOPE + ROPE)
    q_rope = q[:, :, NOPE:]
    q_swap = np.concatenate([q_rope[:, :, ROPE // 2:], q_rope[:, :, :ROPE // 2]], 2)
    uq = np.concatenate([q[:, :, :NOPE].reshape(QL, -1), q_rope.reshape(QL, -1), q_swap.reshape(QL, -1)], 1)
    kv = w_ukv[0].reshape(KVL, HEADS, NOPE + VDIM)
    tri = np.where(np.arange(128)[None, :] <= np.arange(128)[:, None], 0.0, 1e30)
    zeros = np.zeros((128, 1))
    consts = np.concatenate([np.eye(128), np.tile(np.arange(128.0), (128, 1)), np.ones((128, 128)),
                             np.tile(zeros, (1, T - 128)), tri, np.tile(zeros, (1, META))], 1)
    return {
        "xT": c(x[0].T.reshape(KD, 128, T).transpose(1, 0, 2)),
        "metaT": c(meta_tokens.T.reshape(KD, 128, META).transpose(1, 0, 2)),
        "vecs": c(np.concatenate([columns(norm1_g[0]), columns(q_norm_g[0]), columns(kv_norm_g[0]), columns(attn_out_g[0]),
                                  columns(conv_out_g[0]), columns(norm2_g[0]), columns(final_g), columns(conv_w[0].reshape(-1)),
                                  columns(conv_b[0])], 1)),
        "consts": consts.astype(np.float32),
        "rope": _rope_tables(),
        "w_tiles": c(np.concatenate([tiles(np.concatenate(parts, 1)), tiles(w_out[0])])),
        "w_uq": c(tiles(uq).transpose(1, 0, 2, 3)),
        "w_ukv": c(np.concatenate([kv[:, :, :NOPE].reshape(KVL, -1), kv[:, :, NOPE:].reshape(KVL, -1)], 1)),
        "keysT": c(np.stack([peer_keys1[0].T, peer_keys2[0].T], 1)),
        "w_query": c(tiles(peer_w_query[0]).reshape(PHEADS, 2, 128, KD, 128).transpose(0, 2, 1, 3, 4)),
        "uT": c(peer_u[0].reshape(128, CHUNKS, 2, KD, 128).transpose(1, 4, 2, 3, 0)),
        "v": c(peer_v[0]),
    }


def kernel(**inputs):
    import concourse.bacc as bacc
    from concourse.bass_utils import run_bass_kernel_spmd

    arrays = _lay_out(**{n: np.asarray(a) for n, a in inputs.items()})
    nc = bacc.Bacc("TRN2", target_bir_lowering=False, num_devices=1)
    args = {n: nc.dram_tensor(n, a.shape, mybir.dt.from_np(a.dtype), kind="ExternalInput").ap() for n, a in arrays.items()}
    yT = nc.dram_tensor("yT", (128, KD, T), mybir.dt.float32, kind="ExternalOutput").ap()
    hymba_peer_kernel(nc, **args, yT=yT)
    result = run_bass_kernel_spmd(nc, [arrays], core_ids=[0])
    y = result.results[0]["yT"]
    return np.ascontiguousarray(y.transpose(2, 1, 0).reshape(1, T, D))
```

```python
from contextlib import ExitStack

import concourse.bass as bass
import numpy as np
from concourse import mybir

D = 1024
T = 512
META = 16
L = T + META
KD = D // 128
EPS = 1e-6
HEADS, NOPE, ROPE, VDIM = 8, 64, 32, 64
QL, KVL = 256, 128
DC = 512
NK = 128
TOPK = 16
QT = T // 128
SCALE = float(NOPE + ROPE) ** -0.5
NEG = -3.0e38

N_IN = 17
N_OUT = 8
WRING = 4
PHEADS = 8
WIDE = 4
NCAND = WIDE * TOPK + (TOPK - WIDE) * 4
ADV = 10
EARLY = 6
SOLO = ADV - EARLY
CHUNKS = NK // 2
HALF = 64
GROUP = 8
SLOTS = 4
GROUPS = HALF // GROUP
WARM_UPS, WARM_COLUMNS = 8, 256
J_PARTS = (slice(0, 16), slice(16, NK))
GSCALE = 4096.0

G1, GQ, GKV, GA, GC, G2, GF, CW, CB, NVEC = 0, 8, 10, 11, 15, 19, 27, 35, 47, 51


def hymba_peer_kernel(nc, xT, metaT, vecs, consts, rope, w_tiles, w_uq, w_ukv, keysT, w_query, uT, v, yT):
    f32, f32r, f16, u32 = mybir.dt.float32, mybir.dt.float32r, mybir.dt.float16, mybir.dt.uint32
    ALU, ACT, AX = mybir.AluOpType, mybir.ActivationFunctionType, mybir.AxisListType

    gates_dram = nc.dram_tensor("gates_dram", (T // HALF, 128, NK, HALF), f32, kind="Internal").ap()
    gates_of = gates_dram.rearrange("q i j t -> i q j t")
    v_tiles = v.rearrange("(i j) d -> i j d", j=NK)

    ctx = ExitStack()
    with ctx:
        def sb(stack, name, shape, dt=f32):
            return stack.enter_context(nc.sbuf_tensor(name, shape, dt))

        const = sb(ctx, "const", [128, 3 * 128])
        ident, iota, ones = const[:, 0:128], const[:, 128:256], const[:, 256:384]
        vec = sb(ctx, "vec", [128, NVEC])
        eps = sb(ctx, "eps", [128, 1])
        early = ExitStack()
        qr_in = sb(early, "qr_in", [128, 4, T])
        wuq_t = sb(early, "wuq_t", [128, 8, 2, 128])
        early.close()
        acc = sb(ctx, "acc", [128, KD, T])

        front = ExitStack()
        normed = ExitStack()
        h_hi = sb(normed, "h_hi", [128, KD, L], f32r)
        h_lo = sb(normed, "h_lo", [128, KD, L], f32r)
        normed.close()
        m_hi = sb(front, "m_hi", [128, KD, T], f32r)
        m_lo = sb(front, "m_lo", [128, KD, T], f32r)
        spare = sb(front, "spare", [128, 2 * KD * META])
        qn = sb(front, "qn", [128, 4, T])
        qr = sb(front, "qr", [128, 2, T])
        hT = sb(front, "hT", [128, KD, L])
        wring = sb(front, "wring", [128, WRING, KD, 128])
        w_hi_t = sb(front, "w_hi_t", [128, 2, KD, 128], f32r)
        w_lo_t = sb(front, "w_lo_t", [128, 2, KD, 128], f32r)
        kn = sb(front, "kn", [128, 4, L])
        kr = sb(front, "kr", [128, L])
        v_att = sb(front, "v_att", [128, QT, DC])
        v_meta = sb(front, "v_meta", [META, DC])
        conv = sb(front, "conv", [128, 4, T])
        causal = sb(front, "causal", [128, L])
        sq = sb(front, "sq", [128, 2, L])
        sq_model = sb(front, "sq_model", [128, 2, L])
        total = sb(front, "total", [128, L])
        rstd = sb(front, "rstd", [128, 2, L])
        rowsum = sb(front, "rowsum", [128, 2, HEADS * QT])
        negmax = sb(front, "negmax", [128, HEADS * QT])
        xn_f = sb(front, "xn_f", [128, 2, T])
        r_in = sb(front, "r_in", [128, 2, L])
        proj = ExitStack()
        c_q = sb(proj, "c_q", [128, 2, T])
        c_kv = sb(proj, "c_kv", [128, L])
        kr_in = sb(proj, "kr_in", [128, 2, L])
        cgate = sb(proj, "cgate", [128, L])
        rope_t = sb(proj, "rope_t", [128, 2, L])
        wukv_t = sb(proj, "wukv_t", [128, 2 * DC])
        z = sb(proj, "z", [128, 4, L])
        bgate = sb(proj, "bgate", [128, 4, T])
        proj.close()
        probs = sb(front, "probs", [128, 4, L])
        ptr = sb(front, "ptr", [128, 2, QT, T])
        ptm = sb(front, "ptm", [META, 2, T])
        att = sb(front, "att", [128, 4, T])
        front.close()

        main = ExitStack()
        x_hi = sb(main, "x_hi", [128, KD, T], f32r)
        x_lo = sb(main, "x_lo", [128, KD, T], f32r)
        act = sb(main, "act", [128, ADV, 2, T])
        raw, s_hi, s_lo = [None, None], [None, None], [None, None]
        raw[0], s_hi[0], s_lo[0] = (sb(main, "raw0", [128, 2, KD, 128]), sb(main, "s_hi0", [128, 2, KD, 128], f32r),
                                    sb(main, "s_lo0", [128, 2, KD, 128], f32r))
        onehots = ExitStack()
        onehot = sb(onehots, "onehot", [128, SLOTS, 3, NK, GROUP], f16)
        onehots.close()
        raw[1], s_hi[1], s_lo[1] = (sb(main, "raw1", [128, 2, KD, 128]), sb(main, "s_hi1", [128, 2, KD, 128], f32r),
                                    sb(main, "s_lo1", [128, 2, KD, 128], f32r))
        choose = ExitStack()
        keys = sb(choose, "keys", [128, 2, NK])
        qk = sb(choose, "qk", [128, 2, 2, T])
        score = sb(choose, "score", [128, 4, QT, 2, NK])
        rest = sb(choose, "rest", [128, QT, 2, NK])
        topv = sb(choose, "topv", [128, 2, QT, TOPK])
        topi = sb(choose, "topi", [128, 2, QT, TOPK], u32)
        cand = sb(choose, "cand", [128, QT, NCAND])
        cand2 = sb(choose, "cand2", [128, QT, NCAND])
        digit = sb(choose, "digit", [128, 3, QT, TOPK], u32)
        bestv = sb(choose, "bestv", [128, QT, TOPK])
        flat = sb(choose, "flat", [128, QT, TOPK], u32)
        pos = sb(choose, "pos", [128, 2, QT, TOPK])
        norming = ExitStack()
        xtmp = sb(norming, "xtmp", [128, KD, T])
        norming.close()
        hit = sb(choose, "hit", [128, 2, 2, QT, TOPK, TOPK])
        topi_f = sb(choose, "topi_f", [128, 2, 2, QT, TOPK])
        expert = sb(choose, "expert", [128, 2, QT, PHEADS, TOPK])
        best = sb(choose, "best", [128, QT, PHEADS, TOPK])
        bsum = sb(choose, "bsum", [128, QT * PHEADS])
        choose.close()
        gatep = ExitStack()
        gates_in = ExitStack()
        pgate = sb(gates_in, "pgate", [128, T])
        gates_in.close()
        stage = sb(gatep, "stage", [128, 2, NK, HALF])
        pick = sb(gatep, "pick", [128, 4, T], f16)
        iotas = sb(gatep, "iotas", [128, NK, GROUP], f16)
        gatep.close()
        v_raw = sb(main, "v_raw", [128, 2, D])
        v_hi = sb(main, "v_hi", [128, 2, 2, D], f32r)
        gate = sb(main, "gate", [128, 2, T // HALF, 2, HALF])
        v_lo = sb(main, "v_lo", [128, 2, 2, D], f32r)
        w_hi = sb(main, "w_hi", [128, 2, 2, T], f32r)
        w_lo = sb(main, "w_lo", [128, 2, 2, T], f32r)
        main.close()
        fin = ExitStack()
        fin_sq = sb(fin, "fin_sq", [128, 2, T])
        fin_total = sb(fin, "fin_total", [128, T])
        fin_r = sb(fin, "fin_r", [128, T])
        fin.close()
        bank = [ctx.enter_context(nc.psum_tensor(f"bank{p}", [128, 1024], f32)) for p in range(4)]

        def across(pair):
            return pair[:, :].rearrange("p (h n) -> p h n", h=2)[:, :, 0:L // 2]

        def halves(columns):
            return columns.rearrange("p (h n) -> p h n", h=2)

        def spans(with_meta):
            if with_meta:
                return [(slice(h * L // 2, (h + 1) * L // 2), slice(512 * h, 512 * h + L // 2)) for h in range(2)]
            return [(slice(0, T), slice(0, T))]

        def sem(name):
            return ctx.enter_context(nc.semaphore(name))

        x_loaded = [sem(f"x_loaded{k}") for k in range(4)]
        meta_loaded, vec_loaded, const_loaded, causal_loaded, rope_loaded = (
            sem("meta_loaded"), sem("vec_loaded"), sem("const_loaded"), sem("causal_loaded"), sem("rope_loaded"))
        wuq_loaded, wukv_loaded, keys_loaded = sem("wuq_loaded"), sem("wukv_loaded"), sem("keys_loaded")
        w_loaded = [sem(f"w_loaded{s}") for s in range(WRING)]
        raw_loaded = [sem("raw_loaded0"), sem("raw_loaded1")]
        v_loaded = sem("v_loaded")
        gate_loaded = [sem("gate_loaded0"), sem("gate_loaded1")]
        stage_stored = [[sem(f"stage_stored_j{p}_{s}") for s in range(2)] for p in range(2)]
        y_stored = sem("y_stored")
        sq_ready, sq_summed, sum_ready, root_ready = sem("sq_ready"), sem("sq_summed"), sem("sum_ready"), sem("root_ready")
        sq_model_ready, sq_added = sem("sq_model_ready"), sem("sq_added")
        rstd_ready, norm_applied = sem("rstd_ready"), sem("norm_applied")
        eps_set, zeros_set = sem("eps_set"), sem("zeros_set")
        tile_done, in_taken, copied, conv_ready, resid_ready = (
            sem("tile_done"), sem("in_taken"), sem("copied"), sem("conv_ready"), sem("resid_ready"))
        h_hi_ready, h_lo_ready = sem("h_hi_ready"), sem("h_lo_ready")
        blk_ready, blk_hi, blk_lo = sem("blk_ready"), sem("blk_hi"), sem("blk_lo")
        wt_hi, wt_lo = sem("wt_hi"), sem("wt_lo")
        krope_ready, qrope_ready = sem("krope_ready"), sem("qrope_ready")
        scores_ready, bias_ready, probs_ready, probs_scaled = (
            sem("scores_ready"), sem("bias_ready"), sem("probs_ready"), sem("probs_scaled"))
        pt_ready, pt_copied, pv_ready, pv_copied = sem("pt_ready"), sem("pt_copied"), sem("pv_ready"), sem("pv_copied")
        xf_ready, xhi_ready, xlo_ready, xlo_pool_ready = (
            sem("xf_ready"), sem("xhi_ready"), sem("xlo_ready"), sem("xlo_pool_ready"))
        hi_ready, lo_ready, prod_done, prod_taken = sem("hi_ready"), sem("lo_ready"), sem("prod_done"), sem("prod_taken")
        first_loaded, first_hi, first_lo, first_done = (
            sem("first_loaded"), sem("first_hi"), sem("first_lo"), sem("first_done"))
        keyscore_done, keyscore_copied, keyscore_taken = sem("keyscore_done"), sem("keyscore_copied"), sem("keyscore_taken")
        hit_ready, hit_weighed = sem("hit_ready"), sem("hit_weighed")
        shifted, exps_ready, choice_ready = sem("shifted"), sem("exps_ready"), sem("choice_ready")
        pick_done, pick_copied = sem("pick_done"), sem("pick_copied")
        plo_ready = sem("plo_ready")
        onehot_hi_ready, onehot_lo_ready = sem("onehot_hi_ready"), sem("onehot_lo_ready")
        gmat_done, gmat_staged = sem("gmat_done"), sem("gmat_staged")
        w_ready, whi_ready, wlo_ready, vhi_ready, vlo_ready = (
            sem("w_ready"), sem("whi_ready"), sem("wlo_ready"), sem("vhi_ready"), sem("vlo_ready"))
        out_done, out_free = sem("out_done"), sem("out_free")
        y_ready = sem("y_ready")
        dve_step, pool_step = sem("dve_step"), sem("pool_step")

        passed = {e: sem(f"passed_{e}") for e in ("act", "dve")}

        def wait_apart(eng, name, s, value):
            eng.wait_ge(s, value)
            eng.sem_inc(passed[name], 1)

        def wait_taken(eng, n):
            if n < N_IN:
                eng.wait_ge(in_taken, n + 1)
            else:
                eng.wait_ge(copied, n - N_IN + 1)

        N_QKV = 17
        N_PROJ = N_IN + N_QKV
        NORM1, NORMQ, NORMKV, NORMC, NORMA, NORM2, NORMF = range(7)
        SQ_FROM = {NORMQ: 0, NORMKV: 2, NORMC: 3, NORMA: 7}
        SQ_COUNT = {NORMQ: 2, NORMKV: 1, NORMC: 4, NORMA: 4}
        MODEL_NORMS = (NORM1, NORM2, NORMF)

        def sq_model_slot(n, k):
            return (fin_sq[:, k % 2, :] if n == NORMF else sq_model[:, k % 2, 0:T] if n == NORM2 else sq_model[:, k % 2, :])

        def total_of(n):
            return fin_total[:, :] if n == NORMF else total[:, 0:T] if n == NORM2 else total[:, :]

        N_ATT = HEADS * QT
        MIX_STEPS = [9, 11, 13, 15]

        SOLO_FROM = PHEADS + EARLY
        FIRST_AT, SECOND_AT = 6, 3
        POOL_BLOCKS = (0, 2, 4)
        LOOKUP_AFTER = [3, 4, 5, 7, 8, 10, 12, 13]

        def buffer_of(n):
            return 0 if SOLO_FROM <= n < SOLO_FROM + SOLO else n % 2

        def before(n):
            if not isinstance(n, int):
                return n - 2
            return max(m for m in range(n) if buffer_of(m) == buffer_of(n))

        def loads_until(n, b):
            if isinstance(n, int):
                return 16 * sum(buffer_of(m) == b for m in range(n + 1))
            return 8 * (n - b) + 16 * (1 - SOLO // 2 if b else 1 + SOLO // 2)

        def score_banks(i):
            return (bank[0][:, 0:512], bank[0][:, 512:1024], bank[1][:, 0:512], bank[3])[i]

        def score_view(i, columns):
            if i == QT - 1:
                return across(bank[3]), halves(columns)
            return score_banks(i)[:, 0:META + 128 * (i + 1)], columns

        def turn_bank(n):
            return bank[1][:, 512:1024] if n % 2 else bank[2][:, 0:512]

        value_bank = bank[2][:, 512:1024]

        def meta_block(n):
            i = n % QT
            return turn_bank(n)[0:META, 128 * (i + 1):128 * (i + 2)] if i < QT - 1 else bank[3][0:META, 384:512]

        def wait_stored(eng, p, buffers=(0, 1)):
            for s in buffers:
                eng.wait_ge(stage_stored[p][s], 16 * (T // HALF // 2))

        def pick_bank(a):
            return bank[3][:, 0:T] if a == 2 else bank[2][:, 512 * a:512 * a + T]

        block = ctx.enter_context(nc.Block())

        @block.sync
        def _(sp):
            sp.dma_start(vec[:, :], vecs).then_inc(vec_loaded, 16)

            def load_w(n):
                if n >= WRING:
                    sp.wait_ge(wt_lo, n - WRING + 1)
                sp.dma_start(wring[:, n % WRING, :, :], w_tiles[n]).then_inc(w_loaded[n % WRING], 16)

            load_w(0)
            sp.dma_start(hT[:, :, 0:META], metaT).then_inc(meta_loaded, 16)
            for k in range(4):
                sp.dma_start(hT[:, 2 * k:2 * k + 2, META:L], xT[:, 2 * k:2 * k + 2, :]).then_inc(x_loaded[k], 16)
                if k == 3:
                    load_w(1)
            sp.dma_start(const[:, :], consts[:, 0:384]).then_inc(const_loaded, 16)
            for n in range(2, WRING):
                load_w(n)
            sp.dma_start(rope_t[:, :, :], rope).then_inc(rope_loaded, 16)
            sp.dma_start(wuq_t[:, :, :, :], w_uq).then_inc(wuq_loaded, 16)
            sp.dma_start(wukv_t[:, :], w_ukv).then_inc(wukv_loaded, 16)
            sp.dma_start(causal[:, :], consts[:, 384:384 + L]).then_inc(causal_loaded, 16)
            for n in range(WRING, N_IN + N_OUT):
                load_w(n)

            sp.wait_ge(resid_ready, N_OUT)

            def load_query(h):
                sp.dma_start(raw[h % 2][:, :, :, :], w_query[h]).then_inc(raw_loaded[h % 2], 16)

            def load_u(c, b):
                sp.wait_ge(lo_ready, before(c + PHEADS) + 1)
                sp.dma_start(raw[b][:, :, :, :], uT[bass.ds(c, 1)].rearrange("c p t k e -> (c p) t k e")).then_inc(raw_loaded[b], 16)

            def load_v(c):
                if not isinstance(c, int) or c:
                    sp.wait_ge(vlo_ready, c)
                sp.dma_start(v_raw[:, :, :], v_tiles[:, bass.ds(2 * c, 2), :]).then_inc(v_loaded, 16)

            def load_gate(c, b):
                if not isinstance(c, int) or c >= 2:
                    sp.wait_ge(w_ready, c - 1)
                sp.dma_start(gate[:, b], gates_of[:, :, bass.ds(2 * c, 2), :]).then_inc(gate_loaded[b], 16)

            for h in range(PHEADS):
                if h >= 2:
                    sp.wait_ge(lo_ready, h - 1)
                load_query(h)
                if h == 0:
                    sp.wait_ge(norm_applied, NORM2 + 1)
                    sp.dma_start(keys[:, :, :], keysT).then_inc(keys_loaded, 16)
            for c in range(EARLY):
                load_u(c, buffer_of(c + PHEADS))
            for i in range(SOLO + 1):
                c = EARLY + i
                if i:
                    sp.wait_ge(first_lo, i)
                else:
                    sp.wait_ge(lo_ready, before(c + PHEADS) + 1)
                sp.dma_start(raw[0][:, 0], uT[c, :, 0]).then_inc(first_loaded, 16)
                sp.wait_ge(lo_ready, before(c + PHEADS) + 1)
                sp.dma_start(raw[0][:, 1], uT[c, :, 1]).then_inc(raw_loaded[0], 16)
            wait_stored(sp, 0, (0,))
            wait_stored(sp, 1, (0,))
            load_v(0)
            wait_stored(sp, 0)
            load_gate(0, 0)
            load_gate(1, 1)
            load_u(ADV + 1, 1)
            load_v(1)
            wait_stored(sp, 1)
            with sp.Fori(1, (CHUNKS - ADV) // 2) as i:
                for b in range(2):
                    load_u(2 * i + b + ADV, b)
                    load_v(2 * i + b)
                    load_gate(2 * i + b, b)
            with sp.Fori((CHUNKS - ADV) // 2, CHUNKS // 2) as i:
                for b in range(2):
                    load_v(2 * i + b)
                    load_gate(2 * i + b, b)

            for k in range(KD):
                sp.wait_ge(y_ready, k + 1)
                sp.dma_start(yT[:, k, :], acc[:, k, :]).then_inc(y_stored, 16)
            sp.wait_ge(y_stored, 16 * KD)

        @block.tensor
        def _(pe):
            def sum_squares(n, pair, meta=False):
                for k in range(SQ_COUNT[n]):
                    q = SQ_FROM[n] + k
                    last_block = k == SQ_COUNT[n] - 1
                    pe.wait_ge(sq_ready, q + 1)
                    for cols, to in spans(meta):
                        last = nc.tensor.matmul(bank[pair][:, to], ones, sq[:, q % 2, cols], start=(k == 0), stop=last_block)
                    last.then_inc(sum_ready if last_block else sq_summed, 1)

            def sum_total(n, pair):
                pe.wait_ge(sq_added, (MODEL_NORMS.index(n) + 1) * (KD - 1))
                for cols, to in spans(n == NORM1):
                    last = nc.tensor.matmul(bank[pair][:, to], ones, total_of(n)[:, cols], start=True, stop=True)
                last.then_inc(sum_ready, 1)

            def stay_warm(count):
                for _ in range(count):
                    nc.tensor.matmul(bank[3][:, 0:WARM_COLUMNS], xn_f[:, 0, 0:128], xn_f[:, 0, 0:WARM_COLUMNS],
                                     start=True, stop=True)

            def parts_product(to, n, x_parts, part, order, waits=None):
                first = True
                for ws, xs in ((w_hi_t, x_parts[0]), (w_lo_t, x_parts[0]), (w_hi_t, x_parts[1])):
                    if n == 0 and ws is w_lo_t:
                        pe.wait_ge(wt_lo, 1)
                    for k in order:
                        if waits is not None:
                            pe.wait_ge(waits[1] if xs is x_parts[1] else waits[0], order.index(k) + 1)
                        last = nc.tensor.matmul(to, ws[:, n % 2, k, :], xs[:, k, part], start=first,
                                                stop=(ws is w_hi_t and xs is x_parts[1] and k == order[-1]))
                        first = False
                        if n == 0 and ws is w_hi_t and xs is x_parts[0]:
                            stay_warm(1)
                return last

            def in_product(n):
                pe.wait_ge(wt_lo if n else wt_hi, n + 1)
                if n >= 2:
                    wait_taken(pe, n - 2)
                of_meta = n >= 2 and (n < 5 or (n - 5) % 3 < 2)
                for cols, to in spans(True) if of_meta else [(slice(META, L), slice(0, T))]:
                    last = parts_product(bank[n % 2][:, to], n, (h_hi, h_lo), cols, range(KD),
                                         (h_hi_ready, h_lo_ready) if n == 0 else None)
                last.then_inc(tile_done, 1)

            pe.wait_ge(zeros_set, 1)
            stay_warm(WARM_UPS)
            in_product(0)
            pe.wait_ge(const_loaded, 16)
            sum_total(NORM1, 2)
            for n in range(1, 8):
                in_product(n)
            sum_squares(NORMQ, 3)
            pe.wait_ge(root_ready, NORM1 + 1)
            sum_squares(NORMKV, 2, meta=True)
            for n in range(8, N_IN):
                in_product(n)

            pe.wait_ge(wuq_loaded, 16)
            pe.wait_ge(wukv_loaded, 16)
            pe.wait_ge(norm_applied, NORMKV + 1)
            for m in range(N_QKV):
                n = N_IN + m
                wait_taken(pe, n - 2)
                to = bank[n % 2]
                if m < 8:
                    for k in range(2):
                        last = nc.tensor.matmul(to[:, 0:T], wuq_t[:, m, k, :], c_q[:, k, :], start=(k == 0), stop=(k == 1))
                elif m < 12:
                    w = wukv_t[:, (m - 8) * 128:(m - 7) * 128]
                    for cols, where in spans(True):
                        last = nc.tensor.matmul(to[:, where], w, c_kv[:, cols], start=True, stop=True)
                elif m < 16:
                    last = nc.tensor.matmul(to[:, 0:T], c_kv[:, META + (m - 12) * 128:META + (m - 11) * 128], wukv_t[:, DC:2 * DC],
                                            start=True, stop=True)
                else:
                    last = nc.tensor.matmul(to[0:META, 0:T], c_kv[:, 0:META], wukv_t[:, DC:2 * DC], start=True, stop=True)
                last.then_inc(tile_done, 1)

            sum_squares(NORMC, 2)

            pe.wait_ge(copied, N_QKV)
            pe.wait_ge(krope_ready, 1)
            pe.wait_ge(qrope_ready, 1)

            def scores(n):
                h, i = n // QT, n % QT
                if n >= QT:
                    pe.wait_ge(probs_ready, n - QT + 1)
                if i == QT - 1 and n > QT:
                    pe.wait_ge(pt_copied, n - QT + 1)
                if n == 3:
                    pe.wait_ge(root_ready, NORMC + 1)
                s = score_banks(i)
                a, r = 64 * (h % 2), 32 * (h % 4)
                qa = qn[a:a + 64, h // 2, 128 * i:128 * i + 128]
                qb = qr[r:r + 32, h // 4, 128 * i:128 * i + 128]
                width = META + 128 * (i + 1)
                for cols, to in spans(True) if width == L else [(slice(0, width), slice(0, width))]:
                    nc.tensor.matmul(s[:, to], qa, kn[a:a + 64, h // 2, cols], start=True, stop=False)
                    last = nc.tensor.matmul(s[:, to], qb, kr[r:r + 32, cols], start=False, stop=True)
                last.then_inc(scores_ready, 1)

            def transpose_probs(n):
                i = n % QT
                pe.wait_ge(probs_scaled, n + 1)
                if n >= 2:
                    pe.wait_ge(pt_copied, n - 1)
                for j in range(i + 1):
                    nc.tensor.transpose(turn_bank(n)[:, 128 * j:128 * j + 128], probs[:, n % 4, META + 128 * j:META + 128 * j + 128], ident)
                nc.tensor.transpose(meta_block(n), probs[:, n % 4, 0:META], ident).then_inc(pt_ready, 1)

            def attend(h):
                pe.wait_ge(pt_copied, QT * (h + 1))
                if h >= 2 and h % 2 == 0:
                    pe.wait_ge(pv_copied, h // 2)
                to = value_bank[64 * (h % 2):64 * (h % 2) + 64, :]
                nc.tensor.matmul(to[:, 0:T], v_meta[:, VDIM * h:VDIM * h + VDIM], ptm[:, h % 2, :], start=True, stop=False)
                for j in range(QT):
                    last = nc.tensor.matmul(to[:, 128 * j:T], v_att[:, j, VDIM * h:VDIM * h + VDIM],
                                            ptr[:, h % 2, j, 128 * j:T], start=False, stop=(j == QT - 1))
                last.then_inc(pv_ready, 1)

            for n in range(3):
                scores(n)
            for n in range(N_ATT):
                if n + 3 < N_ATT:
                    scores(n + 3)
                transpose_probs(n)
                if n % QT == 1 and n > QT:
                    attend(n // QT - 1)
            attend(HEADS - 1)
            pe.wait_ge(pt_copied, N_ATT)
            sum_squares(NORMA, 3)

            for m in range(N_OUT):
                n = N_IN + m
                pe.wait_ge(wt_lo, n + 1)
                if m >= 2:
                    pe.wait_ge(resid_ready, m - 1)
                parts_product(bank[m % 2][:, 0:T], n, (m_hi, m_lo), slice(0, T), (4, 5, 6, 7, 0, 1, 2, 3),
                              (blk_hi, blk_lo) if m == 0 else None).then_inc(tile_done, 1)
            sum_total(NORM2, 2)

            def product(b, to, piece=range(6 * KD)):
                parts = ((s_hi, x_hi), (s_hi, x_lo), (s_lo, x_hi))
                for n in piece:
                    t, (ws, xs), k = n // (3 * KD), parts[n // KD % 3], n % KD
                    last = nc.tensor.matmul(to[:, 512 * t:512 * t + 512], ws[b][:, t, k, :], xs[:, k, :],
                                            start=(n % (3 * KD) == 0), stop=(n % (3 * KD) == 3 * KD - 1))
                if n == 6 * KD - 1:
                    last.then_inc(prod_done, 1)
                return last

            pe.wait_ge(resid_ready, N_OUT)

            def first_product():
                def part(ws, xs, k, start=False, stop=False):
                    for t in range(2):
                        last = nc.tensor.matmul(bank[0][:, 512 * t:512 * t + 512], ws[0][:, t, k, :], xs[:, k, :],
                                                start=start, stop=stop)
                    return last

                pe.wait_ge(hi_ready, 1)
                for k in range(KD):
                    pe.wait_ge(xhi_ready, k + 1)
                    part(s_hi, x_hi, k, start=(k == 0))
                pe.wait_ge(lo_ready, 1)
                for k in range(KD):
                    part(s_lo, x_hi, k)
                pe.wait_ge(xlo_ready, KD - len(POOL_BLOCKS))
                pe.wait_ge(xlo_pool_ready, len(POOL_BLOCKS))
                for k in range(KD):
                    last = part(s_hi, x_lo, k, stop=(k == KD - 1))
                last.then_inc(prod_done, 1)

            def key_scores(g, b):
                pe.wait_ge(prod_taken, 2 * g + b + 1)
                if not isinstance(g, int):
                    pe.wait_ge(keyscore_copied, 2 * g)
                for t in range(QT):
                    for side in range(2):
                        last = nc.tensor.matmul(bank[2 + b][:, (2 * t + side) * NK:(2 * t + side + 1) * NK],
                                                qk[:, b, side, 128 * t:128 * t + 128], keys[:, side, :],
                                                start=True, stop=True)
                last.then_inc(keyscore_done, 1)

            first_product()
            pe.wait_ge(keys_loaded, 16)
            key_scores(0, 0)
            pe.wait_ge(lo_ready, 2)
            product(1, bank[1])
            key_scores(0, 1)
            with pe.Fori(1, PHEADS // 2) as g:
                for b in range(2):
                    pe.wait_ge(lo_ready, 2 * g + b + 1)
                    pe.wait_ge(prod_taken, 2 * g)
                    product(b, bank[b])
                for b in range(2):
                    key_scores(g, b)

            def u_product(c, b):
                pe.wait_ge(lo_ready, c + PHEADS + 1)
                pe.wait_ge(prod_taken, c + PHEADS - 1)
                product(b, bank[b])

            with pe.Fori(0, EARLY // 2) as i:
                for b in range(2):
                    u_product(2 * i + b, b)

            pe.wait_ge(choice_ready, 1)
            pe.wait_ge(keyscore_copied, PHEADS)
            for a in range(3):
                for t in range(QT):
                    src = expert[:, a, t] if a < 2 else best[:, t]
                    last = nc.tensor.transpose(pick_bank(a)[:, 128 * t:128 * t + 128], src.rearrange("p h s -> p (h s)"), ident)
                last.then_inc(pick_done, 1)

            pe.wait_ge(pick_copied, 4)

            def gate_matrices(i, solo=None):
                for g in range(GROUPS):
                    pe.wait_ge(onehot_hi_ready, GROUPS * i + g + 1)
                    if g % 4 < 3:
                        pe.wait_ge(onehot_lo_ready, 3 * GROUPS // 4 * i + g - g // 4 + 1)
                    if not isinstance(i, int) or i or g > 1:
                        pe.wait_ge(gmat_staged, GROUPS * i + g - 1)
                    for t in range(GROUP):
                        to = bank[2 + g % 2][:, t * NK:(t + 1) * NK]
                        row = onehot[:, g % SLOTS, 0, :, t]
                        nc.tensor.matmul(to, row, onehot[:, g % SLOTS, 2, :, t], start=True, stop=False)
                        last = nc.tensor.matmul(to, row, onehot[:, g % SLOTS, 1, :, t], start=False, stop=True)
                    last.then_inc(gmat_done, 1)
                    if solo is None:
                        continue
                    if g == 0:
                        pe.wait_ge(first_lo, i + 1)
                        pe.wait_ge(prod_taken, SOLO_FROM + i - 1)
                    if g == GROUPS // 2:
                        pe.wait_ge(lo_ready, SOLO_FROM + i + 1)
                    piece = 6 * KD // GROUPS
                    last = product(0, bank[solo], range(piece * g, piece * (g + 1)))
                    if g == GROUPS // 2 - 1:
                        last.then_inc(first_done, 1)

            for s in range(2):
                gate_matrices(s, s)
            with pe.Fori(1, SOLO // 2) as i:
                for s in range(2):
                    gate_matrices(2 * i + s, s)
            with pe.Fori(SOLO, T // HALF) as i:
                gate_matrices(i)

            def out_product(c, b):
                pe.wait_ge(vlo_ready, c + 1)
                pe.wait_ge(wlo_ready, c + 1)
                for m in range(KD):
                    pe.wait_ge(out_free, KD * c + m + 1)
                    to = bank[2 + m % 4 // 2][:, 512 * (m % 2):512 * (m % 2) + 512]
                    n = 0
                    for t in range(2):
                        for vs, ws in ((v_hi, w_hi), (v_hi, w_lo), (v_lo, w_hi)):
                            last = nc.tensor.matmul(to, vs[:, b, t, 128 * m:128 * m + 128], ws[:, b, t, :],
                                                    start=(n == 0), stop=(n == 5))
                            n += 1
                    last.then_inc(out_done, 1)

            with pe.Fori(0, (CHUNKS - ADV) // 2) as i:
                for b in range(2):
                    u_product(2 * i + b + ADV, b)
                    out_product(2 * i + b, b)
            with pe.Fori((CHUNKS - ADV) // 2, CHUNKS // 2) as i:
                for b in range(2):
                    out_product(2 * i + b, b)

            pe.wait_ge(prod_taken, CHUNKS + PHEADS)
            sum_total(NORMF, 0)

        @block.scalar
        def _(sc):
            def square(n, k, src):
                q = SQ_FROM[n] + k
                if q >= 2:
                    ends = sum(SQ_FROM[m] + SQ_COUNT[m] <= q - 1 for m in SQ_FROM)
                    if any(SQ_FROM[m] + SQ_COUNT[m] == q - 1 for m in SQ_FROM):
                        sc.wait_ge(sum_ready, 1 + ends)
                    else:
                        sc.wait_ge(sq_summed, q - 1 - ends)
                nc.scalar.activation(sq[:, q % 2, 0:src.shape[-1]], src, ACT.Square).then_inc(sq_ready, 1)

            def square_model(n, k, src):
                if k >= 2:
                    sc.wait_ge(sq_added, MODEL_NORMS.index(n) * (KD - 1) + max(k - 2, 1))
                nc.scalar.activation(sq_model_slot(n, k), src, ACT.Square).then_inc(sq_model_ready, 1)

            def root(n, pair, width, count):
                sc.wait_ge(sum_ready, n + 1)
                if n >= 2:
                    sc.wait_ge(norm_applied, n - 1)
                to = r_in[:, 0, :] if n == NORM1 else fin_r[:, :] if n == NORMF else rstd[:, n % 2, 0:width]
                src = bank[pair][:, 0:width]
                if width == L:
                    to, src = halves(to), across(bank[pair])
                nc.scalar.activation(to, src, ACT.Sqrt, bias=eps[:, :],
                                     scale=1.0 / count).then_inc(root_ready, 1)


            def tile_hi(n):
                sc.wait_ge(w_loaded[n % WRING], 16 * (n // WRING + 1))
                if n >= 2:
                    sc.wait_ge(tile_done, n - 1 + (N_QKV if n - 2 >= N_IN else 0))
                nc.scalar.activation(w_hi_t[:, n % 2], wring[:, n % WRING], ACT.Copy).then_inc(wt_hi, 1)

            def block_hi(k, to):
                sc.wait_ge(blk_ready, k + 1)
                nc.scalar.activation(to, xn_f[:, k % 2, 0:to.shape[-1]], ACT.Copy).then_inc(blk_hi, 1)

            tile_hi(0)
            sc.wait_ge(vec_loaded, 16)
            sc.wait_ge(meta_loaded, 16)
            for k in range(KD):
                sc.wait_ge(x_loaded[k // 2], 16)
                nc.scalar.activation(h_hi[:, k, :], hT[:, k, :], ACT.Copy, scale=vec[:, G1 + k:G1 + k + 1]).then_inc(h_hi_ready, 1)
                square_model(NORM1, k, hT[:, k, :])
            tile_hi(1)
            sc.wait_ge(eps_set, 1)
            root(NORM1, 2, L, D)

            def take(n, to, src, scale=1.0):
                sc.wait_ge(tile_done, n + 1)
                nc.scalar.activation(to, src, ACT.Copy, scale=scale).then_inc(copied, 1)

            for n in range(2, N_IN + 2):
                tile_hi(n)
                if n == 6:
                    sc.wait_ge(in_taken, 3)
                    for k in range(2):
                        square(NORMQ, k, c_q[:, k, :])
                if n == 8:
                    square(NORMKV, 0, c_kv[:, :])
                if n == 9:
                    root(NORMQ, 3, T, QL)
                    root(NORMKV, 2, L, KVL)
            for m in range(N_QKV):
                n = N_IN + m
                src = bank[n % 2]
                if m < 4:
                    take(n, qn[:, m, :], src[:, 0:T], -SCALE)
                elif m < 8:
                    take(n, qr_in[:, m - 4, :], src[:, 0:T], -SCALE)
                elif m < 12:
                    take(n, halves(kn[:, m - 8, :]), across(src))
                elif m < 16:
                    take(n, v_att[:, m - 12, :], src[:, 0:T])
                else:
                    take(n, v_meta[:, :], src[0:META, 0:T])

            for k in range(4):
                sc.wait_ge(conv_ready, k + 1)
                square(NORMC, k, conv[:, k, :])
            root(NORMC, 2, T, DC)

            sc.wait_ge(tile_done, N_PROJ)
            sc.wait_ge(qrope_ready, 1)
            sc.wait_ge(krope_ready, 1)

            def copy_transposed(n):
                h, i = n // QT, n % QT
                sc.wait_ge(pt_ready, n + 1)
                if h >= 2:
                    sc.wait_ge(pv_ready, h - 1)
                nc.scalar.activation(ptr[:, h % 2, 0:i + 1, 128 * i:128 * i + 128],
                                     turn_bank(n)[:, 0:128 * (i + 1)].rearrange("p (j q) -> p j q", q=128), ACT.Copy)
                nc.scalar.activation(ptm[:, h % 2, 128 * i:128 * i + 128], meta_block(n), ACT.Copy).then_inc(pt_copied, 1)

            def exponentiate(n):
                i = n % QT
                width = 128 * (i + 1) + META
                sc.wait_ge(bias_ready, n + 1)
                if n >= 4:
                    sc.wait_ge(pt_ready, n - 3)
                s, to = score_view(i, probs[:, n % 4, 0:width])
                nc.scalar.activation(to, s, ACT.Exp,
                                     bias=negmax[:, n:n + 1], scale=-1.0,
                                     accum_out=rowsum[:, 0, n:n + 1]).then_inc(probs_ready, 1)

            exponentiate(0)
            for n in range(N_ATT):
                if n + 1 < N_ATT:
                    exponentiate(n + 1)
                if n in MIX_STEPS:
                    k = MIX_STEPS.index(n)
                    block_hi(k, m_hi[:, 4 + k, :])
                copy_transposed(n)

            for k in range(4):
                sc.wait_ge(pv_copied, k + 1)
                square(NORMA, k, att[:, k, :])
            root(NORMA, 3, T, DC)
            for k in range(4):
                block_hi(4 + k, m_hi[:, k, :])
            for k in range(KD):
                if k < N_OUT - 2:
                    tile_hi(N_IN + k + 2)
                sc.wait_ge(resid_ready, k + 1)
                square_model(NORM2, k, acc[:, k, :])
            root(NORM2, 2, T, D)

            def split_hi(c, b):
                n = c + PHEADS
                sc.wait_ge(raw_loaded[b], loads_until(n, b))
                if not (isinstance(n, int) and n < 2):
                    sc.wait_ge(prod_done, before(n) + 1)
                nc.scalar.activation(s_hi[b][:, :, :, :], raw[b][:, :, :, :], ACT.Copy).then_inc(hi_ready, 1)

            sc.wait_ge(tile_done, N_PROJ + N_OUT)
            split_hi(-PHEADS, 0)
            for k in range(KD):
                sc.wait_ge(xf_ready, k + 1)
                nc.scalar.activation(x_hi[:, k, :], xtmp[:, k, :], ACT.Copy).then_inc(xhi_ready, 1)
            for h in range(PHEADS):
                split_hi(h + 1 - PHEADS, (h + 1) % 2)
                sc.wait_ge(prod_done, h + 1)
                if h >= 2:
                    sc.wait_ge(keyscore_done, h - 1)
                nc.scalar.activation(qk[:, h % 2], bank[h % 2][:, :].rearrange("p (s t) -> p s t", s=2),
                                     ACT.Copy).then_inc(prod_taken, 1)
                sc.wait_ge(keyscore_done, h + 1)
                if h >= 4:
                    sc.wait_ge(keyscore_taken, h - 3)
                nc.scalar.activation(score[:, h % 4], bank[2 + h % 2][:, :].rearrange("p (t s n) -> p t s n", t=QT, s=2),
                                     ACT.Copy).then_inc(keyscore_copied, 1)

            def gelu(c, b, slot):
                wait_apart(sc, "act", prod_done, c + PHEADS + 1)
                nc.scalar.activation(act[:, slot].rearrange("p s t n -> p (s t n)"), bank[b][:, :],
                                     ACT.Gelu_apprx_tanh).then_inc(prod_taken, 1)

            def solo_hi(i, tile):
                if tile == 0:
                    sc.wait_ge(first_loaded, 16 * i + 16)
                    if not isinstance(i, int) or i:
                        sc.wait_ge(first_done, i)
                else:
                    sc.wait_ge(raw_loaded[0], 16 * (SOLO_FROM // 2 + 1) + 16 * i)
                if tile == 1 or (isinstance(i, int) and i == 0):
                    sc.wait_ge(prod_done, before(SOLO_FROM) + 1 if isinstance(i, int) and i == 0 else SOLO_FROM + i)
                nc.scalar.activation(s_hi[0][:, tile], raw[0][:, tile], ACT.Copy).then_inc(hi_ready if tile else first_hi, 1)

            for c in range(EARLY):
                if c + 1 < EARLY:
                    split_hi(c + 1, (c + 1) % 2)
                else:
                    solo_hi(0, 0)
                    solo_hi(0, 1)
                gelu(c, c % 2, slice(c, c + 1))

            sc.wait_ge(shifted, 1)
            nc.scalar.activation(best[:, :, :, :], best[:, :, :, :], ACT.Exp).then_inc(exps_ready, 1)
            for a in range(2):
                sc.wait_ge(pick_done, a + 1)
                nc.scalar.activation(pick[:, a, :], pick_bank(a), ACT.Copy).then_inc(pick_copied, 1)
            sc.wait_ge(pick_done, 3)
            nc.scalar.activation(pick[:, 2, :], pick_bank(2), ACT.Copy, scale=GSCALE).then_inc(pick_copied, 1)
            nc.scalar.activation(pgate[:, :], pick_bank(2), ACT.Copy, scale=GSCALE).then_inc(pick_copied, 1)

            def stage_half(q, s, solo=False):
                if not isinstance(q, int) or q:
                    for p in range(2):
                        sc.wait_ge(stage_stored[p][s], 16 * q)
                for part in range(2):
                    with sc.Fori(part * GROUPS // 4, (part + 1) * GROUPS // 4) as i:
                        for r in range(2):
                            wait_apart(sc, "act", gmat_done, (2 * q + s) * GROUPS + 2 * i + r + 1)
                            nc.scalar.activation(
                                stage[:, s, :, bass.ds(GROUP * (2 * i + r), GROUP)].rearrange("p j t -> p t j"),
                                bank[2 + r][:, :].rearrange("p (t j) -> p t j", t=GROUP), ACT.Copy,
                                scale=1.0 / GSCALE).then_inc(gmat_staged, 1)
                    if solo and part == 0:
                        solo_hi(2 * q + s + 1, 0)
                sc.wait_ge(gmat_staged, (2 * q + s + 1) * GROUPS)
                for p in range(2):
                    js = J_PARTS[p]
                    sc.dma_start(gates_dram[bass.ds(2 * q + s, 1), :, js].rearrange("q i j t -> (q i) j t"),
                                 stage[:, s, js]).then_inc(stage_stored[p][s], 16)

            for q in range(2):
                stage_half(0, q, solo=True)
                solo_hi(q + 1, 1)
                gelu(EARLY + q, q, slice(EARLY + q, EARLY + q + 1))
            with sc.Fori(1, SOLO // 2) as q:
                for s in range(2):
                    stage_half(q, s, solo=True)
                    solo_hi(2 * q + s + 1, 1)
                    gelu(EARLY + 2 * q + s, s, bass.ds(EARLY + 2 * q + s, 1))
            with sc.Fori(SOLO // 2, T // HALF // 2) as q:
                for s in range(2):
                    stage_half(q, s)

            def out_hi(c, b, slot):
                sc.wait_ge(v_loaded, 16 * c + 16)
                if not (isinstance(c, int) and c < 2):
                    sc.wait_ge(out_done, KD * (c - 1))
                nc.scalar.activation(v_hi[:, b], v_raw[:, :, :], ACT.Copy).then_inc(vhi_ready, 1)
                if isinstance(c, int) and c == 0:
                    wait_stored(sc, 1)
                wait_apart(sc, "act", w_ready, c + 1)
                nc.scalar.activation(w_hi[:, b].rearrange("p t n -> p (t n)"), act[:, slot].rearrange("p s t n -> p (s t n)"),
                                     ACT.Copy).then_inc(whi_ready, 1)

            out_hi(0, 0, slice(0, 1))

            def step(c, b, slot, next_slot, last=False):
                out_hi(c + 1, 1 - b, next_slot)
                if not last:
                    split_hi(c + ADV + 1, 1 - b)
                sc.wait_ge(wlo_ready, c + 1)
                gelu(c + ADV, b, slot)

            for c in range(2):
                step(c, c, slice(c, c + 1), slice(c + 1, c + 2))
            with sc.Fori(1, (CHUNKS - ADV) // 2 - 1) as i:
                for b in range(2):
                    c = 2 * i + b
                    step(c, b, bass.ds(c % ADV, 1), bass.ds((c + 1) % ADV, 1))
            for c in range(CHUNKS - ADV - 2, CHUNKS - ADV):
                step(c, c % 2, slice(c % ADV, c % ADV + 1), slice((c + 1) % ADV, (c + 1) % ADV + 1), last=c == CHUNKS - ADV - 1)
            for c in range(CHUNKS - ADV + 1, CHUNKS):
                out_hi(c, c % 2, slice(c % ADV, c % ADV + 1))

            sc.wait_ge(prod_done, PHEADS + CHUNKS)
            for k in range(KD):
                sc.wait_ge(out_free, 4 + KD * (CHUNKS - 1) + k + 1)
                square_model(NORMF, k, acc[:, k, :])
            root(NORMF, 0, T, D)

        @block.gpsimd
        def _(pool):
            def tile_lo(n):
                pool.wait_ge(wt_hi, n + 1)
                nc.gpsimd.tensor_tensor(w_lo_t[:, n % 2].rearrange("p k e -> p (k e)"),
                                        wring[:, n % WRING].rearrange("p k e -> p (k e)"),
                                        w_hi_t[:, n % 2].rearrange("p k e -> p (k e)").bitcast(f32), ALU.subtract).then_inc(wt_lo, 1)

            def block_lo(k, to, hi):
                pool.wait_ge(blk_hi, k + 1)
                nc.gpsimd.tensor_tensor(to, xn_f[:, k % 2, 0:to.shape[-1]], hi.bitcast(f32), ALU.subtract).then_inc(blk_lo, 1)

            tile_lo(0)
            tile_lo(1)
            for n in range(2, 7):
                tile_lo(n)
            pool.wait_ge(rope_loaded, 16)
            pool.wait_ge(in_taken, 5)
            nc.gpsimd.tensor_tensor(kr[:, :], kr_in[:, 0, :], rope_t[:, 0, :], ALU.mult)
            nc.gpsimd.tensor_tensor(kr_in[:, 1, :], kr_in[:, 1, :], rope_t[:, 1, :], ALU.mult).then_inc(pool_step, 1)
            pool.wait_ge(pool_step, 1)
            nc.gpsimd.tensor_tensor(kr[:, :], kr[:, :], kr_in[:, 1, :], ALU.add).then_inc(krope_ready, 1)
            for n in range(7, N_IN + 2):
                tile_lo(n)
            for k in range(4):
                block_lo(k, m_lo[:, 4 + k, :], m_hi[:, 4 + k, :])
            for k in range(4):
                block_lo(4 + k, m_lo[:, k, :], m_hi[:, k, :])
            for n in range(N_IN + 2, N_IN + N_OUT):
                tile_lo(n)

            def lookup(h):
                pool.wait_ge(hit_ready, h + 1)
                for s in range(2):
                    last = nc.gpsimd.tensor_tensor(hit[:, h % 2, s], hit[:, h % 2, s],
                                                   topi_f[:, h % 2, s].unsqueeze(2).broadcast_to([128, QT, TOPK, TOPK]), ALU.mult)
                last.then_inc(hit_weighed, 1)

            def split_lo(c, b):
                n = c + PHEADS
                pool.wait_ge(hi_ready, n + 1)
                nc.gpsimd.tensor_tensor(s_lo[b][:, :, :, :].rearrange("p t k e -> p (t k e)"),
                                        raw[b][:, :, :, :].rearrange("p t k e -> p (t k e)"),
                                        s_hi[b][:, :, :, :].rearrange("p t k e -> p (t k e)").bitcast(f32),
                                        ALU.subtract).then_inc(lo_ready, 1)

            def solo_lo(i, tile):
                if tile == 0:
                    pool.wait_ge(first_hi, i + 1)
                else:
                    pool.wait_ge(hi_ready, SOLO_FROM + i + 1)
                nc.gpsimd.tensor_tensor(s_lo[0][:, tile].rearrange("p k e -> p (k e)"), raw[0][:, tile].rearrange("p k e -> p (k e)"),
                                        s_hi[0][:, tile].rearrange("p k e -> p (k e)").bitcast(f32),
                                        ALU.subtract).then_inc(lo_ready if tile else first_lo, 1)

            for n in range(SOLO_FROM + 1):
                if n < SOLO_FROM:
                    split_lo(n - PHEADS, n % 2)
                else:
                    solo_lo(0, 0)
                    solo_lo(0, 1)
                for k in POOL_BLOCKS if n == 0 else ():
                    pool.wait_ge(xhi_ready, k + 1)
                    nc.gpsimd.tensor_tensor(x_lo[:, k, :], xtmp[:, k, :], x_hi[:, k, :].bitcast(f32),
                                            ALU.subtract).then_inc(xlo_pool_ready, 1)
                if n in LOOKUP_AFTER:
                    lookup(LOOKUP_AFTER.index(n))

            pool.wait_ge(plo_ready, 1)

            def low_columns(i, second=True, first=True):
                for g in range(GROUPS):
                    if g == SECOND_AT and second:
                        solo_lo(i, 1)
                    if g % 4 < 3:
                        pool.wait_ge(onehot_hi_ready, GROUPS * i + g + 1)
                        lo = pick[:, 3, bass.ds(HALF * i + GROUP * g, GROUP)]
                        nc.gpsimd.tensor_tensor(onehot[:, g % SLOTS, 1], onehot[:, g % SLOTS, 1],
                                                lo.unsqueeze(1).broadcast_to([128, NK, GROUP]), ALU.mult).then_inc(onehot_lo_ready, 1)
                    if g == FIRST_AT and first:
                        solo_lo(i + 1, 0)

            low_columns(0, second=False)
            with pool.Fori(1, SOLO) as i:
                low_columns(i)
            low_columns(SOLO, first=False)
            with pool.Fori(SOLO + 1, T // HALF) as i:
                low_columns(i, second=False, first=False)

            def weigh(c, b, slot):
                pool.wait_ge(gate_loaded[b], 16 * (c // 2) + 16 if isinstance(c, int) else 8 * (c - b) + 16)
                pool.wait_ge(prod_taken, c + PHEADS + 1)
                w = act[:, slot].rearrange("p s t (q n) -> p (s t) q n", n=HALF)
                nc.gpsimd.tensor_tensor(w, w, gate[:, b].rearrange("p q t n -> p t q n"), ALU.mult).then_inc(w_ready, 1)

            weigh(0, 0, slice(0, 1))
            with pool.Fori(0, (CHUNKS - ADV) // 2 - 1) as i:
                for b in range(2):
                    c = 2 * i + b
                    weigh(c + 1, 1 - b, bass.ds((c + 1) % ADV, 1))
                    split_lo(c + ADV + 1, 1 - b)
            for c in range(CHUNKS - ADV - 2, CHUNKS - 1):
                weigh(c + 1, (c + 1) % 2, slice((c + 1) % ADV, (c + 1) % ADV + 1))
                if c < CHUNKS - ADV - 1:
                    split_lo(c + ADV + 1, (c + 1) % 2)

        @block.vector
        def _(dve):
            steps = [0]

            def chain(ins):
                steps[0] += 1
                ins.then_inc(dve_step, 1)
                dve.wait_ge(dve_step, steps[0])

            def invert(n, width):
                dve.wait_ge(root_ready, n + 1)
                r = r_in[:, 0, :] if n == NORM1 else fin_r[:, :] if n == NORMF else rstd[:, n % 2, 0:width]
                nc.vector.reciprocal(r, r).then_inc(rstd_ready, 1)
                dve.wait_ge(rstd_ready, n + 1)
                return r

            def add_square(n, k):
                first = MODEL_NORMS.index(n)
                dve.wait_ge(sq_model_ready, first * KD + k + 1)
                if k > 1:
                    dve.wait_ge(sq_added, first * (KD - 1) + k - 1)
                nc.vector.tensor_tensor(total_of(n), total_of(n) if k > 1 else sq_model_slot(n, 0), sq_model_slot(n, k),
                                        ALU.add).then_inc(sq_added, 1)

            def apply(to, src, gain, r):
                return nc.vector.scalar_tensor_tensor(to, src, vec[:, gain:gain + 1], r, ALU.mult, ALU.mult)

            nc.vector.memset(xn_f[:, 0, :], 0.0).then_inc(zeros_set, 1)
            nc.vector.memset(eps[:, :], EPS).then_inc(eps_set, 1)
            dve.wait_ge(vec_loaded, 16)
            for k in range(KD):
                dve.wait_ge(h_hi_ready, k + 1)
                nc.vector.scalar_tensor_tensor(h_lo[:, k, :], hT[:, k, :], vec[:, G1 + k:G1 + k + 1], h_hi[:, k, :].bitcast(f32),
                                               ALU.mult, ALU.subtract).then_inc(h_lo_ready, 1)
                if k:
                    add_square(NORM1, k)
            r = invert(NORM1, L)
            chain(nc.vector.tensor_tensor(r_in[:, 1, :], r, r, ALU.mult))
            dve.sem_inc(norm_applied, 1)

            def take(n, to, width, square=0):
                dve.wait_ge(tile_done, n + 1)
                if width == L:
                    to, src, by = halves(to), across(bank[n % 2]), halves(r_in[:, square, :])
                else:
                    src, by = bank[n % 2][:, 0:T], r_in[:, square, META:L]
                nc.vector.tensor_tensor(to, src, by, ALU.mult).then_inc(in_taken, 1)

            def conv_input(j):
                n = 6 + 3 * j
                dve.wait_ge(tile_done, n + 1)
                dve.wait_ge(in_taken, n)
                nc.vector.tensor_tensor(halves(z[:, j, :]), across(bank[n % 2]), halves(cgate[:, :]),
                                        ALU.mult).then_inc(in_taken, 1)

            take(0, c_q[:, 0, :], T)
            take(1, c_q[:, 1, :], T)
            take(2, c_kv[:, :], L)
            take(3, kr_in[:, 0, :], L)
            take(4, kr_in[:, 1, :], L)
            for j in range(4):
                take(5 + 3 * j, cgate[:, :], L, square=1)
                if j == 1:
                    r = invert(NORMKV, L)
                    apply(c_kv[:, :], c_kv[:, :], GKV, r).then_inc(norm_applied, 1)
                conv_input(j)
                take(7 + 3 * j, bgate[:, j, :], T)
                if j == 0:
                    r = invert(NORMQ, T)
                    for k in range(2):
                        last = apply(c_q[:, k, :], c_q[:, k, :], GQ + k, r)
                    last.then_inc(norm_applied, 1)

            dve.wait_ge(in_taken, N_IN)
            for j in range(4):
                last = nc.vector.tensor_scalar(conv[:, j, :], z[:, j, META - 2:L - 2], vec[:, CW + j:CW + j + 1],
                                               vec[:, CB + j:CB + j + 1], ALU.mult, ALU.add)
            chain(last)
            for tap in (1, 2):
                for j in range(4):
                    w = CW + 4 * tap + j
                    last = nc.vector.scalar_tensor_tensor(conv[:, j, :], z[:, j, META - 2 + tap:L - 2 + tap], vec[:, w:w + 1],
                                                          conv[:, j, :], ALU.mult, ALU.add)
                chain(last)
            for j in range(4):
                nc.vector.tensor_tensor(conv[:, j, :], conv[:, j, :], bgate[:, j, 0:T], ALU.mult).then_inc(conv_ready, 1)

            dve.wait_ge(rope_loaded, 16)
            dve.wait_ge(copied, 8)
            for m in range(2):
                nc.vector.tensor_tensor(qr[:, m, :], qr_in[:, m, :], rope_t[:, 0, META:L], ALU.mult)
            for m in range(2):
                last = nc.vector.tensor_tensor(qr_in[:, 2 + m, :], qr_in[:, 2 + m, :], rope_t[:, 1, META:L], ALU.mult)
            chain(last)
            for m in range(2):
                last = nc.vector.tensor_tensor(qr[:, m, :], qr[:, m, :], qr_in[:, 2 + m, :], ALU.add)
            last.then_inc(qrope_ready, 1)

            dve.wait_ge(causal_loaded, 16)

            def maximum(n):
                i = n % QT
                width = 128 * (i + 1) + META
                s, mask = score_view(i, causal[:, L - width:L])
                dve.wait_ge(scores_ready, n + 1)
                nc.vector.tensor_tensor_reduce(out=s, in0=s, in1=mask, scale=1.0, scalar=-NEG,
                                               op0=ALU.add, op1=ALU.min, accum_out=negmax[:, n:n + 1]).then_inc(bias_ready, 1)

            def normalise(n):
                width = 128 * (n % QT + 1) + META
                dve.wait_ge(probs_ready, n + 1)
                chain(nc.vector.reciprocal(rowsum[:, 1, n:n + 1], rowsum[:, 0, n:n + 1]))
                nc.vector.tensor_scalar(probs[:, n % 4, 0:width], probs[:, n % 4, 0:width], rowsum[:, 1, n:n + 1],
                                        None, ALU.mult).then_inc(probs_scaled, 1)

            def take_pair(p):
                dve.wait_ge(pv_ready, 2 * p + 2)
                nc.vector.tensor_copy(att[:, p, :], value_bank).then_inc(pv_copied, 1)

            def mix(n, src, gain, b, k):
                if k == 0:
                    invert(n, T)
                if b >= 2:
                    dve.wait_ge(blk_lo, b - 1)
                apply(xn_f[:, b % 2, 0:T], src[:, k, :], gain + k, rstd[:, n % 2, 0:T]).then_inc(blk_ready, 1)
                if k == 3:
                    dve.wait_ge(blk_ready, b + 1)
                    dve.sem_inc(norm_applied, 1)

            maximum(0)
            maximum(1)
            for n in range(N_ATT):
                if n + 2 < N_ATT:
                    maximum(n + 2)
                normalise(n)
                if n + 1 in MIX_STEPS:
                    k = MIX_STEPS.index(n + 1)
                    mix(NORMC, conv, GC, k, k)
                if n % (2 * QT) == 2 and n > 2 * QT:
                    take_pair(n // (2 * QT) - 1)
            take_pair(3)
            for k in range(4):
                mix(NORMA, att, GA, 4 + k, k)

            for m in range(N_OUT):
                dve.wait_ge(tile_done, N_PROJ + m + 1)
                nc.vector.tensor_tensor(acc[:, m, :], bank[m % 2][:, 0:T], hT[:, m, META:L], ALU.add).then_inc(resid_ready, 1)
                if m >= 2:
                    add_square(NORM2, m - 1)
            add_square(NORM2, KD - 1)

            r = invert(NORM2, T)
            dve.wait_ge(resid_ready, N_OUT)
            for k in range(KD):
                apply(xtmp[:, k, :], acc[:, k, :], G2 + k, r).then_inc(xf_ready, 1)
            dve.wait_ge(xf_ready, KD)
            dve.sem_inc(norm_applied, 1)
            for k in range(KD):
                if k not in POOL_BLOCKS:
                    dve.wait_ge(xhi_ready, k + 1)
                    nc.vector.tensor_tensor(x_lo[:, k, :], xtmp[:, k, :], x_hi[:, k, :].bitcast(f32),
                                            ALU.subtract).then_inc(xlo_ready, 1)

            first = steps[0]
            tails = 0

            def top16(values, vals, idx, scratch, link):
                n = len(values)
                for i in range(n):
                    last = nc.vector.max(vals[i][:, 0:8], values[i])
                link(last)
                for i in range(n):
                    nc.vector.max_index(idx[i][:, 0:8], vals[i][:, 0:8], values[i])
                    last = nc.vector.match_replace(scratch[i], vals[i][:, 0:8], values[i], NEG)
                link(last)
                for i in range(n):
                    last = nc.vector.max(vals[i][:, 8:16], scratch[i])
                link(last)
                for i in range(n):
                    last = nc.vector.max_index(idx[i][:, 8:16], vals[i][:, 8:16], scratch[i])
                return last

            def reduce_hits(h, b):
                wait_apart(dve, "dve", hit_weighed, h + 1)
                for s in range(2):
                    nc.vector.tensor_reduce(expert[:, s, :, bass.ds(h, 1), :].rearrange("p t h s -> p t (h s)"),
                                            hit[:, b, s], AX.X, ALU.add)

            PER_HEAD = 12
            with dve.Fori(0, PHEADS // 4) as g:
                for q in range(4):
                    h = 4 * g + q
                    done = [0]

                    def link(ins):
                        done[0] += 1
                        ins.then_inc(dve_step, 1)
                        wait_apart(dve, "dve", dve_step, first + PER_HEAD * h + done[0])

                    wait_apart(dve, "dve", keyscore_copied, h + 1)
                    both = [(t, s) for t in range(QT) for s in range(2)]
                    last = top16([score[:, q, t, s, :] for t, s in both], [topv[:, s, t, :] for t, s in both],
                                 [topi[:, s, t, :] for t, s in both], [rest[:, t, s, :] for t, s in both], link)
                    link(last)
                    dve.sem_inc(keyscore_taken, 1)
                    wide = cand[:, :, 0:WIDE * TOPK].rearrange("p t (a b) -> p t a b", a=WIDE)
                    tall = cand[:, :, WIDE * TOPK:NCAND].rearrange("p t (a b) -> p t a b", b=4)
                    nc.vector.tensor_tensor(wide, topv[:, 0, :, 0:WIDE].unsqueeze(3).broadcast_to([128, QT, WIDE, TOPK]),
                                            topv[:, 1].unsqueeze(2).broadcast_to([128, QT, WIDE, TOPK]), ALU.add)
                    nc.vector.tensor_copy(topi_f[:, q % 2], topi[:, :, :, :])
                    link(nc.vector.tensor_tensor(tall, topv[:, 0, :, WIDE:].unsqueeze(3).broadcast_to([128, QT, TOPK - WIDE, 4]),
                                                 topv[:, 1, :, 0:4].unsqueeze(2).broadcast_to([128, QT, TOPK - WIDE, 4]), ALU.add))
                    last = top16([cand[:, t] for t in range(QT)], [bestv[:, t, :] for t in range(QT)],
                                 [flat[:, t, :] for t in range(QT)], [cand2[:, t, :] for t in range(QT)], link)
                    if q:
                        reduce_hits(h - 1, (q - 1) % 2)
                    link(last)
                    nc.vector.tensor_copy(best[:, :, bass.ds(h, 1), :].rearrange("p t h s -> p t (h s)"), bestv[:, :, :])
                    nc.vector.tensor_scalar(digit[:, 0], flat[:, :, :], 2, None, ALU.logical_shift_right)
                    nc.vector.tensor_scalar(digit[:, 1], flat[:, :, :], 4, None, ALU.logical_shift_right)
                    nc.vector.tensor_scalar(digit[:, 2], flat[:, :, :], 12, None, ALU.bitwise_and)
                    link(nc.vector.tensor_scalar(flat[:, :, :], flat[:, :, :], TOPK * WIDE + 3, None, ALU.bitwise_and))
                    nc.vector.scalar_tensor_tensor(pos[:, 0], digit[:, 0], -12.0, digit[:, 1], ALU.add, ALU.max)
                    nc.vector.scalar_tensor_tensor(pos[:, 1], flat[:, :, :], float(TOPK * WIDE), digit[:, 2], ALU.is_lt, ALU.mult)
                    link(nc.vector.tensor_scalar(flat[:, :, :], flat[:, :, :], 3, None, ALU.bitwise_and))
                    link(nc.vector.tensor_tensor(pos[:, 1], pos[:, 1], flat[:, :, :], ALU.add))
                    for s in range(2):
                        last = nc.vector.tensor_tensor(hit[:, q % 2, s], pos[:, s].unsqueeze(3).broadcast_to([128, QT, TOPK, TOPK]),
                                                       iota[:, 0:TOPK].unsqueeze(1).unsqueeze(1).broadcast_to([128, QT, TOPK, TOPK]),
                                                       ALU.is_equal)
                    last.then_inc(hit_ready, 1)
                    if q == 3:
                        reduce_hits(h, 1)
                    assert done[0] == PER_HEAD, done[0]
            steps[0] = first + PER_HEAD * PHEADS

            gates = best[:, :, :, :].rearrange("p t h s -> p (t h) s")
            chain(nc.vector.tensor_copy(bsum[:, :], gates[:, :, 0]))
            nc.vector.tensor_tensor(gates, gates, bsum[:, :].unsqueeze(2).broadcast_to([128, QT * PHEADS, TOPK]),
                                    ALU.subtract).then_inc(shifted, 1)
            dve.wait_ge(exps_ready, 1)
            chain(nc.vector.tensor_reduce(bsum[:, :], gates, AX.X, ALU.add))
            chain(nc.vector.reciprocal(bsum[:, :], bsum[:, :]))
            nc.vector.tensor_tensor(gates, gates, bsum[:, :].unsqueeze(2).broadcast_to([128, QT * PHEADS, TOPK]),
                                    ALU.mult).then_inc(choice_ready, 1)

            for t in range(GROUP):
                last = nc.vector.tensor_copy(iotas[:, :, t], iota)
            chain(last)
            dve.wait_ge(pick_copied, 2)
            first_hot = steps[0]

            def onehots_of(i):
                for g in range(GROUPS):
                    def spread(a):
                        return pick[:, a, bass.ds(HALF * i + GROUP * g, GROUP)].unsqueeze(1).broadcast_to([128, NK, GROUP])

                    if not isinstance(i, int) or g >= SLOTS:
                        wait_apart(dve, "dve", gmat_done, GROUPS * i + g - SLOTS + 1)
                    hot = onehot[:, g % SLOTS]
                    nc.vector.tensor_tensor(hot[:, 1], iotas[:, :, :], spread(1), ALU.is_equal).then_inc(dve_step, 1)
                    nc.vector.tensor_tensor(hot[:, 0], iotas[:, :, :], spread(0), ALU.is_equal)
                    wait_apart(dve, "dve", dve_step, first_hot + GROUPS * i + g + 1)
                    if isinstance(i, int) and g == 0:
                        dve.wait_ge(pick_copied, 4)
                        nc.vector.tensor_tensor(pick[:, 3, :], pgate[:, :], pick[:, 2, :], ALU.subtract).then_inc(plo_ready, 1)
                    last = nc.vector.tensor_tensor(hot[:, 2], hot[:, 1], spread(2), ALU.mult)
                    if g % 4 == 3:
                        last = nc.vector.tensor_tensor(hot[:, 1], hot[:, 1], spread(3), ALU.mult)
                    last.then_inc(onehot_hi_ready, 1)

            onehots_of(0)
            with dve.Fori(1, T // HALF) as i:
                onehots_of(i)

            def out_lo(c, b, slot):
                dve.wait_ge(vhi_ready, c + 1)
                if isinstance(c, int) and c == 0:
                    wait_stored(dve, 1)
                nc.vector.tensor_tensor(v_lo[:, b], v_raw[:, :, :], v_hi[:, b].bitcast(f32), ALU.subtract).then_inc(vlo_ready, 1)
                dve.wait_ge(whi_ready, c + 1)
                nc.vector.tensor_tensor(w_lo[:, b].rearrange("p t n -> p (t n)"), act[:, slot].rearrange("p s t n -> p (s t n)"),
                                        w_hi[:, b].rearrange("p t n -> p (t n)").bitcast(f32), ALU.subtract).then_inc(wlo_ready, 1)

            def add_out(c):
                last = isinstance(c, int) and c == CHUNKS - 1
                for m in range(KD):
                    dve.wait_ge(out_done, KD * c + m + 1)
                    nc.vector.tensor_tensor(acc[:, m, :], acc[:, m, :], bank[2 + m % 4 // 2][:, 512 * (m % 2):512 * (m % 2) + 512],
                                            ALU.add).then_inc(out_free, 1)
                    if last and m >= 2:
                        add_square(NORMF, m - 1)
                if last:
                    add_square(NORMF, KD - 1)

            dve.sem_inc(out_free, 4)
            out_lo(0, 0, slice(0, 1))
            with dve.Fori(0, CHUNKS // 2 - 1) as i:
                for b in range(2):
                    c = 2 * i + b
                    out_lo(c + 1, 1 - b, bass.ds((c + 1) % ADV, 1))
                    add_out(c)
            out_lo(CHUNKS - 1, 1, slice((CHUNKS - 1) % ADV, (CHUNKS - 1) % ADV + 1))
            add_out(CHUNKS - 2)
            add_out(CHUNKS - 1)

            r = invert(NORMF, T)
            for k in range(KD):
                apply(acc[:, k, :], acc[:, k, :], GF + k, r).then_inc(y_ready, 1)


def _rope_tables():
    half = ROPE // 2
    inv = (1.0 / (np.float32(10000.0) ** (np.arange(0, ROPE, 2, dtype=np.float32) / np.float32(ROPE)))).astype(np.float32)
    position = np.arange(L, dtype=np.float32)
    angle = inv[:, None] * position[None, :]
    cos = np.concatenate([np.cos(angle)] * 2)
    sin = np.concatenate([-np.sin(angle), np.sin(angle)])
    return np.tile(np.stack([cos, sin], 1), (128 // ROPE, 1, 1)).astype(np.float32)


def _lay_out(x, meta_tokens, norm1_g, w_in, q_norm_g, w_uq, kv_norm_g, w_ukv, conv_w, conv_b, attn_out_g, conv_out_g,
             w_out, norm2_g, peer_w_query, peer_keys1, peer_keys2, peer_u, peer_v, final_g):
    c = np.ascontiguousarray

    def columns(g):
        return g.reshape(-1, 128).T

    def tiles(w):
        return w.reshape(w.shape[0] // 128, 128, -1, 128).transpose(2, 1, 0, 3)

    wi = w_in[0]
    o2, o3 = QL + KVL, QL + KVL + ROPE
    kr = wi[:, o2:o3]
    swapped = np.concatenate([kr[:, ROPE // 2:], kr[:, :ROPE // 2]], 1)
    parts = [wi[:, :o2]] + [kr] * 4 + [swapped] * 4
    bcu = [wi[:, o3 + n * DC:o3 + (n + 1) * DC] for n in range(3)]
    for j in range(4):
        parts += [bcu[n][:, 128 * j:128 * j + 128] for n in (1, 2, 0)]
    q = w_uq[0].reshape(QL, HEADS, NOPE + ROPE)
    q_rope = q[:, :, NOPE:]
    q_swap = np.concatenate([q_rope[:, :, ROPE // 2:], q_rope[:, :, :ROPE // 2]], 2)
    uq = np.concatenate([q[:, :, :NOPE].reshape(QL, -1), q_rope.reshape(QL, -1), q_swap.reshape(QL, -1)], 1)
    kv = w_ukv[0].reshape(KVL, HEADS, NOPE + VDIM)
    tri = np.where(np.arange(128)[None, :] <= np.arange(128)[:, None], 0.0, 1e30)
    zeros = np.zeros((128, 1))
    consts = np.concatenate([np.eye(128), np.tile(np.arange(128.0), (128, 1)), np.ones((128, 128)),
                             np.tile(zeros, (1, L - 128)), tri], 1)
    return {
        "xT": c(x[0].T.reshape(KD, 128, T).transpose(1, 0, 2)),
        "metaT": c(meta_tokens.T.reshape(KD, 128, META).transpose(1, 0, 2)),
        "vecs": c(np.concatenate([columns(norm1_g[0]), columns(q_norm_g[0]), columns(kv_norm_g[0]), columns(attn_out_g[0]),
                                  columns(conv_out_g[0]), columns(norm2_g[0]), columns(final_g), columns(conv_w[0].reshape(-1)),
                                  columns(conv_b[0])], 1)),
        "consts": consts.astype(np.float32),
        "rope": _rope_tables(),
        "w_tiles": c(np.concatenate([tiles(np.concatenate(parts, 1)), tiles(w_out[0])])),
        "w_uq": c(tiles(uq).transpose(1, 0, 2, 3)),
        "w_ukv": c(np.concatenate([kv[:, :, :NOPE].reshape(KVL, -1), kv[:, :, NOPE:].reshape(KVL, -1)], 1)),
        "keysT": c(np.stack([peer_keys1[0].T, peer_keys2[0].T], 1)),
        "w_query": c(tiles(peer_w_query[0]).reshape(PHEADS, 2, 128, KD, 128).transpose(0, 2, 1, 3, 4)),
        "uT": c(peer_u[0].reshape(128, CHUNKS, 2, KD, 128).transpose(1, 4, 2, 3, 0)),
        "v": c(peer_v[0]),
    }


def kernel(**inputs):
    import concourse.bacc as bacc
    from concourse.bass_utils import run_bass_kernel_spmd

    arrays = _lay_out(**{n: np.asarray(a) for n, a in inputs.items()})
    nc = bacc.Bacc("TRN2", target_bir_lowering=False, num_devices=1)
    args = {n: nc.dram_tensor(n, a.shape, mybir.dt.from_np(a.dtype), kind="ExternalInput").ap() for n, a in arrays.items()}
    yT = nc.dram_tensor("yT", (128, KD, T), mybir.dt.float32, kind="ExternalOutput").ap()
    hymba_peer_kernel(nc, **args, yT=yT)
    result = run_bass_kernel_spmd(nc, [arrays], core_ids=[0])
    y = result.results[0]["yT"]
    return np.ascontiguousarray(y.transpose(2, 1, 0).reshape(1, T, D))
```
